# Optimizing a Trainium2 kernel written in Bass

```python
import jax, jax.numpy as jnp
from jax import lax
import numpy as np

'''One inference step of a hybrid diffusion / flow-matching backbone: DEPTH parallel-head-group layers.

Every layer: adaLN-modulated RMSNorm -> ONE combined input projection whose columns are split among four
parallel head groups that all read the same normalised input:
  (A) chunked spatial-gating MLP (4 heads x 64 ch, 128x128 position mixing per head, bidirectional),
  (B) short gated convolution y = B * conv3(C * h) (256 depthwise channels, centred width 3),
  (C) windowed grouped-query attention (+-128 tokens, 4 q heads / 2 kv heads, learned sink logit,
      2-D axial rotary on latent tokens),
  (D) 2-D neighbourhood attention over the latent grid (min(8,ROWS) x 16 clamped window,
      learned per-head relative-position bias).
Each group output is multiplied by its own SiLU gate path, groups are concatenated and passed through ONE
output projection, then added to the residual with the adaLN gate. One final RMSNorm.
Context tokens (modulated by c_ctx) read only context tokens; latent tokens additionally read all context
keys/values in attention mixers C and D inside the same softmax. Mixers A and B treat context and latent
as separate sequences.

Inputs:
  x_prompt  (BATCH, SEQ, D_MODEL)            context tokens of new requests
  x_sample  (DEC_BATCH, DEC_SEQ, D_MODEL)    noisy latent tokens (grid of DEC_SEQ // GRID_W rows)
  cache_c_k, cache_c_v (DEC_BATCH, DEPTH, PAST_LEN, C_KV_HEADS, HEAD_DIM)  context k/v of mixer C
  cache_d_k, cache_d_v (DEC_BATCH, DEPTH, PAST_LEN, D_HEADS, HEAD_DIM)     context k/v of mixer D
  c (DEC_BATCH, D_MODEL) conditioning vectors; c_ctx (D_MODEL,) learned context modulation vector
Output tuple:
  (y_prompt  (BATCH, SEQ, D_MODEL),
   y_sample  (DEC_BATCH, DEC_SEQ, D_MODEL),
   state_c_k, state_c_v (BATCH, DEPTH, SEQ, C_KV_HEADS, HEAD_DIM),
   state_d_k, state_d_v (BATCH, DEPTH, SEQ, D_HEADS, HEAD_DIM))
'''

D_MODEL = 1024
BATCH = 1
SEQ = 128
DEPTH = 2
DEC_BATCH = 1
DEC_SEQ = 1024
PAST_LEN = 128

GRID_W = 64
GROUP_W = 256
D_MIX = 4 * GROUP_W
HEAD_DIM = 64
A_HEADS = 4
CHUNK = 128
C_Q_HEADS = 4
C_KV_HEADS = 2
C_GROUPS = C_Q_HEADS // C_KV_HEADS
WINDOW = 128
QBLK = 128
D_HEADS = 4
WIN_R = 8
WIN_C = 16
CONV_W = 3
ROPE_BASE = 10000.0
EPS = 1e-6
NEG = -1e30
SPLIT_SIZES = (GROUP_W, GROUP_W, GROUP_W,
               GROUP_W, GROUP_W, GROUP_W, GROUP_W,
               C_Q_HEADS * HEAD_DIM, C_KV_HEADS * HEAD_DIM, C_KV_HEADS * HEAD_DIM, GROUP_W,
               D_HEADS * HEAD_DIM, D_HEADS * HEAD_DIM, D_HEADS * HEAD_DIM, GROUP_W)
D_IN = 7 * GROUP_W + (C_Q_HEADS + 2 * C_KV_HEADS) * HEAD_DIM + GROUP_W + 3 * D_HEADS * HEAD_DIM + GROUP_W

kernel_name = 'hybrid_diffusion_denoise_step'

def rmsnorm(x, g):
    xf = x.astype(jnp.float32)
    y = xf * lax.rsqrt(jnp.mean(xf * xf, axis=-1, keepdims=True) + EPS)
    return (y * g.astype(jnp.float32)).astype(x.dtype)

def modulate(x, cond, g, w_mod, b_mod):
    mod = jax.nn.silu(cond) @ w_mod + b_mod
    shift, scale, gate = jnp.split(mod[:, None, :], 3, axis=-1)
    return rmsnorm(x, g) * (1 + scale) + shift, gate

def split_proj(p):
    idx = [int(i) for i in np.cumsum(SPLIT_SIZES)[:-1]]
    return jnp.split(p, idx, axis=-1)

def rope1d(x, pos):
    half = x.shape[-1] // 2
    freqs = ROPE_BASE ** (-jnp.arange(half, dtype=jnp.float32) / half)
    ang = pos.astype(jnp.float32)[:, None] * freqs
    cos = jnp.cos(ang)[:, None, :].astype(x.dtype)
    sin = jnp.sin(ang)[:, None, :].astype(x.dtype)
    x1, x2 = x[..., :half], x[..., half:]
    return jnp.concatenate([x1 * cos - x2 * sin, x1 * sin + x2 * cos], axis=-1)

def rope2d(x):
    t = jnp.arange(x.shape[1])
    half = x.shape[-1] // 2
    return jnp.concatenate([rope1d(x[..., :half], t // GRID_W),
                            rope1d(x[..., half:], t % GRID_W)], axis=-1)

def sink_softmax(s, sink):
    s = s.astype(jnp.float32)
    sink = sink.astype(jnp.float32)
    m = jnp.maximum(jnp.max(s, axis=-1, keepdims=True), sink)
    e = jnp.exp(s - m)
    return e / (jnp.sum(e, axis=-1, keepdims=True) + jnp.exp(sink - m))

def chunk_mlp(u, v, w_s, b_s):
    B, T, _ = v.shape
    n = T // CHUNK
    vh = v.reshape(B, n, CHUNK, A_HEADS, HEAD_DIM)
    vf = vh.astype(jnp.float32)
    vh = (vf * lax.rsqrt(jnp.mean(vf * vf, axis=-1, keepdims=True) + EPS)).astype(v.dtype)
    mixed = jnp.einsum('hpq,bnqhd->bnphd', w_s, vh) + b_s.T[None, None, :, :, None]
    return u * mixed.reshape(B, T, GROUP_W)

def short_conv(bg, cg, h, w_conv):
    xc = cg * h
    xp = jnp.pad(xc, ((0, 0), (1, 1), (0, 0)))
    y = w_conv[0] * xp[:, :-2] + w_conv[1] * xp[:, 1:-1] + w_conv[2] * xp[:, 2:]
    return bg * y

def dense_attn(q, k, v, sink):
    B, L, Hkv, G, dh = q.shape
    nb = L // QBLK
    scale = dh ** -0.5
    qb = jnp.moveaxis(q.reshape(B, nb, QBLK, Hkv, G, dh), 1, 0)

    def block(qi):
        s = jnp.einsum('bqhgd,bkhd->bhgqk', qi, k).astype(jnp.float32) * scale
        if sink is None:
            p = jax.nn.softmax(s, axis=-1)
        else:
            p = sink_softmax(s, sink.reshape(Hkv, G)[None, :, :, None, None])
        return jnp.einsum('bhgqk,bkhd->bqhgd', p.astype(v.dtype), v)

    o = lax.map(block, qb)
    return jnp.moveaxis(o, 0, 1).reshape(B, L, Hkv * G * dh)

def window_attn(q, k, v, kc, vc, sink):
    B, T, Hq, dh = q.shape
    nb = T // QBLK
    scale = dh ** -0.5
    qb = q.reshape(B, nb, QBLK, C_KV_HEADS, C_GROUPS, dh)
    pad = ((0, 0), (QBLK, QBLK), (0, 0), (0, 0))
    kp = jnp.pad(k, pad).reshape(B, nb + 2, QBLK, C_KV_HEADS, dh)
    vp = jnp.pad(v, pad).reshape(B, nb + 2, QBLK, C_KV_HEADS, dh)
    kw = jnp.concatenate([kp[:, :-2], kp[:, 1:-1], kp[:, 2:]], axis=2)
    vw = jnp.concatenate([vp[:, :-2], vp[:, 1:-1], vp[:, 2:]], axis=2)
    n = np.arange(nb)[:, None, None]
    p = np.arange(QBLK)[None, :, None]
    j = np.arange(3 * QBLK)[None, None, :]
    kpos = (n - 1) * QBLK + j
    qpos = n * QBLK + p
    mask = jnp.asarray((np.abs(kpos - qpos) <= WINDOW) & (kpos >= 0) & (kpos < T))
    s_loc = jnp.einsum('bnqhgd,bnjhd->bnhgqj', qb, kw).astype(jnp.float32) * scale
    s_loc = jnp.where(mask[None, :, None, None], s_loc, NEG)
    s_ctx = jnp.einsum('bnqhgd,blhd->bnhgql', qb, kc).astype(jnp.float32) * scale
    pr = sink_softmax(jnp.concatenate([s_loc, s_ctx], axis=-1),
                      sink.reshape(C_KV_HEADS, C_GROUPS)[None, None, :, :, None, None]).astype(v.dtype)
    p_loc, p_ctx = pr[..., :3 * QBLK], pr[..., 3 * QBLK:]
    o = (jnp.einsum('bnhgqj,bnjhd->bnqhgd', p_loc, vw)
         + jnp.einsum('bnhgql,blhd->bnqhgd', p_ctx, vc))
    return o.reshape(B, T, Hq * dh)

def neighbourhood_attn(q, k, v, kc, vc, rpb):
    B, T, H, dh = q.shape
    rows = T // GRID_W
    kr = min(WIN_R, rows)
    scale = dh ** -0.5
    qg = q.reshape(B, rows, GRID_W, H, dh)
    kg = k.reshape(B, rows, GRID_W, H, dh)
    vg = v.reshape(B, rows, GRID_W, H, dh)
    cols = np.arange(GRID_W)
    cstart = np.clip(cols - WIN_C // 2, 0, GRID_W - WIN_C)
    col_idx = cstart[:, None] + np.arange(WIN_C)
    dc = col_idx - cols[:, None] + (WIN_C - 1)
    rpb_c = rpb[:, :, dc]

    def one_row(r):
        rs = jnp.clip(r - kr // 2, 0, rows - kr)
        ridx = rs + jnp.arange(kr)
        k_nb = jnp.take(kg, ridx, axis=1)[:, :, col_idx]
        v_nb = jnp.take(vg, ridx, axis=1)[:, :, col_idx]
        qr = lax.dynamic_index_in_dim(qg, r, axis=1, keepdims=False)
        s_loc = jnp.einsum('bchd,brcwhd->bhcrw', qr, k_nb).astype(jnp.float32) * scale
        bias = jnp.transpose(jnp.take(rpb_c, ridx - r + (WIN_R - 1), axis=1), (0, 2, 1, 3))
        s_loc = s_loc + bias[None].astype(jnp.float32)
        s_ctx = jnp.einsum('bchd,blhd->bhcl', qr, kc).astype(jnp.float32) * scale
        s = jnp.concatenate([s_loc.reshape(B, H, GRID_W, kr * WIN_C), s_ctx], axis=-1)
        pr = jax.nn.softmax(s, axis=-1).astype(v.dtype)
        p_loc = pr[..., :kr * WIN_C].reshape(B, H, GRID_W, kr, WIN_C)
        p_ctx = pr[..., kr * WIN_C:]
        return (jnp.einsum('bhcrw,brcwhd->bchd', p_loc, v_nb)
                + jnp.einsum('bhcl,blhd->bchd', p_ctx, vc))

    o = lax.map(one_row, jnp.arange(rows))
    return jnp.moveaxis(o, 0, 1).reshape(B, T, H * dh)

def project(x, cond, g, w_mod, b_mod, w_in):
    h, gate = modulate(x, cond, g, w_mod, b_mod)
    return split_proj(h @ w_in), gate

def branches_ab(parts, w_s, b_s, w_conv):
    au, av, az, bb, bc, bh, bz = parts
    ya = chunk_mlp(au, av, w_s, b_s) * jax.nn.silu(az)
    yb = short_conv(bb, bc, bh, w_conv) * jax.nn.silu(bz)
    return ya, yb

def context_layer(x, c_ctx, g, w_mod, b_mod, w_in, w_out, w_s, b_s, w_conv, sink):
    B, L, _ = x.shape
    parts, gate = project(x, c_ctx[None, :], g, w_mod, b_mod, w_in)
    ya, yb = branches_ab(parts[:7], w_s, b_s, w_conv)
    cq, ck, cv, cz, dq, dk, dv, dz = parts[7:]
    ck = ck.reshape(B, L, C_KV_HEADS, HEAD_DIM)
    cv = cv.reshape(B, L, C_KV_HEADS, HEAD_DIM)
    dk = dk.reshape(B, L, D_HEADS, HEAD_DIM)
    dv = dv.reshape(B, L, D_HEADS, HEAD_DIM)
    yc = dense_attn(cq.reshape(B, L, C_KV_HEADS, C_GROUPS, HEAD_DIM), ck, cv, sink) * jax.nn.silu(cz)
    yd = dense_attn(dq.reshape(B, L, D_HEADS, 1, HEAD_DIM), dk, dv, None) * jax.nn.silu(dz)
    y = jnp.concatenate([ya, yb, yc, yd], axis=-1) @ w_out
    return x + gate * y, ck, cv, dk, dv

def latent_layer(x, c, kc, vc, kd, vd, g, w_mod, b_mod, w_in, w_out, w_s, b_s, w_conv, sink, rpb):
    B, T, _ = x.shape
    parts, gate = project(x, c, g, w_mod, b_mod, w_in)
    ya, yb = branches_ab(parts[:7], w_s, b_s, w_conv)
    cq, ck, cv, cz, dq, dk, dv, dz = parts[7:]
    cq = rope2d(cq.reshape(B, T, C_Q_HEADS, HEAD_DIM))
    ck = rope2d(ck.reshape(B, T, C_KV_HEADS, HEAD_DIM))
    cv = cv.reshape(B, T, C_KV_HEADS, HEAD_DIM)
    yc = window_attn(cq, ck, cv, kc, vc, sink) * jax.nn.silu(cz)
    yd = neighbourhood_attn(dq.reshape(B, T, D_HEADS, HEAD_DIM), dk.reshape(B, T, D_HEADS, HEAD_DIM),
                            dv.reshape(B, T, D_HEADS, HEAD_DIM), kd, vd, rpb) * jax.nn.silu(dz)
    y = jnp.concatenate([ya, yb, yc, yd], axis=-1) @ w_out
    return x + gate * y

def setup_inputs(seed: int = 0) -> dict:
    key = jax.random.key(seed)
    ks = jax.random.split(key, 20)
    nrm = jax.random.normal
    f32 = jnp.float32
    return {
        'x_prompt': nrm(ks[0], (BATCH, SEQ, D_MODEL), f32),
        'x_sample': nrm(ks[1], (DEC_BATCH, DEC_SEQ, D_MODEL), f32),
        'cache_c_k': nrm(ks[2], (DEC_BATCH, DEPTH, PAST_LEN, C_KV_HEADS, HEAD_DIM), f32),
        'cache_c_v': nrm(ks[3], (DEC_BATCH, DEPTH, PAST_LEN, C_KV_HEADS, HEAD_DIM), f32),
        'cache_d_k': nrm(ks[4], (DEC_BATCH, DEPTH, PAST_LEN, D_HEADS, HEAD_DIM), f32),
        'cache_d_v': nrm(ks[5], (DEC_BATCH, DEPTH, PAST_LEN, D_HEADS, HEAD_DIM), f32),
        'c': nrm(ks[6], (DEC_BATCH, D_MODEL), f32),
        'c_ctx': nrm(ks[7], (D_MODEL,), f32),
        'norm_g': 1.0 + 0.02 * nrm(ks[8], (DEPTH, D_MODEL), f32),
        'w_mod': 0.5 * D_MODEL ** -0.5 * nrm(ks[9], (DEPTH, D_MODEL, 3 * D_MODEL), f32),
        'b_mod': 0.02 * nrm(ks[10], (DEPTH, 3 * D_MODEL), f32),
        'w_in': D_MODEL ** -0.5 * nrm(ks[11], (DEPTH, D_MODEL, D_IN), f32),
        'w_out': D_MIX ** -0.5 * nrm(ks[12], (DEPTH, D_MIX, D_MODEL), f32),
        'w_s': CHUNK ** -0.5 * nrm(ks[13], (DEPTH, A_HEADS, CHUNK, CHUNK), f32),
        'b_s': 1.0 + 0.02 * nrm(ks[14], (DEPTH, A_HEADS, CHUNK), f32),
        'w_conv': CONV_W ** -0.5 * nrm(ks[15], (DEPTH, CONV_W, GROUP_W), f32),
        'sink': 0.5 * nrm(ks[16], (DEPTH, C_Q_HEADS), f32),
        'rpb': 0.1 * nrm(ks[17], (DEPTH, D_HEADS, 2 * WIN_R - 1, 2 * WIN_C - 1), f32),
        'final_g': 1.0 + 0.02 * nrm(ks[18], (D_MODEL,), f32),
    }

def reference(x_prompt, x_sample, cache_c_k, cache_c_v, cache_d_k, cache_d_v, c, c_ctx,
              norm_g, w_mod, b_mod, w_in, w_out, w_s, b_s, w_conv, sink, rpb, final_g):
    xp = x_prompt
    xs = x_sample
    ck_list, cv_list, dk_list, dv_list = [], [], [], []
    for l in range(DEPTH):
        xp, ck, cv, dk, dv = context_layer(xp, c_ctx, norm_g[l], w_mod[l], b_mod[l], w_in[l], w_out[l],
                                           w_s[l], b_s[l], w_conv[l], sink[l])
        ck_list.append(ck)
        cv_list.append(cv)
        dk_list.append(dk)
        dv_list.append(dv)
        xs = latent_layer(xs, c, cache_c_k[:, l], cache_c_v[:, l], cache_d_k[:, l], cache_d_v[:, l],
                          norm_g[l], w_mod[l], b_mod[l], w_in[l], w_out[l], w_s[l], b_s[l], w_conv[l],
                          sink[l], rpb[l])
    y_prompt = rmsnorm(xp, final_g)
    y_sample = rmsnorm(xs, final_g)
    state_c_k = jnp.stack(ck_list, axis=1)
    state_c_v = jnp.stack(cv_list, axis=1)
    state_d_k = jnp.stack(dk_list, axis=1)
    state_d_v = jnp.stack(dv_list, axis=1)
    return (y_prompt, y_sample, state_c_k, state_c_v, state_d_k, state_d_v)


_drawn_inputs = setup_inputs


def setup_inputs(seed=0):
    import zlib

    import numpy as np

    out = dict(_drawn_inputs(seed))
    spreads = {}
    factors = {'cache_c_k': 8.0,
     'cache_c_v': 7.693,
     'cache_d_k': 6.697,
     'cache_d_v': 5.416,
     'norm_g': 2.882,
     'b_s': 8.0,
     'sink': 64.0,
     'rpb': 64.0,
     'final_g': 2.874}
    for name, (base, spread) in spreads.items():
        noise = np.random.default_rng([zlib.crc32(name.encode()), seed]).standard_normal(out[name].shape)
        drawn = base * np.exp(spread * noise) if base else spread * noise
        out[name] = __import__('jax').numpy.asarray(drawn.astype(out[name].dtype))
    for name, factor in factors.items():
        out[name] = (out[name] * factor).astype(out[name].dtype)
    return out
```

```python
from contextlib import ExitStack

import numpy as np

import concourse.bass as bass
from concourse import mybir

F32 = mybir.dt.float32
F32R = mybir.dt.float32r
I32 = mybir.dt.int32
ALU = mybir.AluOpType
ACT = mybir.ActivationFunctionType
AX_X = mybir.AxisListType.X

P = 128
D_MODEL = 1024
DEPTH = 2
SEQ = 128
DEC_SEQ = 1024
T = DEC_SEQ + SEQ
KT = D_MODEL // P
CH = 384
NCH = T // CH
TT = T // P
LT = DEC_SEQ // P
GRID_W = 64
ROWS = DEC_SEQ // GRID_W
WIN_R = 8
WIN_C = 16
HEAD_DIM = 64
EPS = 1e-6
NEG = -1e30
SCALE = HEAD_DIM ** -0.5
ROPE_BASE = 10000.0

TILES = [("av", 0), ("av", 1), ("az", 0), ("au", 0), ("az", 1), ("au", 1),
         ("bz", 0), ("bb", 0), ("bc", 0), ("bh", 0), ("bz", 1), ("bb", 1), ("bc", 1), ("bh", 1),
         ("cz", 0), ("cz", 1), ("cq", 0), ("cq", 1), ("ck", 0), ("cv", 0),
         ("dz", 0), ("dz", 1), ("dv", 0), ("dv", 1), ("dk", 0), ("dk", 1), ("dq", 0), ("dq", 1)]
N_IN = len(TILES)
NO = {x: n for n, x in enumerate(TILES)}
N_TILES = N_IN + KT
COLUMNS = {"au": 0, "av": 256, "az": 512, "bb": 768, "bc": 1024, "bh": 1280, "bz": 1536, "cq": 1792,
           "ck": 2048, "cv": 2176, "cz": 2304, "dq": 2560, "dk": 2816, "dv": 3072, "dz": 3328}
C_HEADS = (0, 2, 1, 3)
COPIED = ("av", "bc", "cq", "ck", "cv", "dv", "dk", "dq")

REL0 = -6
BIAS_N = 14 * GRID_W
ZERO0 = BIAS_N
INNER0 = ZERO0 + P
TABLE = INNER0 + 9 * GRID_W
S_D = P + 9 * GRID_W
RSQRT_MAGIC = 0x5F3759DF


def d_window(i):
    lo = min(max(2 * i - WIN_R // 2, 0), ROWS - WIN_R)
    hi = min(max(2 * i + 1 - WIN_R // 2, 0), ROWS - WIN_R) + WIN_R
    return lo, hi - lo


def attention_units():
    units = [("C", i, t, r) for i in range(LT + 1) for t in range(2) for r in range(2)]
    units += [("D", i, t, r) for t in range(2) for r in range(2) for i in range(LT + 1)]
    return units


UNITS = attention_units()
NU = len(UNITS)
N_C = sum(u[0] == "C" for u in UNITS)


def build(nc, xT, cond, w_mod, b_mod, norm_g, final_g, w_tiles, w_sT, b_s, w_conv, sink, rpb,
          cckT, ccv, cdkT, cdv, ident_c, rope_c, band_c, window_c, yT, sckT, scvT, sdkT, sdvT):
    with ExitStack() as ctx:
        def sb(name, shape, dt=F32):
            return ctx.enter_context(nc.sbuf_tensor(name, shape, dt))

        def sem(name):
            return ctx.enter_context(nc.semaphore(name))

        x_kept = nc.dram_tensor("x_kept", [P, KT, T], F32, kind="Internal").ap()

        h_hi = sb("h_hi", [P, KT, T], F32R)
        h_lo = sb("h_lo", [P, KT, T], F32R)
        xy = sb("xy", [P, KT, T])
        slots = sb("slots", [P, 10, T])
        w_raw = sb("w_raw", [P, 2, KT, P])
        w_hi = sb("w_hi", [P, 2, KT, P], F32R)
        w_lo = sb("w_lo", [P, 2, KT, P], F32R)
        prob = sb("prob", [P, 3, S_D])
        probT = sb("probT", [P, 2, 6 * P])
        table = sb("table", [P, 2, TABLE])
        ident = sb("ident", [P, P])
        window = sb("window", [P, 2, GRID_W])
        ck_d = sb("ck_d", [P, 2, P])
        cv_d = sb("cv_d", [P, 2, P])
        mods = sb("mods", [P, DEPTH, 24, 2])
        mod = sb("mod", [P, 24, 2])
        fin_g = sb("fin_g", [P, KT])
        conv_w = sb("conv_w", [P, 2, 3])
        sinks = sb("sinks", [P, 4])
        stat = sb("stat", [P, 4, 4])
        psum = ctx.enter_context(nc.psum_tensor("psum", [P, 8, 512], F32))

        qC, kC, qD, kD = (lambda t: slots[:, t]), slots[:, 2], (lambda t: slots[:, 3 + t]), (lambda t: slots[:, 5 + t])
        vC = slots[:, 7].rearrange("p (t d) -> p t d", t=TT)
        vD = slots[:, 8:10].rearrange("p a n -> p (a n)").rearrange("p (t d) -> p t d", t=TT)
        flat_prob = prob[:, :, :].rearrange("p a n -> p (a n)")
        flat_probT = probT[:, :, :].rearrange("p a n -> p (a n)")
        flat_table = table[:, :, :].rearrange("p a n -> p (a n)")
        squares = flat_prob[:, 0:T]
        square = flat_probT[:, 0:T]
        small = flat_prob[:, T:T + 8 * 36].rearrange("p (a n) -> p a n", a=8)
        ck_c = probT[:, 1, 4 * P:5 * P]
        cv_c = probT[:, 1, 5 * P:6 * P]
        wsT = probT[:, 0, 0:4 * P].rearrange("p (h n) -> p h n", h=4)
        bs = probT[:, 0, 4 * P:6 * P].rearrange("p (j n) -> p j n", j=2)
        cos_t = flat_table[:, 0:DEC_SEQ]
        sin_t = flat_table[:, DEC_SEQ:2 * DEC_SEQ]
        swapped = flat_table[:, 2 * DEC_SEQ:3 * DEC_SEQ]
        x_new = flat_table[:, 0:2 * T].rearrange("p (a n) -> p a n", a=2)
        band = table[:, 1, 0:4 * P]
        BANK_A = 6

        def chunks(ap):
            return ap.rearrange("p (c n) -> p c n", c=NCH)

        def tile_read(eng, n):
            eng.wait_ge(set_free[n % 2], n // 2 + 1)

        def tile_psum(n):
            return psum[:, 3 * (n % 2):3 * (n % 2) + 3, 0:CH]

        consts_in = sem("consts_in")
        x_in = sem("x_in")
        wmod_in = [sem(f"wmod_in{i}") for i in range(3)]
        cond_tanh = sem("cond_tanh")
        cond_ready = sem("cond_ready")
        wmod_used = sem("wmod_used")
        modrow_ready = sem("modrow_ready")
        modT_ready = sem("modT_ready")
        modT_read = sem("modT_read")
        x_squared = sem("x_squared")
        squares_added = sem("squares_added")
        pro_step = sem("pro_step")

        stage = slots[:, :, :].rearrange("p a n -> p (a n)")
        wmod_sb = stage[:, 0:3 * 3072].rearrange("p (b n) -> p b n", b=3)
        modrow = w_raw[:, :, :, :].rearrange("p a k n -> p a (k n)")[:, :, 0:1024]
        silu_c = stage[:, 9216:9216 + KT * 32].rearrange("p (k m) -> p k m", k=KT)
        cond_sb = stage[:, 9472:9472 + 2 * KT].rearrange("p (k c) -> p k c", c=2)
        tanh_c = stage[:, 9488:9488 + 2 * KT].rearrange("p (k c) -> p k c", c=2)
        bmod_sb = stage[:, 9504:9504 + 24 * DEPTH].rearrange("p (l n) -> p l n", l=DEPTH)
        ng_sb = stage[:, 9552:9552 + KT * DEPTH].rearrange("p (l n) -> p l n", l=DEPTH)
        CONSTS = 6

        with nc.Block() as block:
            @block.sync
            def _(sp):
                sp.dma_start(cond_sb, cond).then_inc(consts_in, 16)
                sp.dma_start(ident[:, :], ident_c).then_inc(consts_in, 16)
                sp.dma_start(bmod_sb, b_mod).then_inc(consts_in, 16)
                sp.dma_start(ng_sb, norm_g).then_inc(consts_in, 16)
                sp.dma_start(window[:, :, :], window_c).then_inc(consts_in, 16)
                sp.dma_start(fin_g[:, :], final_g).then_inc(consts_in, 16)
                for n in range(DEPTH * KT):
                    if n >= 3:
                        sp.wait_ge(wmod_used, n - 2)
                    sp.dma_start(wmod_sb[:, n % 3], w_mod[n // KT, (n % KT) * P:(n % KT + 1) * P, :]
                                 ).then_inc(wmod_in[n % 3], 16)
                    if n == 2:
                        for k in range(KT):
                            sp.dma_start(xy[:, k], xT[k]).then_inc(x_in, 16)
                sp.wait_ge(x_in, 16 * KT)
                sp.dma_start(x_kept, xy[:, :, :]).then_inc(x_in, 16)
                sp.wait_ge(x_in, 16 * KT + 16)

            @block.scalar
            def _(act):
                act.wait_ge(consts_in, 16 * CONSTS)
                nc.scalar.activation(tanh_c, cond_sb, ACT.Tanh, scale=0.5).then_inc(cond_tanh, 1)
                act.wait_ge(x_in, 16 * KT)
                nc.scalar.activation(squares, xy[:, 0], ACT.Square).then_inc(x_squared, 1)
                for k in range(1, KT):
                    if k > 1:
                        act.wait_ge(squares_added, k - 1)
                    nc.scalar.activation(square, xy[:, k], ACT.Square).then_inc(x_squared, 1)

            @block.tensor
            def _(pe):
                pe.wait_ge(cond_ready, 1)
                for l in range(DEPTH):
                    for k in range(KT):
                        n = l * KT + k
                        pe.wait_ge(wmod_in[n % 3], 16 * (n // 3 + 1))
                        for c in range(6):
                            q = 32 * (c % 4)
                            last = nc.tensor.matmul(psum[q:q + 32, 2 * l + c // 4, :], silu_c[:, k, :],
                                                    wmod_sb[:, n % 3, c * 512:(c + 1) * 512],
                                                    start=(k == 0), stop=(k == KT - 1), skip_group_check=True)
                        last.then_inc(wmod_used, 1)
                for l in range(DEPTH):
                    pe.wait_ge(modrow_ready, 2 * (l + 1))
                    if l > 0:
                        pe.wait_ge(modT_read, l)
                    for b in range(2):
                        rows = P if b == 0 else 64
                        for j in range(4):
                            last = nc.tensor.transpose(psum[:, 4 + b, j * P:j * P + rows],
                                                       modrow[0:rows, l, b * 512 + j * P:b * 512 + (j + 1) * P],
                                                       ident[0:rows, 0:rows])
                    last.then_inc(modT_ready, 1)

            @block.vector
            def _(dve):
                step = [0]

                def own(ins):
                    ins.then_inc(pro_step, 1)
                    step[0] += 1

                def settle():
                    dve.wait_ge(pro_step, step[0])

                own(nc.vector.memset(silu_c, 0.0))
                dve.wait_ge(cond_tanh, 1)
                settle()
                own(nc.vector.scalar_tensor_tensor(tanh_c, tanh_c, 1.0, cond_sb, ALU.add, ALU.mult))
                settle()
                nc.vector.tensor_scalar(silu_c[:, :, 0:2], tanh_c, 0.5, None, ALU.mult).then_inc(cond_ready, 1)
                for k in range(1, KT):
                    dve.wait_ge(x_squared, k + 1)
                    if k > 1:
                        dve.wait_ge(squares_added, k - 1)
                    nc.vector.tensor_tensor(squares, squares, square, ALU.add).then_inc(squares_added, 1)
                for l in range(DEPTH):
                    dve.wait_ge(wmod_used, (l + 1) * KT)
                    nc.vector.tensor_copy(modrow[:, l, 0:512], psum[:, 2 * l, :]).then_inc(modrow_ready, 1)
                    nc.vector.tensor_copy(modrow[0:64, l, 512:1024], psum[0:64, 2 * l + 1, :]
                                          ).then_inc(modrow_ready, 1)
                    dve.wait_ge(modT_ready, l + 1)
                    for b in range(2):
                        nq = 4 if b == 0 else 2
                        src = psum[:, 4 + b, :].rearrange("p (j n) -> p j n", j=4)[:, :, 0:32 * nq]
                        src = src.rearrange("p j (q m) -> p q j m", q=nq)
                        for cnd in range(2):
                            dst = mods[:, l, 16 * b:16 * b + 4 * nq, cnd].rearrange("p (q j) -> p q j", q=nq)
                            bias = bmod_sb[:, l, 16 * b:16 * b + 4 * nq].rearrange("p (q j) -> p q j", q=nq)
                            ins = nc.vector.tensor_tensor(dst, src[:, :, :, cnd], bias, ALU.add)
                            own(ins)
                    settle()
                    for cnd in range(2):
                        ins = nc.vector.scalar_tensor_tensor(mods[:, l, 8:16, cnd], mods[:, l, 8:16, cnd], 1.0,
                                                             ng_sb[:, l], ALU.add, ALU.mult)
                        if cnd == 0:
                            own(ins)
                        else:
                            ins.then_inc(modT_read, 1)

        names = ["layer_in", "w_loaded0", "w_loaded1", "hi_ready", "lo_ready", "tile_done", "set_free0",
                 "set_free1", "sums_ready", "diag_ready", "rstd_ready", "scaled", "h_hi_ready", "h_ready",
                 "mod_ready", "x_saved", "tanh_ready", "av_turned", "av_natural",
                 "av_normal", "mixed", "mix_read", "cv_turned", "cv_natural", "dv_turned", "dv_natural",
                 "swap_ready", "cos_ready", "rope_ready", "c_out", "v_out", "k_out", "rope_in",
                 "band_in", "bias_in0", "bias_in1", "bias_ready", "scores_ready", "biased", "expd", "normed", "turned",
                 "turned_act", "turned_dve", "values_ready", "y_hi_ready", "y_split", "x_loaded0", "x_loaded1",
                 "x_sq", "sq_added", "act_step", "dve_step", "pool_step", "mix_in", "sink_put",
                 "bc_used", "gated", "ones_ready"]
        S = {n: sem(n) for n in names}
        nums = [S[n].num for n in names]
        layer_sems = range(min(nums), max(nums) + 1)
        assert len(layer_sems) == len(names)
        (layer_in, w_loaded0, w_loaded1, hi_ready, lo_ready, tile_done, set_free0, set_free1, sums_ready,
         diag_ready, rstd_ready, scaled, h_hi_ready, h_ready, mod_ready, x_saved, tanh_ready, 
         av_turned, av_natural, av_normal, mixed, mix_read, cv_turned, cv_natural, dv_turned, dv_natural,
         swap_ready, cos_ready, rope_ready, c_out, v_out, k_out, rope_in, band_in, bias_in0, bias_in1, bias_ready,
         scores_ready, biased, expd, normed, turned, turned_act, turned_dve, values_ready, y_hi_ready,
         y_split, x_loaded0, x_loaded1, x_sq, sq_added, act_step, dve_step, pool_step, mix_in, sink_put,
         bc_used, gated, ones_ready) = [S[n] for n in names]
        w_loaded = (w_loaded0, w_loaded1)
        set_free = (set_free0, set_free1)
        bias_in = (bias_in0, bias_in1)
        x_loaded = (x_loaded0, x_loaded1)

        diag = slots[:, 8].rearrange("p (t n) -> p t n", t=TT)
        ones = slots[:, 9, 0:P]
        RSTD_BANK = 3

        def norm_pe(pe):
            pe.wait_ge(ones_ready, 1)
            for t in range(TT):
                last = nc.tensor.matmul(psum[:, BANK_A, t:t + 1], squares[:, t * P:(t + 1) * P], ones[:, 0:1],
                                        start=True, stop=True)
            last.then_inc(sums_ready, 1)
            for t in range(TT):
                pe.wait_ge(diag_ready, t + 1)
                nc.tensor.matmul(psum[:, RSTD_BANK + t // 3, (t % 3) * P:(t % 3 + 1) * P], ones[:, :], diag[:, t],
                                 start=True, stop=True).then_inc(rstd_ready, 1)

        def rsqrt(own, settle, out, v, s0, s1):
            own(nc.vector.tensor_scalar(s0.bitcast(I32), v.bitcast(I32), 1, None, ALU.arith_shift_right))
            settle()
            own(nc.vector.tensor_scalar(out.bitcast(I32), s0.bitcast(I32), -1, RSQRT_MAGIC, ALU.mult, ALU.add))
            settle()
            for _ in range(4):
                own(nc.vector.tensor_tensor(s0, out, out, ALU.mult))
                settle()
                own(nc.vector.tensor_tensor(s1, s0, v, ALU.mult))
                settle()
                own(nc.vector.tensor_scalar(s0, s1, -0.5, 1.5, ALU.mult, ALU.add))
                settle()
                own(nc.vector.tensor_tensor(out, out, s0, ALU.mult))
                settle()

        def norm_dve(dve, own, settle):
            ms, rstd = small[:, 0, 0:TT], small[:, 1, 0:TT]
            nc.vector.memset(ones, 1.0).then_inc(ones_ready, 1)
            dve.wait_ge(sums_ready, 1)
            own(nc.vector.tensor_scalar(ms, psum[:, BANK_A, 0:TT], 1.0 / D_MODEL, EPS, ALU.mult, ALU.add))
            settle()
            rsqrt(own, settle, rstd, ms, small[:, 2, 0:TT], small[:, 3, 0:TT])
            for t in range(TT):
                nc.vector.tensor_scalar(diag[:, t], ident[:, :], rstd[:, t:t + 1], None, ALU.mult
                                        ).then_inc(diag_ready, 1)

        def pieces():
            return [(slice(0, 2), slice(0, CH), 0), (slice(2, 3), slice(0, DEC_SEQ - 2 * CH), 0),
                    (slice(2, 3), slice(DEC_SEQ - 2 * CH, CH), 1)]

        LAT, CTX = slice(0, DEC_SEQ), slice(DEC_SEQ, T)
        PARTS = ((LAT, 0), (CTX, 1))

        def c_keys(i):
            return [(i + d, at) for d, at in ((-1, 0), (0, P), (1, 3 * P)) if 0 <= i + d < LT]

        def base(u):
            return P if (UNITS[u][0] == "C" and UNITS[u][1] == 0) else 0

        def score_pieces(u):
            mixer, i, t, r = UNITS[u]
            half = slice(64 * r, 64 * r + 64)
            if mixer == "C":
                if i == LT:
                    return [(kC[half, CTX], 0, P)]
                off = base(u)
                return ([(kC[half, k * P:(k + 1) * P], at - off, P) for k, at in c_keys(i)]
                        + [(ck_c[half, :], 2 * P - off, P)])
            k = kD(t)
            if i == LT:
                return [(k[half, CTX], 0, P)]
            lo, rows = d_window(i)
            first = min(rows * GRID_W, 512 - P)
            out = [(ck_d[half, t, :], 0, P), (k[half, lo * GRID_W:lo * GRID_W + first], P, first)]
            rest = rows * GRID_W - first
            out.append((k[half, lo * GRID_W + first:(lo + rows) * GRID_W], 512, rest))
            return out

        def unit_width(u):
            return sum(w for _, _, w in score_pieces(u))

        def key_tiles(u):
            mixer, i, t, r = UNITS[u]
            if mixer == "C":
                d = slice(64 * r, 64 * r + 64)
                if i == LT:
                    return [(0, P, vC[:, LT, d])]
                off = base(u)
                return sorted([(at - off, P, vC[:, k, d]) for k, at in c_keys(i)]
                              + [(2 * P - off, P, cv_c[:, d])], key=lambda x: x[0])
            d = slice((2 * t + r) * 64, (2 * t + r + 1) * 64)
            if i == LT:
                return [(0, P, vD[:, LT, d])]
            lo, rows = d_window(i)
            out = [(0, P, cv_d[:, t, r * 64:(r + 1) * 64])]
            for b in range((rows + 1) // 2):
                w = min(P, rows * GRID_W - b * P)
                out.append((P + b * P, w, vD[0:w, lo // 2 + b, d]))
            return out

        with nc.Fori(0, DEPTH) as layer:
          with nc.Block() as block:

            @block.sync
            def _(sp):
                def load_weights(n):
                    sp.dma_start(w_raw[:, n % 2], w_tiles[layer, n]).then_inc(w_loaded[n % 2], 16)

                load_weights(0)
                load_weights(1)
                sp.dma_start(conv_w[:, :, :], w_conv[layer]).then_inc(layer_in, 16)
                sp.dma_start(sinks[:, :], sink[layer]).then_inc(layer_in, 16)
                sp.dma_start(ck_c, cckT[layer]).then_inc(layer_in, 16)
                sp.dma_start(cv_c, ccv[layer]).then_inc(layer_in, 16)
                sp.dma_start(ck_d[:, :, :], cdkT[layer]).then_inc(layer_in, 16)
                sp.dma_start(cv_d[:, :, :], cdv[layer]).then_inc(layer_in, 16)
                sp.dma_start(flat_table[:, 0:2 * DEC_SEQ], rope_c).then_inc(rope_in, 16)
                sp.dma_start(wsT, w_sT[layer]).then_inc(mix_in, 16)
                sp.dma_start(bs, b_s[layer]).then_inc(mix_in, 16)

                def weights(lo, hi):
                    with sp.Fori(lo // 2, hi // 2) as pair:
                        for p in range(2):
                            sp.wait_ge(lo_ready, 2 * pair + p - 1)
                            sp.dma_start(w_raw[:, p], w_tiles[layer, 2 * pair + p]).then_inc(w_loaded[p], 16)

                weights(2, 28)
                sp.wait_ge(rope_ready, 3)
                sp.dma_start(band, band_c).then_inc(band_in, 16)

                def load_bias(h):
                    sp.dma_start(table[:, h % 2, 0:BIAS_N], rpb[layer, h]).then_inc(bias_in[h % 2], 16)

                load_bias(0)
                weights(28, 30)
                for h in range(1, 4):
                    sp.wait_ge(biased, N_C + (h - 1) * (LT + 1))
                    load_bias(h)
                sp.wait_ge(biased, NU)
                for f in range(KT):
                    if f >= 2:
                        tile_read(sp, N_IN + f - 2)
                    sp.dma_start(x_new[:, f % 2], x_kept[:, f]).then_inc(x_loaded[f % 2], 16)
                    if 2 <= f:
                        n = N_IN + f
                        sp.wait_ge(lo_ready, n - 1)
                        load_weights(n)
                for f in range(KT):
                    tile_read(sp, N_IN + f)
                    sp.dma_start(x_kept[:, f], xy[:, f]).then_inc(x_saved, 16)
                sp.wait_ge(x_saved, 16 * KT)
                for done in (c_out, v_out, k_out):
                    sp.wait_ge(done, 32)

            @block.gpsimd
            def _(pool):
                def low_halves(lo, hi):
                    with pool.Fori(lo // 2, hi // 2) as pair:
                        for p in range(2):
                            pool.wait_ge(hi_ready, 2 * pair + p + 1)
                            nc.gpsimd.tensor_tensor(w_lo[:, p], w_raw[:, p], w_hi[:, p], ALU.subtract
                                                    ).then_inc(lo_ready, 1)

                low_halves(0, 18)
                for t in range(3):
                    pool.wait_ge(swap_ready, t + 1)
                    if t == 0:
                        pool.wait_ge(rope_in, 16)
                    raw = slots[:, t, LAT]
                    nc.gpsimd.tensor_tensor(raw, raw, cos_t, ALU.mult).then_inc(cos_ready, 1)
                    if t == 1:
                        low_halves(18, 20)
                low_halves(20, 28)
                step = [0]

                def own(ins):
                    ins.then_inc(pool_step, 1)
                    step[0] += 1

                def settle():
                    pool.wait_ge(pool_step, step[0])

                def make_bias(h):
                    tab = table[:, h % 2]
                    rel = tab[:, 0:BIAS_N].rearrange("p (j k) -> p j k", j=14)
                    keep = window[:, 0:1, :].broadcast_to([P, 14, GRID_W])
                    drop = window[:, 1:2, :].broadcast_to([P, 14, GRID_W])
                    pool.wait_ge(bias_in[h % 2], 16 * (h // 2 + 1))
                    own(nc.gpsimd.tensor_tensor(rel, rel, keep, ALU.mult))
                    settle()
                    own(nc.gpsimd.tensor_tensor(rel, rel, drop, ALU.add))
                    own(nc.gpsimd.memset(tab[:, ZERO0:INNER0], 0.0))
                    settle()
                    inner = (-4 - REL0) * GRID_W
                    own(nc.gpsimd.tensor_copy(tab[:, INNER0:TABLE], tab[:, inner:inner + 9 * GRID_W]))
                    settle()
                    own(nc.gpsimd.memset(tab[GRID_W:P, INNER0:INNER0 + GRID_W], -NEG))
                    settle()
                    nc.gpsimd.memset(tab[0:GRID_W, TABLE - GRID_W:TABLE], -NEG).then_inc(bias_ready, 1)

                make_bias(0)
                low_halves(28, 30)
                for h in range(1, 4):
                    make_bias(h)
                low_halves(30, N_TILES)

            @block.scalar
            def _(act):
                def high_half(n):
                    act.wait_ge(w_loaded[n % 2], 16 * (n // 2 + 1))
                    if n >= 2:
                        act.wait_ge(tile_done, n - 1)
                    nc.scalar.copy(w_hi[:, n % 2], w_raw[:, n % 2]).then_inc(hi_ready, 1)

                high_half(0)
                nc.scalar.copy(mod[:, :, :], mods[:, layer]).then_inc(mod_ready, 1)
                act.wait_ge(mod_ready, 1)
                for k in range(KT):
                    act.wait_ge(scaled, k + 1)
                    for cols, c in PARTS:
                        last = nc.scalar.activation(h_hi[:, k, cols], slots[:, k, cols], ACT.Identity,
                                                    bias=mod[:, k, c:c + 1])
                    last.then_inc(h_hi_ready, 1)
                naturals = {"av": (av_turned, av_natural), "cv": (cv_turned, cv_natural),
                            "dv": (dv_turned, dv_natural)}

                def copy_turned(part, dst_of, count):
                    sem_in, sem_out = naturals[part]
                    for q in range(count):
                        act.wait_ge(sem_in, q + 1)
                        nc.scalar.copy(dst_of(q), psum[:, BANK_A + q % 2, 0:CH].rearrange("p (t d) -> p t d", t=3)
                                       ).then_inc(sem_out, 1)

                two_tiles = lambda v: (lambda q: v[:, 3 * (q % 3):3 * (q % 3) + 3, P * (q // 3):P * (q // 3) + P])
                n_tanh = 0
                gates = [n for n, x in enumerate(TILES) if x[0][1] == "z"]
                for n, (part, t) in enumerate(TILES):
                    high_half(n + 1)
                    if part[1] == "z":
                        act.wait_ge(tile_done, n + 1)
                        before = gates[n_tanh - 2] if part != "dz" else NO[("cz", 0) if t == 0 else ("dz", 0)]
                        if n_tanh >= 2:
                            tile_read(act, before)
                        nc.scalar.activation(chunks(kD(1 - n_tanh % 2) if part != "dz" else kD(1)),
                                             tile_psum(n), ACT.Tanh, scale=0.5).then_inc(tanh_ready, 1)
                        n_tanh += 1
                    elif part in COPIED:
                        dst = {"av": qD(t), "bc": kC, "cq": qC(t), "ck": kC, "cv": kD(0), "dv": qD(t),
                               "dk": kD(t), "dq": qD(t)}[part]
                        act.wait_ge(tile_done, n + 1)
                        if (part, t) == ("bc", 1) or part == "ck":
                            act.wait_ge(bc_used, 1 + (part == "ck"))
                        if part == "cv":
                            tile_read(act, NO["cz", 1])
                        if part == "cq" and t == 0:
                            act.wait_ge(bc_used, 2)
                        if part == "dk":
                            tile_read(act, NO["dz", 1])
                            act.wait_ge(c_out, 32)
                            act.wait_ge(cv_turned, 3)
                        if part == "dq":
                            act.wait_ge(dv_turned, 6)
                            act.wait_ge(v_out, 32)
                        scale = -SCALE if part[1] == "q" else 1.0
                        nc.scalar.mul(chunks(dst), tile_psum(n), scale).then_inc(set_free[n % 2], 1)
                        if part in ("ck", "cv", "dv", "dk"):
                            tile_read(act, n)
                            out = {"ck": sckT[layer], "cv": scvT[layer], "dv": sdvT[layer, t],
                                   "dk": sdkT[layer, t]}[part]
                            done = {"dv": v_out, "dk": k_out}.get(part, c_out)
                            act.dma_start(out, dst[:, CTX]).then_inc(done, 16)
                    if (part, t) == ("au", 0):
                        copy_turned("av", two_tiles(vD), 6)
                    if (part, t) == ("dz", 1):
                        copy_turned("cv", lambda q: vC[:, 3 * q:3 * q + 3, :], 3)
                    if (part, t) == ("dk", 1):
                        copy_turned("dv", two_tiles(vD), 6)

                high_half(N_IN + 1)

                def exp_unit(u):
                    width = unit_width(u)
                    act.wait_ge(biased, u + 1)
                    if UNITS[u][0] == "C":
                        act.wait_ge(sink_put, u + 1)
                        width += 1
                    row = prob[:, u % 3, 0:width]
                    nc.scalar.activation(row, row, ACT.Exp, scale=-1.0, bias=stat[:, u % 4, 0:1],
                                         accum_out=stat[:, u % 4, 1:2]).then_inc(expd, 1)

                def copy_probs(u):
                    n = (len(key_tiles(u)) + 1) // 2
                    act.wait_ge(turned, u + 1)
                    if u >= 2:
                        act.wait_ge(values_ready, u - 1)
                    nc.scalar.copy(probT[:, u % 2, 0:n * P], psum[:, 4, 0:n * P]).then_inc(turned_act, 1)

                for s in range(NU + 2):
                    if s < NU:
                        exp_unit(s)
                    if s >= 2:
                        copy_probs(s - 2)
                act.wait_ge(gated, NU)
                for k in range(KT):
                    nc.scalar.copy(h_hi[:, k], xy[:, k]).then_inc(y_hi_ready, 1)
                for f in range(KT):
                    if f + 2 < KT:
                        high_half(N_IN + f + 2)
                    tile_read(act, N_IN + f)
                    dst = squares if f == 0 else square
                    if f >= 2:
                        act.wait_ge(sq_added, f - 1)
                    nc.scalar.activation(dst, xy[:, f], ACT.Square).then_inc(x_sq, 1)

            @block.tensor
            def _(pe):
                norm_pe(pe)

                def project_pair(pair, first=False):
                    for p in range(2):
                        pe.wait_ge(lo_ready, 2 * pair + p + 1)
                        if not first:
                            pe.wait_ge(set_free[p], pair)
                        for k in range(KT):
                            for w, h in ((w_hi, h_hi), (w_hi, h_lo), (w_lo, h_hi)):
                                for c in range(NCH):
                                    last = nc.tensor.matmul(psum[:, 3 * p + c, 0:CH], w[:, p, k, :],
                                                            h[:, k, c * CH:(c + 1) * CH],
                                                            start=(k == 0 and w is w_hi and h is h_hi),
                                                            stop=(k == KT - 1 and w is w_lo))
                        last.then_inc(tile_done, 1)

                def project(lo, hi):
                    with pe.Fori(lo // 2, hi // 2) as pair:
                        project_pair(pair)

                def turn(src_of, count, tile, sem_out, sem_read):
                    tile_read(pe, tile - 1)
                    tile_read(pe, tile)
                    for q in range(count):
                        if q >= 2:
                            pe.wait_ge(sem_read, q - 1)
                        for i in range(3):
                            t = 3 * (q % 3) + i
                            last = nc.tensor.transpose(psum[:, BANK_A + q % 2, i * P:(i + 1) * P],
                                                       src_of(q // 3)[:, t * P:(t + 1) * P], ident[:, :])
                        last.then_inc(sem_out, 1)

                pe.wait_ge(h_ready, KT)
                project_pair(0, first=True)
                project(2, 4)
                turn(qD, 6, NO["av", 1], av_turned, av_natural)
                project(4, 8)
                pe.wait_ge(av_normal, 1)
                pe.wait_ge(mix_in, 32)
                for q in range(6):
                    j = q // 3
                    if q >= 2:
                        pe.wait_ge(mix_read, q - 1)
                    for i in range(3):
                        t = 3 * (q % 3) + i
                        for r in range(2):
                            last = nc.tensor.matmul(psum[64 * r:64 * r + 64, BANK_A + q % 2, i * P:(i + 1) * P],
                                                    vD[:, t, (2 * j + r) * 64:(2 * j + r + 1) * 64],
                                                    wsT[:, 2 * j + r, :], start=True, stop=True,
                                                    skip_group_check=True)
                    last.then_inc(mixed, 1)
                project(8, 22)
                pe.wait_ge(mix_read, 6)
                turn(lambda j: kD(0), 3, NO["cv", 0], cv_turned, cv_natural)
                project(22, 26)
                pe.wait_ge(cv_natural, 3)
                turn(qD, 6, NO["dv", 1], dv_turned, dv_natural)
                project(26, 28)

                pe.wait_ge(set_free0, N_IN // 2)
                pe.wait_ge(set_free1, N_IN // 2)
                pe.wait_ge(dv_natural, 6)
                pe.wait_ge(rope_ready, 3)
                pe.wait_ge(layer_in, 16 * 6)

                def scores(u):
                    mixer, i, t, r = UNITS[u]
                    if u >= 2:
                        pe.wait_ge(biased, u - 1)
                    q = (qC if mixer == "C" else qD)(t)[64 * r:64 * r + 64, i * P:(i + 1) * P]
                    bank = 2 * (u % 2)
                    for src, at, width in score_pieces(u):
                        b, off = divmod(at, 512)
                        last = nc.tensor.matmul(psum[:, bank + b, off:off + width], q, src, start=True, stop=True,
                                                skip_group_check=True)
                    last.then_inc(scores_ready, 1)

                def turn_probs(u):
                    tiles = key_tiles(u)
                    half = (len(tiles) + 1) // 2
                    pe.wait_ge(normed, u + 1)
                    if u >= 1:
                        pe.wait_ge(turned_act, u)
                        pe.wait_ge(turned_dve, u)
                    for b, (at, width, _) in enumerate(tiles):
                        bank, slot = (4, b) if b < half else (5, b - half)
                        last = nc.tensor.transpose(psum[0:width, bank, slot * P:(slot + 1) * P],
                                                   prob[:, u % 3, at:at + width], ident[:, :])
                    last.then_inc(turned, 1)

                def values(u):
                    mixer, i, t, r = UNITS[u]
                    pe.wait_ge(turned_act, u + 1)
                    pe.wait_ge(turned_dve, u + 1)
                    if u >= 2:
                        pe.wait_ge(gated, u - 1)
                    tiles = key_tiles(u)
                    for b, (_, width, v) in enumerate(tiles):
                        last = nc.tensor.matmul(psum[64 * r:64 * r + 64, BANK_A + u % 2, 0:P], v,
                                                probT[0:width, u % 2, b * P:(b + 1) * P],
                                                start=(b == 0), stop=(b == len(tiles) - 1))
                    last.then_inc(values_ready, 1)

                for s in range(NU + 3):
                    if s < NU:
                        scores(s)
                    if 2 <= s < NU + 2:
                        turn_probs(s - 2)
                    if s >= 3:
                        values(s - 3)
                pe.wait_ge(y_split, KT)
                project(28, 36)

            @block.vector
            def _(dve):
                told, pending = {}, {}

                def tell(ins, signal=dve_step, count=None):
                    ins.then_inc(signal, 1)
                    told[signal.name] = count or told.get(signal.name, 0) + 1
                    pending[signal.name] = (signal, told[signal.name])

                def settle():
                    for signal, count in pending.values():
                        dve.wait_ge(signal, count)
                    pending.clear()

                norm_dve(dve, tell, settle)
                dve.wait_ge(rstd_ready, TT)
                dve.wait_ge(mod_ready, 1)

                def low(k):
                    dve.wait_ge(h_hi_ready, k + 1)
                    for cols, c in PARTS:
                        last = nc.vector.scalar_tensor_tensor(h_lo[:, k, cols], slots[:, k, cols],
                                                              mod[:, k, c:c + 1], h_hi[:, k, cols],
                                                              ALU.add, ALU.subtract)
                    last.then_inc(h_ready, 1)

                for k in range(KT):
                    out, x = chunks(slots[:, k]), chunks(xy[:, k])
                    for ch, cols, c in pieces():
                        last = nc.vector.scalar_tensor_tensor(
                            out[:, ch, cols], x[:, ch, cols], mod[:, KT + k, c:c + 1],
                            psum[:, RSTD_BANK:RSTD_BANK + 3, 0:CH][:, ch, cols], ALU.mult, ALU.mult)
                        tell(last, scaled if c == 1 else dve_step)
                    if k >= 1:
                        low(k - 1)
                settle()
                low(KT - 1)

                def y_of(part, t):
                    return xy[:, 2 * "abcd".index(part[0]) + t]

                n_tanh = 0
                n_rope = 0
                for n, (part, t) in enumerate(TILES):
                    y = y_of(part, t)
                    free = set_free[n % 2]
                    if part[1] == "z":
                        dve.wait_ge(tanh_ready, n_tanh + 1)
                        th = kD(1 - n_tanh % 2) if part != "dz" else kD(1)
                        tell(nc.vector.scalar_tensor_tensor(chunks(y), chunks(th), 1.0, tile_psum(n),
                                                                 ALU.add, ALU.mult), free, n // 2 + 1)
                        n_tanh += 1
                    elif part in ("au", "bb"):
                        dve.wait_ge(tile_done, n + 1)
                        settle()
                        tell(nc.vector.scalar_tensor_tensor(chunks(y), tile_psum(n), 0.5, chunks(y),
                                                                 ALU.mult, ALU.mult), free, n // 2 + 1)
                    elif part == "bh":
                        dve.wait_ge(tile_done, n + 1)
                        tile_read(dve, NO["bc", t])
                        tell(nc.vector.tensor_tensor(chunks(kC), tile_psum(n), chunks(kC), ALU.mult), free, n // 2 + 1)
                        settle()
                        if t == 0:
                            dve.wait_ge(layer_in, 16 * 6)
                        s = qC(t)
                        tell(nc.vector.tensor_scalar(s, kC, conv_w[:, t, 1:2], None, ALU.mult))
                        settle()
                        for a, b in ((0, DEC_SEQ), (DEC_SEQ, T)):
                            tell(nc.vector.scalar_tensor_tensor(s[:, a + 1:b], kC[:, a:b - 1], conv_w[:, t, 0:1],
                                                               s[:, a + 1:b], ALU.mult, ALU.add))
                        settle()
                        for a, b in ((0, DEC_SEQ), (DEC_SEQ, T)):
                            tell(nc.vector.scalar_tensor_tensor(s[:, a:b - 1], kC[:, a + 1:b], conv_w[:, t, 2:3],
                                                               s[:, a:b - 1], ALU.mult, ALU.add))
                        settle()
                        tell(nc.vector.tensor_tensor(y, y, s, ALU.mult), bc_used)
                    elif part in ("cq", "ck"):
                        tile_read(dve, n)
                        raw = slots[:, n_rope, LAT]
                        if n_rope == 0:
                            dve.wait_ge(rope_in, 16)
                        else:
                            settle()
                        tell(nc.vector.stream_shuffle(swapped, raw, [(i + 16) % 32 for i in range(32)]), swap_ready)
                        settle()
                        tell(nc.vector.tensor_tensor(swapped, swapped, sin_t, ALU.mult))
                        settle()
                        dve.wait_ge(cos_ready, n_rope + 1)
                        tell(nc.vector.tensor_tensor(raw, raw, swapped, ALU.add), rope_ready)
                        n_rope += 1
                    if (part, t) == ("az", 1):
                        vh = vD[:, :, :].rearrange("p t (h d) -> p t h d", h=4)
                        ss, rs = small[:, 4, :], small[:, 5, :]
                        dve.wait_ge(av_natural, 6)
                        for j in range(2):
                            sq = squares.rearrange("p (t d) -> p t d", t=TT)
                            vj = vD[:, :, j * P:(j + 1) * P]
                            tell(nc.vector.tensor_tensor(sq, vj, vj, ALU.mult))
                            settle()
                            tell(nc.vector.tensor_reduce(
                                ss.rearrange("p (t h) -> p t h", t=TT)[:, :, 2 * j:2 * j + 2],
                                squares.rearrange("p (t h d) -> p t h d", t=TT, h=2), AX_X, ALU.add))
                            settle()
                        tell(nc.vector.tensor_scalar(ss, ss, 1.0 / HEAD_DIM, EPS, ALU.mult, ALU.add))
                        settle()
                        rsqrt(tell, settle, rs, ss, small[:, 6, :], small[:, 7, :])
                        flat = vD[:, :, :].rearrange("p t (h d) -> p (t h) d", h=4)
                        tell(nc.vector.tensor_tensor(
                            flat, flat, rs.rearrange("p (n o) -> p n o", o=1).broadcast_to([P, 36, HEAD_DIM]),
                            ALU.mult), av_normal)
                    if (part, t) == ("bb", 0):
                        dve.wait_ge(mix_in, 32)
                        for q in range(6):
                            j, c = q // 3, q % 3
                            dve.wait_ge(mixed, q + 1)
                            tmp = flat_prob[:, (q % 2) * CH:(q % 2 + 1) * CH].rearrange("p (t n) -> p t n", t=3)
                            tell(nc.vector.tensor_tensor(
                                tmp, psum[:, BANK_A + q % 2, 0:CH].rearrange("p (t n) -> p t n", t=3),
                                bs[:, j:j + 1, :].broadcast_to([P, 3, P]), ALU.add), mix_read)
                            settle()
                            yq = xy[:, j, c * CH:(c + 1) * CH].rearrange("p (t n) -> p t n", t=3)
                            tell(nc.vector.tensor_tensor(yq, yq, tmp, ALU.mult))

                settle()
                tell(nc.vector.tensor_scalar(sinks[:, :], sinks[:, :], -1.0, None, ALU.mult))
                settle()

                def bias_unit(u):
                    mixer, i, t, r = UNITS[u]
                    width = unit_width(u)
                    bank = 2 * (u % 2)
                    sc = psum[:, bank:bank + 2, :].rearrange("p b n -> p (b n)")
                    low_ = stat[:, u % 4, 0:1]
                    dve.wait_ge(scores_ready, u + 1)
                    if u >= 3:
                        dve.wait_ge(turned, u - 2)
                    if u == 0:
                        dve.wait_ge(band_in, 16)
                    if mixer == "C":
                        at = 2 * P if i == LT else base(u)
                        ops = [(0, width, band[:, at:at + width])]
                        first = sinks[:, 2 * t + r:2 * t + r + 1]
                    else:
                        head = 2 * t + r
                        tab = table[:, head % 2]
                        first = -NEG
                        if i == 0:
                            dve.wait_ge(bias_ready, head + 1)
                        if i == LT:
                            ops = [(0, P, tab[:, ZERO0:INNER0])]
                        elif d_window(i)[1] == 9:
                            ops = [(0, width, tab[:, ZERO0:TABLE])]
                        else:
                            off = (d_window(i)[0] - 2 * i - REL0) * GRID_W
                            ops = [(0, P, tab[:, ZERO0:INNER0]), (P, width, tab[:, off:off + width - P])]
                    if mixer == "C":
                        tell(nc.vector.tensor_copy(prob[:, u % 3, width:width + 1],
                                                        sinks[:, 2 * t + r:2 * t + r + 1]), sink_put)
                    for n_, (a, b, tab_) in enumerate(ops):
                        ins = nc.vector.tensor_tensor_reduce(out=prob[:, u % 3, a:b], in0=sc[:, a:b], in1=tab_,
                                                             scale=1.0, scalar=first, op0=ALU.add, op1=ALU.min,
                                                             accum_out=low_)
                        if n_ < len(ops) - 1:
                            tell(ins)
                            settle()
                            first = low_
                        else:
                            ins.then_inc(biased, 1)

                def norm_unit(u):
                    width = unit_width(u)
                    dve.wait_ge(expd, u + 1)
                    tell(nc.vector.reciprocal(stat[:, u % 4, 2:3], stat[:, u % 4, 1:2]))
                    settle()
                    row = prob[:, u % 3, 0:width]
                    nc.vector.tensor_scalar(row, row, stat[:, u % 4, 2:3], None, ALU.mult).then_inc(normed, 1)

                def copy_probs(u):
                    tiles = key_tiles(u)
                    half = (len(tiles) + 1) // 2
                    n = len(tiles) - half
                    dve.wait_ge(turned, u + 1)
                    if u >= 2:
                        dve.wait_ge(values_ready, u - 1)
                    ins = None
                    full = [w for _, w, _ in tiles[half:]]
                    n_full = sum(w == P for w in full)
                    if n_full:
                        ins = nc.vector.tensor_copy(probT[:, u % 2, half * P:(half + n_full) * P],
                                                    psum[:, 5, 0:n_full * P])
                    if n_full < n:
                        b = half + n_full
                        ins = nc.vector.tensor_copy(probT[0:GRID_W, u % 2, b * P:(b + 1) * P],
                                                    psum[0:GRID_W, 5, n_full * P:(n_full + 1) * P])
                    if ins is None:
                        dve.sem_inc(turned_dve, 1)
                    else:
                        ins.then_inc(turned_dve, 1)

                def gate_unit(u):
                    mixer, i, t, r = UNITS[u]
                    dve.wait_ge(values_ready, u + 1)
                    y = xy[64 * r:64 * r + 64, (4 if mixer == "C" else 6) + t, i * P:(i + 1) * P]
                    nc.vector.scalar_tensor_tensor(y, psum[64 * r:64 * r + 64, BANK_A + u % 2, 0:P], 0.5, y,
                                                   ALU.mult, ALU.mult).then_inc(gated, 1)

                for s in range(NU + 3):
                    if s < NU:
                        bias_unit(s)
                    if 1 <= s < NU + 1:
                        norm_unit(s - 1)
                    if 2 <= s < NU + 2:
                        copy_probs(s - 2)
                    if s >= 3:
                        gate_unit(s - 3)
                dve.wait_ge(gated, NU)
                for k in range(KT):
                    dve.wait_ge(y_hi_ready, k + 1)
                    nc.vector.tensor_tensor(h_lo[:, k], xy[:, k], h_hi[:, k], ALU.subtract).then_inc(y_split, 1)
                dve.wait_ge(y_split, KT)
                for f in range(KT):
                    n = N_IN + f
                    dve.wait_ge(tile_done, n + 1)
                    dve.wait_ge(x_loaded[f % 2], 16 * (f // 2 + 1))
                    new, old = chunks(xy[:, f]), chunks(x_new[:, f % 2])
                    for ch, cols, c in pieces():
                        last = nc.vector.scalar_tensor_tensor(new[:, ch, cols], tile_psum(n)[:, ch, cols],
                                                              mod[:, 2 * KT + f, c:c + 1], old[:, ch, cols],
                                                              ALU.mult, ALU.add)
                        if c == 1:
                            last.then_inc(set_free[n % 2], 1)
                    if f >= 2:
                        dve.wait_ge(x_sq, f)
                        if f >= 3:
                            dve.wait_ge(sq_added, f - 2)
                        nc.vector.tensor_tensor(squares, squares, square, ALU.add).then_inc(sq_added, 1)
                dve.wait_ge(x_sq, KT)
                dve.wait_ge(sq_added, KT - 2)
                nc.vector.tensor_tensor(squares, squares, square, ALU.add).then_inc(sq_added, 1)

          nc.all_engine_barrier(sems_to_clear=layer_sems)

        y_scaled = sem("y_scaled")
        y_out = sem("y_out")
        with nc.Block() as block:
            @block.sync
            def _(sp):
                for k in range(KT):
                    sp.wait_ge(y_scaled, k + 1)
                    sp.dma_start(yT[k], slots[:, k]).then_inc(y_out, 16)
                sp.wait_ge(y_out, 16 * KT)

            @block.tensor
            def _(pe):
                norm_pe(pe)

            @block.vector
            def _(dve):
                step = [0]

                def own(ins):
                    ins.then_inc(dve_step, 1)
                    step[0] += 1

                def settle():
                    dve.wait_ge(dve_step, step[0])

                norm_dve(dve, own, settle)
                dve.wait_ge(rstd_ready, TT)
                for k in range(KT):
                    nc.vector.scalar_tensor_tensor(chunks(slots[:, k]), chunks(xy[:, k]), fin_g[:, k:k + 1],
                                                   psum[:, RSTD_BANK:RSTD_BANK + 3, 0:CH], ALU.mult, ALU.mult
                                                   ).then_inc(y_scaled, 1)


def constants():
    f = np.float32
    ident = np.eye(P, dtype=f)
    half = HEAD_DIM // 4
    freqs = f(ROPE_BASE) ** (-np.arange(half, dtype=f) / f(half))
    t = np.arange(DEC_SEQ)
    d = np.arange(P) % HEAD_DIM
    pos = np.where(d[:, None] < HEAD_DIM // 2, (t // GRID_W)[None, :], (t % GRID_W)[None, :]).astype(f)
    ang = (pos * freqs[d % half][:, None]).astype(f)
    sign = np.where(d % (2 * half) < half, f(-1), f(1))[:, None]
    rope = np.concatenate([np.cos(ang), sign * np.sin(ang)], axis=1).astype(f)
    q, k = np.arange(P)[:, None], np.arange(P)[None, :]
    zero = np.zeros((P, P), f)
    band = np.concatenate([np.where(k >= q, f(0), f(-NEG)), zero, zero, np.where(k <= q, f(0), f(-NEG))],
                          axis=1).astype(f)
    col = np.arange(P)[:, None] % GRID_W
    start = np.clip(col - WIN_C // 2, 0, GRID_W - WIN_C)
    key = np.arange(GRID_W)[None, :]
    inside = (key >= start) & (key < start + WIN_C)
    window = np.stack([np.where(inside, f(-1), f(0)), np.where(inside, f(0), f(-NEG))], axis=1).astype(f)
    return ident, rope, band, window


def rpb_rows(rpb):
    padded = np.pad(rpb, ((0, 0), (0, 0), (0, 0), (GRID_W - WIN_C, GRID_W - WIN_C)))
    entry = GRID_W - 1 - np.arange(GRID_W)[:, None] + np.arange(GRID_W)[None, :]
    by_column = padded[:, :, :, entry]
    halves = [by_column[:, :, 1 - a:15 - a] for a in range(2)]
    return np.stack(halves, axis=2).transpose(0, 1, 2, 4, 3, 5).reshape(DEPTH, 4, P, BIAS_N)


def kernel(x_prompt, x_sample, cache_c_k, cache_c_v, cache_d_k, cache_d_v, c, c_ctx, norm_g, w_mod, b_mod,
           w_in, w_out, w_s, b_s, w_conv, sink, rpb, final_g):
    import concourse.bacc as bacc
    from concourse.bass_utils import run_bass_kernel_spmd

    a = dict(x_prompt=x_prompt, x_sample=x_sample, cache_c_k=cache_c_k, cache_c_v=cache_c_v, cache_d_k=cache_d_k,
             cache_d_v=cache_d_v, c=c, c_ctx=c_ctx, norm_g=norm_g, w_mod=w_mod, b_mod=b_mod, w_in=w_in,
             w_out=w_out, w_s=w_s, b_s=b_s, w_conv=w_conv, sink=sink, rpb=rpb, final_g=final_g)
    a = {k: np.asarray(v) for k, v in a.items()}
    cat, con = np.concatenate, np.ascontiguousarray

    def heads_c(m, axis):
        parts = np.split(m, 4, axis=axis)
        return cat([parts[h] for h in C_HEADS], axis=axis)

    def columns(part, t):
        m = a["w_in"][:, :, COLUMNS[part]:COLUMNS[part] + (P if part in ("ck", "cv") else 2 * P)]
        if part in ("cq", "cz"):
            m = heads_c(m, 2)
        return m[:, :, t * P:(t + 1) * P]

    w_out_p = cat([a["w_out"][:, :512], heads_c(a["w_out"][:, 512:768], 1), a["w_out"][:, 768:]], axis=1)
    tiles = [columns(*x) for x in TILES] + [w_out_p[:, :, f * P:(f + 1) * P] for f in range(KT)]
    ident, rope, band, window = constants()
    by_p = lambda m: con(np.moveaxis(m.reshape(*m.shape[:-1], -1, P), -1, 1))
    data = {
        "xT": cat([a["x_sample"][0], a["x_prompt"][0]]).T.reshape(KT, P, T),
        "cond": np.stack([a["c"][0], a["c_ctx"]], axis=1).reshape(KT, P, 2).transpose(1, 0, 2),
        "w_mod": a["w_mod"],
        "b_mod": a["b_mod"].reshape(DEPTH, 24, P).transpose(2, 0, 1),
        "norm_g": a["norm_g"].reshape(DEPTH, KT, P).transpose(2, 0, 1),
        "final_g": a["final_g"].reshape(KT, P).T,
        "w_tiles": np.stack([m.reshape(DEPTH, KT, P, P).transpose(0, 2, 1, 3) for m in tiles], axis=1),
        "w_sT": a["w_s"].transpose(0, 3, 1, 2),
        "b_s": np.repeat(a["b_s"].reshape(DEPTH, 2, 2, 1, P), HEAD_DIM, axis=3
                         ).reshape(DEPTH, 2, P, P).transpose(0, 2, 1, 3),
        "w_conv": a["w_conv"].reshape(DEPTH, 3, 2, P).transpose(0, 3, 2, 1),
        "sink": np.repeat(a["sink"][:, None, list(C_HEADS)], P, axis=1),
        "rpb": rpb_rows(a["rpb"]),
        "cckT": a["cache_c_k"][0].reshape(DEPTH, P, P).transpose(0, 2, 1),
        "ccv": a["cache_c_v"][0].reshape(DEPTH, P, P),
        "cdkT": a["cache_d_k"][0].reshape(DEPTH, P, 2, P).transpose(0, 3, 2, 1),
        "cdv": a["cache_d_v"][0].reshape(DEPTH, P, 2, P),
        "ident_c": ident, "rope_c": rope, "band_c": band, "window_c": window,
    }
    outs = {"yT": (KT, P, T), "sckT": (DEPTH, P, P), "scvT": (DEPTH, P, P), "sdkT": (DEPTH, 2, P, P),
            "sdvT": (DEPTH, 2, P, P)}
    nc = bacc.Bacc("TRN2", target_bir_lowering=False, num_devices=1)
    data = {k: con(v) for k, v in data.items()}
    args = {k: nc.dram_tensor("in_" + k, v.shape, F32, kind="ExternalInput").ap() for k, v in data.items()}
    args |= {k: nc.dram_tensor("out_" + k, s, F32, kind="ExternalOutput").ap() for k, s in outs.items()}
    build(nc, **args)
    r = run_bass_kernel_spmd(nc, [{"in_" + k: v for k, v in data.items()}], core_ids=[0]).results[0]

    y = r["out_yT"].reshape(D_MODEL, T).T
    natural = lambda m: m.reshape(DEPTH, -1, SEQ).transpose(0, 2, 1).reshape(1, DEPTH, SEQ, -1, HEAD_DIM)
    return (con(y[DEC_SEQ:])[None], con(y[:DEC_SEQ])[None], con(natural(r["out_sckT"])),
            con(natural(r["out_scvT"])), con(natural(r["out_sdkT"])), con(natural(r["out_sdvT"])))
```

```python
from contextlib import ExitStack

import numpy as np

import concourse.bass as bass
from concourse import mybir

F32 = mybir.dt.float32
F32R = mybir.dt.float32r
I32 = mybir.dt.int32
ALU = mybir.AluOpType
ACT = mybir.ActivationFunctionType
AX_X = mybir.AxisListType.X

P = 128
D_MODEL = 1024
DEPTH = 2
SEQ = 128
DEC_SEQ = 1024
T = DEC_SEQ + SEQ
KT = D_MODEL // P
CH = 384
NCH = T // CH
TT = T // P
LT = DEC_SEQ // P
GRID_W = 64
ROWS = DEC_SEQ // GRID_W
WIN_R = 8
WIN_C = 16
HEAD_DIM = 64
EPS = 1e-6
NEG = -1e30
SCALE = HEAD_DIM ** -0.5
ROPE_BASE = 10000.0

TILES = [("av", 0), ("av", 1), ("az", 0), ("au", 0), ("az", 1), ("au", 1),
         ("bz", 0), ("bb", 0), ("bc", 0), ("bh", 0), ("bz", 1), ("bb", 1), ("bc", 1), ("bh", 1),
         ("cz", 0), ("cz", 1), ("cq", 0), ("cq", 1), ("ck", 0), ("cv", 0),
         ("dz", 0), ("dz", 1), ("dv", 0), ("dv", 1), ("dk", 0), ("dk", 1), ("dq", 0), ("dq", 1)]
N_IN = len(TILES)
NO = {x: n for n, x in enumerate(TILES)}
N_TILES = N_IN + KT
COLUMNS = {"au": 0, "av": 256, "az": 512, "bb": 768, "bc": 1024, "bh": 1280, "bz": 1536, "cq": 1792,
           "ck": 2048, "cv": 2176, "cz": 2304, "dq": 2560, "dk": 2816, "dv": 3072, "dz": 3328}
C_HEADS = (0, 2, 1, 3)
COPIED = ("av", "bc", "cq", "ck", "cv", "dv", "dk", "dq")

RSQRT_MAGIC = 0x5F3759DF

QR, QC = 8, 16
KR, KC = QR + WIN_R // 2, 2 * WIN_C
BLK_R = P // KC
N_CG = GRID_W // QC
N_BLK = ROWS // BLK_R
BIAS_CLASS = (0, 1, 1, 2)
N_CLASS = 3
TABLES = 6
S_W = P + KR * KC
assert S_W == 512


def d_keys(i):
    rg, cg = divmod(i, N_CG)
    return (0, ROWS - KR)[rg], min(max(cg * QC - WIN_C // 2, 0), GRID_W - KC)


GROUPS = (("D", 0), ("C", 0), ("C", 1), ("D", 1))
UNITS = [(mixer, i, t, r) for mixer, t in GROUPS for i in range(LT + 1) for r in range(2)]
NU = len(UNITS)
GROUP_U = 2 * (LT + 1)
GROUP_P = LT + 1


def bias_table(u):
    _, i, t, r = UNITS[u]
    rg, cg = divmod(i, N_CG)
    return (((t * 2 + rg) * N_CLASS + BIAS_CLASS[cg]) * 2) + r


N_TABLES = 4 * 2 * N_CLASS
READERS = [[u for u in range(NU) if UNITS[u][0] == "D" and UNITS[u][1] < LT and bias_table(u) == m]
           for m in range(N_TABLES)]


def build(nc, xT, cond, w_mod, b_mod, norm_g, final_g, w_tiles, w_sT, b_s, w_conv, sink, rpb,
          cckT, ccv, cdkT, cdv, ident_c, rope_c, band_c, row_c, col_c, yT, sckT, scvT, sdkT, sdvT):
    with ExitStack() as ctx:
        def sb(name, shape, dt=F32):
            return ctx.enter_context(nc.sbuf_tensor(name, shape, dt))

        def sem(name):
            return ctx.enter_context(nc.semaphore(name))

        x_kept = nc.dram_tensor("x_kept", [P, KT, T], F32, kind="Internal").ap()

        h_hi = sb("h_hi", [P, KT, T], F32R)
        h_lo = sb("h_lo", [P, KT, T], F32R)
        xy = sb("xy", [P, KT, T])
        slots = sb("slots", [P, 11, T])
        w_raw = sb("w_raw", [P, 2, KT, P])
        w_hi = sb("w_hi", [P, 2, KT, P], F32R)
        w_lo = sb("w_lo", [P, 2, KT, P], F32R)
        prob = sb("prob", [P, 3, S_W + 2])
        probT = sb("probT", [P, 2, S_W])
        table = sb("table", [P, TABLES, S_W])
        ident = sb("ident", [P, P])
        row_mask = sb("row_mask", [P, 2, KR])
        col_mask = sb("col_mask", [P, N_CLASS, KC])
        ck_c = sb("ck_c", [P, P])
        cv_c = sb("cv_c", [P, P])
        ck_d = sb("ck_d", [P, 2, P])
        mods = sb("mods", [P, DEPTH, 24, 2])
        mod = sb("mod", [P, 24, 2])
        layer_g = sb("layer_g", [P, DEPTH, KT])
        ones_m = sb("ones_m", [P, 32])
        silu = sb("silu", [P, KT, 2])
        fin_g = sb("fin_g", [P, KT])
        conv_w = sb("conv_w", [P, 2, 3])
        sinks = sb("sinks", [P, 4])
        stat = sb("stat", [P, 4, 4])
        psum = ctx.enter_context(nc.psum_tensor("psum", [P, 8, 512], F32))

        qC, kC, qD, kD = (lambda t: slots[:, t]), slots[:, 2], (lambda t: slots[:, 3 + t]), (lambda t: slots[:, 5 + t])
        vC = slots[:, 7].rearrange("p (t d) -> p t d", t=TT)
        v_flat = slots[:, 8:10].rearrange("p a n -> p (a n)")
        vA = v_flat.rearrange("p (t d) -> p t d", t=TT)
        vD = v_flat.rearrange("p (b d) -> p b d", d=P)
        V_CTX, V_CACHE = N_CG * N_BLK, N_CG * N_BLK + 1
        dv_kept = (slots[:, 3], slots[:, 10])
        flat_prob = prob[:, :, :].rearrange("p a n -> p (a n)")
        flat_probT = probT[:, :, :].rearrange("p a n -> p (a n)")
        flat_table = table[:, :, :].rearrange("p a n -> p (a n)")
        squares = flat_prob[:, 0:T]
        square = slots[:, 10]
        small = flat_prob[:, T:T + 8 * 36].rearrange("p (a n) -> p a n", a=8)
        wsT = flat_probT[:, 0:4 * P].rearrange("p (h n) -> p h n", h=4)
        bs = flat_probT[:, 4 * P:6 * P].rearrange("p (j n) -> p j n", j=2)
        cos_t = flat_table[:, 0:DEC_SEQ]
        sin_t = flat_table[:, DEC_SEQ:2 * DEC_SEQ]
        swapped = flat_table[:, 2 * DEC_SEQ:3 * DEC_SEQ]
        x_new = flat_table[:, 0:2 * T].rearrange("p (a n) -> p a n", a=2)
        band = w_raw[:, 1].rearrange("p k n -> p (k n)")[:, 0:4 * P]
        BANK_A = 6

        LAT, CTX = slice(0, DEC_SEQ), slice(DEC_SEQ, T)

        def chunks(ap):
            return ap.rearrange("p (c n) -> p c n", c=NCH)

        def tile_read(eng, n):
            eng.wait_ge(set_free[n % 2], n // 2 + 1)

        def tile_psum(n):
            return psum[:, 3 * (n % 2):3 * (n % 2) + 3, 0:CH]

        consts_in = sem("consts_in")
        x_in = sem("x_in")
        wmod_in = [sem(f"wmod_in{i}") for i in range(3)]
        cond_tanh = sem("cond_tanh")
        cond_ready = sem("cond_ready")
        wmod_used = sem("wmod_used")
        modrow_ready = sem("modrow_ready")
        modT_ready = sem("modT_ready")
        x_squared = sem("x_squared")
        squares_added = sem("squares_added")
        pro_step = sem("pro_step")
        gate_start = sem("gate_start")

        stage = slots[:, :, :].rearrange("p a n -> p (a n)")
        MOD_W = 2 * D_MODEL
        wmod_sb = stage[:, 0:3 * MOD_W].rearrange("p (b n) -> p b n", b=3)
        modrow = w_raw[:, 0].rearrange("p k n -> p (k n)")[:, 0:512]
        silu_c = stage[:, 9216:9216 + KT * 32].rearrange("p (k m) -> p k m", k=KT)
        cond_sb = stage[:, 9472:9472 + 2 * KT].rearrange("p (k c) -> p k c", c=2)
        tanh_c = stage[:, 9488:9488 + 2 * KT].rearrange("p (k c) -> p k c", c=2)
        bmod_sb = stage[:, 9504:9504 + 24 * DEPTH].rearrange("p (l n) -> p l n", l=DEPTH)
        CONSTS = 7

        with nc.Block() as block:
            @block.sync
            def _(sp):
                sp.dma_start(cond_sb, cond).then_inc(consts_in, 16)
                sp.dma_start(ident[:, :], ident_c).then_inc(consts_in, 16)
                sp.dma_start(bmod_sb, b_mod).then_inc(consts_in, 16)
                sp.dma_start(layer_g[:, :, :], norm_g).then_inc(consts_in, 16)
                sp.dma_start(row_mask[:, :, :], row_c).then_inc(consts_in, 16)
                sp.dma_start(col_mask[:, :, :], col_c).then_inc(consts_in, 16)
                sp.dma_start(fin_g[:, :], final_g).then_inc(consts_in, 16)
                for n in range(KT):
                    if n >= 3:
                        sp.wait_ge(wmod_used, n - 2)
                    sp.dma_start(wmod_sb[:, n % 3], w_mod[0, n * P:(n + 1) * P, 0:MOD_W]
                                 ).then_inc(wmod_in[n % 3], 16)
                    if n == 2:
                        for k in range(KT):
                            sp.dma_start(xy[:, k], xT[k]).then_inc(x_in, 16)
                sp.wait_ge(x_in, 16 * KT)

            @block.scalar
            def _(act):
                act.wait_ge(consts_in, 16 * CONSTS)
                nc.scalar.activation(tanh_c, cond_sb, ACT.Tanh, scale=0.5).then_inc(cond_tanh, 1)
                act.wait_ge(x_in, 16 * KT)
                nc.scalar.activation(squares, xy[:, 0], ACT.Square).then_inc(x_squared, 1)
                for k in range(1, KT):
                    if k > 1:
                        act.wait_ge(squares_added, k - 1)
                    nc.scalar.activation(square, xy[:, k], ACT.Square).then_inc(x_squared, 1)

            @block.tensor
            def _(pe):
                pe.wait_ge(cond_ready, 1)
                for k in range(KT):
                    pe.wait_ge(wmod_in[k % 3], 16 * (k // 3 + 1))
                    for c in range(4):
                        q = 32 * c
                        last = nc.tensor.matmul(psum[q:q + 32, 0, :], silu_c[:, k, :],
                                                wmod_sb[:, k % 3, c * 512:(c + 1) * 512],
                                                start=(k == 0), stop=(k == KT - 1), skip_group_check=True)
                    last.then_inc(wmod_used, 1)
                pe.wait_ge(modrow_ready, 1)
                for j in range(4):
                    last = nc.tensor.transpose(psum[:, 4, j * P:(j + 1) * P], modrow[:, j * P:(j + 1) * P],
                                               ident[:, :])
                last.then_inc(modT_ready, 1)

            @block.vector
            def _(dve):
                step = [0]

                def own(ins):
                    ins.then_inc(pro_step, 1)
                    step[0] += 1

                def settle():
                    dve.wait_ge(pro_step, step[0])

                own(nc.vector.memset(silu_c, 0.0))
                nc.vector.memset(ones_m[:, :], 1.0).then_inc(gate_start, 1)
                dve.wait_ge(cond_tanh, 1)
                settle()
                own(nc.vector.scalar_tensor_tensor(tanh_c, tanh_c, 1.0, cond_sb, ALU.add, ALU.mult))
                settle()
                nc.vector.tensor_scalar(silu_c[:, :, 0:2], tanh_c, 0.5, None, ALU.mult).then_inc(cond_ready, 1)
                nc.vector.tensor_scalar(silu[:, :, :], tanh_c, 0.5, None, ALU.mult).then_inc(gate_start, 1)
                for k in range(1, KT):
                    dve.wait_ge(x_squared, k + 1)
                    if k > 1:
                        dve.wait_ge(squares_added, k - 1)
                    nc.vector.tensor_tensor(squares, squares, square, ALU.add).then_inc(squares_added, 1)
                dve.wait_ge(consts_in, 16 * CONSTS)
                for cnd in range(2):
                    own(nc.vector.tensor_copy(mods[:, :, :, cnd], bmod_sb))
                settle()
                dve.wait_ge(wmod_used, KT)
                nc.vector.tensor_copy(modrow, psum[:, 0, :]).then_inc(modrow_ready, 1)
                dve.wait_ge(modT_ready, 1)
                src = psum[:, 4, :].rearrange("p (j q m) -> p q j m", j=4, q=4)
                for cnd in range(2):
                    dst = mods[:, 0, 0:16, cnd].rearrange("p (q j) -> p q j", q=4)
                    own(nc.vector.tensor_tensor(dst, src[:, :, :, cnd], dst, ALU.add))
                settle()
                for cnd in range(2):
                    own(nc.vector.scalar_tensor_tensor(mods[:, 0, 8:16, cnd], mods[:, 0, 8:16, cnd], 1.0,
                                                       layer_g[:, 0], ALU.add, ALU.mult))

        names = ["layer_in", "w_loaded0", "w_loaded1", "hi_ready", "lo_ready", "tile_done", "set_free0", "set_free1",
                 "ones_ready", "sums_ready", "diag_ready", "rstd_ready", "scaled", "h_hi_ready", "shifted",
                 "h_even", "h_odd", "mod_ready", "x_saved", "tanh_ready", "av_turned", "av_natural",
                 "av_normal", "mixed", "mix_read", "ya_ready", "cv_turned", "cv_natural", "dv_turned",
                 "dv_natural", "swap_ready", "cos_ready", "rope_ready", "c_out", "v_out", "k_out",
                 "rope_in", "band_in", "cache0_in", "cache1_in", "bias_ready", "scores_ready", "biased",
                 "expd", "normed", "turned_a", "turned_b", "copied_a", "copied_b", "values_ready", "gated",
                 "y_hi_ready", "y_split", "y_last", "x_loaded0", "x_loaded1", "x_sq", "sq_added",
                 "act_step", "dve_step", "pool_step", "mix_in", "sink_put", "bc_used", "v1_turned",
                 "v1_natural", "chunk0_put", "chunk1_put", "zeros_put", "rstd_copied", "mod_in0", "mod_in1",
                 "mod_used", "mod_sum", "mod_copied", "mod_turned", "mod_read", "part_step", "bias_in0", "bias_in1", "bias_in2", "bias_in3", "bias_in4",
                 "bias_in5"]
        S = {n: sem(n) for n in names}
        nums = [S[n].num for n in names]
        layer_sems = range(min(nums), max(nums) + 1)
        assert len(layer_sems) == len(names)
        (layer_in, w_loaded0, w_loaded1, hi_ready, lo_ready, tile_done, set_free0, set_free1, ones_ready,
         sums_ready, diag_ready, rstd_ready, scaled, h_hi_ready, shifted, h_even, h_odd, mod_ready, x_saved,
         tanh_ready, av_turned, av_natural, av_normal, mixed, mix_read, ya_ready, cv_turned, cv_natural,
         dv_turned, dv_natural, swap_ready, cos_ready, rope_ready, c_out, v_out, k_out, rope_in, band_in,
         cache0_in, cache1_in, bias_ready, scores_ready, biased, expd, normed, turned_a, turned_b, copied_a,
         copied_b, values_ready, gated, y_hi_ready, y_split, y_last, x_loaded0, x_loaded1, x_sq, sq_added,
         act_step, dve_step, pool_step, mix_in, sink_put, bc_used, v1_turned, v1_natural,
         chunk0_put, chunk1_put, zeros_put, rstd_copied, mod_in0, mod_in1, mod_used,
         mod_sum, mod_copied, mod_turned, mod_read, part_step,
         bias_in0, bias_in1, bias_in2, bias_in3, bias_in4, bias_in5) = [S[n] for n in names]
        w_loaded = (w_loaded0, w_loaded1)
        set_free = (set_free0, set_free1)
        bias_in = (bias_in0, bias_in1, bias_in2, bias_in3, bias_in4, bias_in5)
        x_loaded = (x_loaded0, x_loaded1)

        diag = slots[:, 8].rearrange("p (t n) -> p t n", t=TT)
        ones = slots[:, 9, 0:P]
        RSTD_BANK = 3

        rstd_all = slots[:, 10]

        def norm_pe(pe):
            pe.wait_ge(ones_ready, 1)
            for t in range(TT):
                last = nc.tensor.matmul(psum[:, BANK_A, t:t + 1], squares[:, t * P:(t + 1) * P], ones[:, 0:1],
                                        start=True, stop=True)
            last.then_inc(sums_ready, 1)
            for t in range(TT):
                pe.wait_ge(diag_ready, t + 1)
                nc.tensor.matmul(psum[:, RSTD_BANK + t // 3, (t % 3) * P:(t % 3 + 1) * P], ones[:, :], diag[:, t],
                                 start=True, stop=True).then_inc(rstd_ready, 1)

        def rsqrt(own, settle, out, v, s0, s1):
            own(nc.vector.tensor_scalar(s0.bitcast(I32), v.bitcast(I32), 1, None, ALU.arith_shift_right))
            settle()
            own(nc.vector.tensor_scalar(out.bitcast(I32), s0.bitcast(I32), -1, RSQRT_MAGIC, ALU.mult, ALU.add))
            settle()
            for _ in range(3):
                own(nc.vector.tensor_tensor(s0, out, out, ALU.mult))
                settle()
                own(nc.vector.tensor_tensor(s1, s0, v, ALU.mult))
                settle()
                own(nc.vector.tensor_scalar(s0, s1, -0.5, 1.5, ALU.mult, ALU.add))
                settle()
                own(nc.vector.tensor_tensor(out, out, s0, ALU.mult))
                settle()

        def norm_dve(dve, own, settle):
            ms, rstd = small[:, 0, 0:TT], small[:, 1, 0:TT]
            nc.vector.memset(ones, 1.0).then_inc(ones_ready, 1)
            dve.wait_ge(sums_ready, 1)
            own(nc.vector.tensor_scalar(ms, psum[:, BANK_A, 0:TT], 1.0 / D_MODEL, EPS, ALU.mult, ALU.add))
            settle()
            rsqrt(own, settle, rstd, ms, small[:, 2, 0:TT], small[:, 3, 0:TT])
            for t in range(TT):
                nc.vector.tensor_scalar(diag[:, t], ident[:, :], rstd[:, t:t + 1], None, ALU.mult
                                        ).then_inc(diag_ready, 1)

        def pieces():
            return [(slice(0, 2), slice(0, CH), 0), (slice(2, 3), slice(0, DEC_SEQ - 2 * CH), 0),
                    (slice(2, 3), slice(DEC_SEQ - 2 * CH, CH), 1)]

        PARTS = ((LAT, 0), (CTX, 1))

        def c_keys(i):
            return [(i + d, at) for d, at in ((-1, 0), (0, P), (1, 3 * P)) if 0 <= i + d < LT]

        def base(u):
            return P if (UNITS[u][0] == "C" and UNITS[u][1] == 0) else 0

        def grid(ap):
            return ap[:, LAT].rearrange("p (r c) -> p r c", c=GRID_W)

        def queries(u):
            mixer, i, t, r = UNITS[u]
            half = slice(64 * r, 64 * r + 64)
            return (qC if mixer == "C" else qD)(t)[half, i * P:(i + 1) * P]

        def score_pieces(u):
            mixer, i, t, r = UNITS[u]
            half = slice(64 * r, 64 * r + 64)
            k = kC if mixer == "C" else kD(t)
            if i == LT:
                return [(k[half, CTX], 0, P)]
            if mixer == "C":
                off = base(u)
                return ([(k[half, j * P:(j + 1) * P], at - off, P) for j, at in c_keys(i)]
                        + [(ck_c[half, :], 2 * P - off, P)])
            row, col = d_keys(i)
            return [(ck_d[half, t, :], 0, P), (grid(k[half])[:, row:row + KR, col:col + KC], P, KR * KC)]

        def unit_width(u):
            return sum(w for _, _, w in score_pieces(u))

        def unit_values(u):
            mixer, i, t, r = UNITS[u]
            d = slice(64 * r, 64 * r + 64)
            if mixer == "C":
                if i == LT:
                    return [vC[:, LT, d]]
                off = base(u)
                at = {a - off: vC[:, j, d] for j, a in c_keys(i)} | {2 * P - off: cv_c[:, d]}
                return [at[x] for x in sorted(at)]
            if i == LT:
                return [vD[:, V_CTX, d]]
            rg, cg = divmod(i, N_CG)
            first = d_keys(i)[0] // BLK_R
            return [vD[:, V_CACHE, d]] + [vD[:, cg * N_BLK + first + b, d] for b in range(KR // BLK_R)]

        BLOCKS = [len(unit_values(u)) for u in range(NU)]

        def copies_a(u):
            return sum(n > 1 for n in BLOCKS[:u + 1])

        BANK_O, BANK_V = 6, 7
        LAYER_IN = 5

        def put_chunk(q, src, dst):
            col = d_keys(q)[1]
            return nc.gpsimd.tensor_copy(dst.rearrange("p (r c) -> p r c", c=KC), grid(src)[:, :, col:col + KC])

        CHUNK_W = N_BLK * P
        chunk0 = [probT[:, 0, :], probT[:, 1, :], flat_prob[:, 0:CHUNK_W], flat_prob[:, CHUNK_W:2 * CHUNK_W]]
        chunk1 = w_raw[:, 1].rearrange("p k n -> p (k n)")[:, 4 * P:4 * P + CHUNK_W]

        MOD_TILE, MOD_ROWS, THIRDS = 9, 2, 3
        mod_in = (mod_in0, mod_in1)
        mod_rows = (slots[:, 8, 0:D_MODEL], slots[:, 9, 0:D_MODEL])
        mod_part = (slots[:, 7, 0:D_MODEL], slots[:, 10, 0:D_MODEL])
        mod_row = flat_prob[:, 2 * CHUNK_W:3 * CHUNK_W]
        MOD_STEPS = THIRDS * KT // MOD_ROWS
        SUM_TILES, TURN_TILES = (13, 17, 21), (15, 19, 23)

        Y_SPLIT = {6: 0, 11: 1, 16: 2, 21: 3, GROUP_U + 8: 6, 2 * GROUP_U + 8: 4, 3 * GROUP_U + 8: 5}
        V1_STEPS = {GROUP_U + 6 + 2 * q: q for q in range(5)}
        W29_STEP = 3 * GROUP_U + 4
        Y_ORDER = list(Y_SPLIT.values()) + [7]

        with nc.Fori(0, DEPTH) as layer:
          with nc.Block() as block:

            @block.sync
            def _(sp):
                def load_weights(n):
                    sp.dma_start(w_raw[:, n % 2], w_tiles[layer, n]).then_inc(w_loaded[n % 2], 16)

                load_weights(0)
                load_weights(1)
                sp.dma_start(conv_w[:, :, :], w_conv[layer]).then_inc(layer_in, 16)
                sp.dma_start(sinks[:, :], sink[layer]).then_inc(layer_in, 16)
                sp.dma_start(ck_c[:, :], cckT[layer]).then_inc(layer_in, 16)
                sp.dma_start(cv_c[:, :], ccv[layer]).then_inc(layer_in, 16)
                sp.dma_start(ck_d[:, :, :], cdkT[layer]).then_inc(layer_in, 16)
                for k in range(KT):
                    sp.dma_start(x_kept[:, k], xy[:, k]).then_inc(x_saved, 16)
                sp.dma_start(wsT, w_sT[layer]).then_inc(mix_in, 16)
                sp.dma_start(bs, b_s[layer]).then_inc(mix_in, 16)
                sp.dma_start(flat_table[:, 0:2 * DEC_SEQ], rope_c).then_inc(rope_in, 16)

                def weights(lo, hi):
                    with sp.Fori(lo // 2, hi // 2) as pair:
                        for p in range(2):
                            sp.wait_ge(lo_ready, 2 * pair + p - 1)
                            sp.dma_start(w_raw[:, p], w_tiles[layer, 2 * pair + p]).then_inc(w_loaded[p], 16)

                def mod_loads(step):
                    for g in range(MOD_ROWS * step, MOD_ROWS * (step + 1)):
                        j, k = divmod(g, KT)
                        if g >= 2:
                            sp.wait_ge(mod_used, g - 1)
                        rows = (w_mod[layer, k * P:(k + 1) * P, MOD_W:] if j == 0
                                else w_mod[1, k * P:(k + 1) * P, (j - 1) * D_MODEL:j * D_MODEL])
                        sp.dma_start(mod_rows[g % 2], rows).then_inc(mod_in[g % 2], 16)

                weights(2, MOD_TILE + 1)
                sp.wait_ge(mixed, 6)
                sp.dma_start(vD[:, V_CACHE], cdv[layer, :, 0, :]).then_inc(cache0_in, 16)
                for n in range(MOD_TILE + 1, 24):
                    sp.wait_ge(lo_ready, n - 1)
                    load_weights(n)
                    step = n - MOD_TILE - 2
                    if 0 <= step < MOD_STEPS // THIRDS:
                        mod_loads(step)
                    elif MOD_STEPS // THIRDS <= step < MOD_STEPS:
                        with sp.If(layer < DEPTH - 1):
                            mod_loads(step)
                weights(24, 28)

                def load_table(m):
                    if m >= TABLES:
                        sp.wait_ge(biased, READERS[m - TABLES][-1] + 1)
                    sp.dma_start(table[:, m % TABLES, P:S_W], rpb[layer, m]).then_inc(bias_in[m % TABLES], 16)

                sp.wait_ge(rope_ready, 3)
                for m in range(TABLES):
                    load_table(m)
                sp.wait_ge(lo_ready, N_IN - 1)
                load_weights(N_IN)
                sp.wait_ge(lo_ready, N_IN)
                sp.dma_start(band, band_c).then_inc(band_in, 16)
                steps = [(READERS[m - TABLES][-1], "table", m) for m in range(TABLES, N_TABLES)]
                steps += [(GROUP_U + 3, "cache", 1), (3 * GROUP_U, "weights", 1)]
                for _, what, m in sorted(steps):
                    if what == "table":
                        load_table(m)
                    elif what == "cache":
                        sp.wait_ge(values_ready, GROUP_P)
                        sp.dma_start(vD[:, V_CACHE], cdv[layer, :, 1, :]).then_inc(cache1_in, 16)
                    else:
                        sp.wait_ge(biased, 3 * GROUP_U)
                        sp.wait_ge(v1_turned, N_CG)
                        load_weights(N_IN + 1)
                for n in (N_IN + 2, N_IN + 3):
                    sp.wait_ge(lo_ready, n - 1)
                    load_weights(n)
                sp.wait_ge(biased, NU)
                sp.wait_ge(x_saved, 16 * KT)
                for f in range(KT):
                    n = N_IN + f
                    if f >= 4:
                        sp.wait_ge(lo_ready, n - 1)
                        load_weights(n)
                    if f >= 2:
                        tile_read(sp, n - 2)
                    sp.dma_start(x_new[:, f % 2], x_kept[:, f]).then_inc(x_loaded[f % 2], 16)
                for done in (c_out, v_out, k_out):
                    sp.wait_ge(done, 32)

            @block.gpsimd
            def _(pool):
                def low_halves(lo, hi):
                    with pool.Fori(lo // 2, hi // 2) as pair:
                        for p in range(2):
                            pool.wait_ge(hi_ready, 2 * pair + p + 1)
                            nc.gpsimd.tensor_tensor(w_lo[:, p], w_raw[:, p], w_hi[:, p], ALU.subtract
                                                    ).then_inc(lo_ready, 1)

                def low_half(n):
                    pool.wait_ge(hi_ready, n + 1)
                    nc.gpsimd.tensor_tensor(w_lo[:, n % 2], w_raw[:, n % 2], w_hi[:, n % 2], ALU.subtract
                                            ).then_inc(lo_ready, 1)

                low_half(0)
                low_half(1)
                for k in range(1, KT, 2):
                    pool.wait_ge(shifted, k // 2 + 1)
                    pool.wait_ge(h_hi_ready, k + 1)
                    nc.gpsimd.tensor_tensor(h_lo[:, k], slots[:, k], h_hi[:, k], ALU.subtract).then_inc(h_odd, 1)
                low_halves(2, 18)
                for t in range(3):
                    low_half(NO["ck", 0] + t)
                    pool.wait_ge(swap_ready, t + 1)
                    if t == 0:
                        pool.wait_ge(rope_in, 16)
                    raw = slots[:, t, LAT]
                    nc.gpsimd.tensor_tensor(raw, raw, cos_t, ALU.mult).then_inc(cos_ready, 1)
                low_half(21)
                low_halves(22, 26)
                tile_read(pool, NO["dv", 0])
                for q in range(N_CG):
                    put_chunk(q, dv_kept[0], chunk0[q]).then_inc(chunk0_put, 1)
                low_halves(26, 28)
                step = [0]

                def own(ins):
                    ins.then_inc(pool_step, 1)
                    step[0] += 1

                def settle():
                    pool.wait_ge(pool_step, step[0])

                pool.wait_ge(rope_ready, 3)
                nc.gpsimd.memset(table[:, :, 0:P], 0.0).then_inc(zeros_put, 1)

                def make_table(m):
                    tab = table[:, m % TABLES, P:S_W].rearrange("p (r c) -> p r c", c=KC)
                    rg, cls = m // (2 * N_CLASS) % 2, m // 2 % N_CLASS
                    rows = row_mask[:, rg, :].rearrange("p (r o) -> p r o", o=1).broadcast_to([P, KR, KC])
                    cols = col_mask[:, cls:cls + 1, :].broadcast_to([P, KR, KC])
                    pool.wait_ge(bias_in[m % TABLES], 16 * (m // TABLES + 1))
                    own(nc.gpsimd.tensor_tensor(tab, rows, tab, ALU.subtract))
                    settle()
                    nc.gpsimd.tensor_tensor(tab, tab, cols, ALU.add).then_inc(bias_ready, 1)

                def y_low(k):
                    pool.wait_ge(y_hi_ready, Y_ORDER.index(k) + 1)
                    nc.gpsimd.tensor_tensor(h_lo[:, k], xy[:, k], h_hi[:, k], ALU.subtract).then_inc(y_split, 1)

                def chunk_1(q):
                    if q >= 1:
                        pool.wait_ge(v1_turned, q)
                    put_chunk(q, dv_kept[1], chunk1).then_inc(chunk1_put, 1)

                for m in range(TABLES):
                    make_table(m)
                low_half(N_IN)
                steps = [(READERS[m - TABLES][-1], make_table, m) for m in range(TABLES, N_TABLES)]
                steps += [(s - 1, chunk_1, q) for s, q in V1_STEPS.items() if q < N_CG]
                steps += [(s, y_low, k) for s, k in Y_SPLIT.items()] + [(W29_STEP, low_half, N_IN + 1)]
                for _, work, m in sorted(steps, key=lambda x: (x[0], x[2])):
                    work(m)
                low_halves(N_IN + 2, N_TILES)

            @block.scalar
            def _(act):
                def high_half(n):
                    act.wait_ge(w_loaded[n % 2], 16 * (n // 2 + 1))
                    if n >= 2:
                        act.wait_ge(tile_done, n - 1)
                    nc.scalar.copy(w_hi[:, n % 2], w_raw[:, n % 2]).then_inc(hi_ready, 1)

                high_half(0)
                nc.scalar.copy(mod[:, :, :], mods[:, layer]).then_inc(mod_ready, 1)
                high_half(1)
                for c in range(NCH):
                    act.wait_ge(rstd_ready, 3 * (c + 1))
                    nc.scalar.copy(rstd_all[:, c * CH:(c + 1) * CH], psum[:, RSTD_BANK + c, 0:CH]
                                   ).then_inc(rstd_copied, 1)
                act.wait_ge(mod_ready, 1)
                for k in range(KT):
                    act.wait_ge(scaled, k + 1)
                    for cols, c in PARTS:
                        last = nc.scalar.activation(h_hi[:, k, cols], slots[:, k, cols], ACT.Identity,
                                                    bias=mod[:, k, c:c + 1])
                    last.then_inc(h_hi_ready, 1)
                    if k % 2:
                        for cols, c in PARTS:
                            last = nc.scalar.activation(slots[:, k, cols], slots[:, k, cols], ACT.Identity,
                                                        bias=mod[:, k, c:c + 1])
                        last.then_inc(shifted, 1)
                naturals = {"av": (av_turned, av_natural), "cv": (cv_turned, cv_natural)}

                def copy_chunk(q, bank, signal):
                    dst = vD[:, q * N_BLK:(q + 1) * N_BLK, :] if q < N_CG else vD[:, V_CTX:V_CTX + 1, :]
                    src = psum[:, bank, 0:N_BLK * P if q < N_CG else P].rearrange("p (b d) -> p b d", d=P)
                    nc.scalar.copy(dst, src).then_inc(signal, 1)

                def copy_turned(part, dst_of, count):
                    sem_in, sem_out = naturals[part]
                    for q in range(count):
                        act.wait_ge(sem_in, q + 1)
                        nc.scalar.copy(dst_of(q), psum[:, BANK_A + q % 2, 0:CH].rearrange("p (t d) -> p t d", t=3)
                                       ).then_inc(sem_out, 1)

                two_tiles = lambda v: (lambda q: v[:, 3 * (q % 3):3 * (q % 3) + 3, P * (q // 3):P * (q // 3) + P])
                n_tanh = 0
                gates = [n for n, x in enumerate(TILES) if x[0][1] == "z"]
                for n, (part, t) in enumerate(TILES):
                    if n != 1:
                        high_half(n + 1 if n else 2)
                    if part[1] == "z":
                        act.wait_ge(tile_done, n + 1)
                        before = gates[n_tanh - 2] if part != "dz" else NO[("cz", 0) if t == 0 else ("dz", 0)]
                        if n_tanh >= 2:
                            tile_read(act, before)
                        nc.scalar.activation(chunks(kD(1 - n_tanh % 2) if part != "dz" else kD(1)),
                                             tile_psum(n), ACT.Tanh, scale=0.5).then_inc(tanh_ready, 1)
                        n_tanh += 1
                    elif part in COPIED:
                        dst = {"av": qD(t), "bc": kC, "cq": qC(t), "ck": kC, "cv": kD(0), "dv": dv_kept[t],
                               "dk": kD(t), "dq": qD(t)}[part]
                        act.wait_ge(tile_done, n + 1)
                        if (part, t) == ("bc", 1) or part == "ck":
                            act.wait_ge(bc_used, 1 + (part == "ck"))
                        if part == "cv":
                            tile_read(act, NO["cz", 1])
                        if part == "cq" and t == 0:
                            act.wait_ge(bc_used, 2)
                        if part == "dk":
                            tile_read(act, NO["dz", 1])
                            act.wait_ge(c_out, 32)
                            act.wait_ge(cv_turned, 3)
                        if part == "dq":
                            act.wait_ge(dv_turned, N_CG + 1)
                            act.wait_ge(v_out, 32)
                        scale = -SCALE if part[1] == "q" else 1.0
                        if part == "dq":
                            for lo, hi in ((0, 6), (6, 8), (8, 12), (12, 16)):
                                rg, c = lo // QR, lo * GRID_W // CH
                                src = tile_psum(n)[:, c, lo * GRID_W - c * CH:hi * GRID_W - c * CH]
                                to = dst[:, rg * QR * GRID_W:(rg + 1) * QR * GRID_W].rearrange(
                                    "p (g r c) -> p g r c", g=N_CG, r=QR)[:, :, lo - rg * QR:hi - rg * QR, :]
                                nc.scalar.mul(to.rearrange("p g r c -> p r g c"),
                                              src.rearrange("p (r g c) -> p r g c", g=N_CG, c=QC), scale)
                            nc.scalar.mul(dst[:, CTX], tile_psum(n)[:, 2, DEC_SEQ - 2 * CH:CH], scale
                                          ).then_inc(set_free[n % 2], 1)
                            continue
                        nc.scalar.mul(chunks(dst), tile_psum(n), scale).then_inc(set_free[n % 2], 1)
                        if part in ("ck", "cv", "dv", "dk"):
                            tile_read(act, n)
                            out = {"ck": sckT[layer], "cv": scvT[layer], "dv": sdvT[layer, t],
                                   "dk": sdkT[layer, t]}[part]
                            done = {"dv": v_out, "dk": k_out}.get(part, c_out)
                            act.dma_start(out, dst[:, CTX]).then_inc(done, 16)
                    if (part, t) == ("au", 0):
                        copy_turned("av", two_tiles(vA), 6)
                    if (part, t) == ("dz", 1):
                        copy_turned("cv", lambda q: vC[:, 3 * q:3 * q + 3, :], 3)
                    if (part, t) == ("dk", 1):
                        for q in range(N_CG + 1):
                            act.wait_ge(dv_turned, q + 1)
                            copy_chunk(q, BANK_O + q % 2, dv_natural)

                def exp_unit(u):
                    width = unit_width(u)
                    act.wait_ge(biased, u + 1)
                    if UNITS[u][0] == "C":
                        act.wait_ge(sink_put, u - GROUP_U + 1)
                        width += 1
                    row = prob[:, u % 3, 0:width]
                    nc.scalar.activation(row, row, ACT.Exp, scale=-1.0, bias=stat[:, u % 4, 0:1],
                                         accum_out=stat[:, u % 4, 1:2]).then_inc(expd, 1)

                def copy_probs(u):
                    n = BLOCKS[u] - 1
                    if n == 0:
                        return
                    act.wait_ge(turned_a, copies_a(u))
                    if u >= 2:
                        act.wait_ge(values_ready, u // 2)
                    nc.scalar.copy(probT[:, u % 2, 0:n * P], psum[:, 2 + 2 * (u % 2), 0:n * P]).then_inc(copied_a, 1)

                def y_high(k):
                    act.wait_ge(tile_done, N_IN)
                    if k < 2:
                        act.wait_ge(ya_ready, 6)
                    elif k < 4:
                        act.wait_ge(bc_used, k - 1)
                    else:
                        act.wait_ge(gated, GROUP_P * {6: 1, 4: 2, 5: 3, 7: 4}[k])
                    nc.scalar.copy(h_hi[:, k], xy[:, k]).then_inc(y_hi_ready, 1)

                for s in range(NU + 2):
                    if s % 2:
                        if s >= 2:
                            copy_probs(s - 2)
                    if s < NU:
                        exp_unit(s)
                    if s >= 2 and s % 2 == 0:
                        copy_probs(s - 2)
                    if s in V1_STEPS:
                        q = V1_STEPS[s]
                        act.wait_ge(v1_turned, q + 1)
                        act.wait_ge(values_ready, GROUP_P)
                        copy_chunk(q, BANK_V, v1_natural)
                    if s in Y_SPLIT:
                        y_high(Y_SPLIT[s])
                    if s == W29_STEP:
                        high_half(N_IN + 1)
                y_high(7)
                for f in range(KT):
                    if f + 2 < KT:
                        high_half(N_IN + f + 2)
                    tile_read(act, N_IN + f)
                    dst = squares if f == 0 else square
                    if f >= 2:
                        act.wait_ge(sq_added, f - 1)
                    nc.scalar.activation(dst, xy[:, f], ACT.Square).then_inc(x_sq, 1)

            @block.tensor
            def _(pe):
                norm_pe(pe)

                def products(p, k, order):
                    for w, h in ((w_hi, h_hi), (w_hi, h_lo), (w_lo, h_hi)):
                        for c in range(NCH):
                            last = nc.tensor.matmul(psum[:, 3 * p + c, 0:CH], w[:, p, k, :],
                                                    h[:, k, c * CH:(c + 1) * CH],
                                                    start=(k == order[0] and w is w_hi and h is h_hi),
                                                    stop=(k == order[-1] and w is w_lo))
                    return last

                def project_pair(pair, order=range(KT), until=None):
                    for p in range(2):
                        pe.wait_ge(lo_ready, 2 * pair + p + 1)
                        pe.wait_ge(set_free[p], pair)
                        for k in order:
                            if p == 0 and until:
                                until(k)
                            last = products(p, k, order)
                        last.then_inc(tile_done, 1)

                def project_first():
                    pe.wait_ge(lo_ready, 2)
                    pe.wait_ge(rstd_copied, NCH)
                    together = 5
                    for k in range(together):
                        pe.wait_ge(h_odd if k % 2 else h_even, k // 2 + 1)
                        for p in range(2):
                            products(p, k, range(KT))
                    for p in range(2):
                        for k in range(together, KT):
                            if p == 0:
                                pe.wait_ge(h_odd if k % 2 else h_even, k // 2 + 1)
                            last = products(p, k, range(KT))
                        last.then_inc(tile_done, 1)

                def project(lo, hi, order=range(KT)):
                    with pe.Fori(lo // 2, hi // 2) as pair:
                        project_pair(pair, order=order)

                def turn(src_of, count, tile, sem_out, sem_read):
                    tile_read(pe, tile - 1)
                    tile_read(pe, tile)
                    for q in range(count):
                        if q >= 2:
                            pe.wait_ge(sem_read, q - 1)
                        for i in range(3):
                            t = 3 * (q % 3) + i
                            last = nc.tensor.transpose(psum[:, BANK_A + q % 2, i * P:(i + 1) * P],
                                                       src_of(q // 3)[:, t * P:(t + 1) * P], ident[:, :])
                        last.then_inc(sem_out, 1)

                def turn_values(src, bank, signal):
                    for b in range(src.shape[-1] // P):
                        last = nc.tensor.transpose(psum[:, bank, b * P:(b + 1) * P], src[:, b * P:(b + 1) * P],
                                                   ident[:, :])
                    last.then_inc(signal, 1)

                def mod_sums(j):
                    pe.wait_ge(mod_used, KT * (j + 1))
                    if j > 0:
                        pe.wait_ge(mod_copied, j)
                    for q in range(4):
                        c, half = divmod(q, 2)
                        last = nc.tensor.matmul(psum[32 * q:32 * q + 32, BANK_V, :], ones_m[:, :],
                                                mod_part[c][:, half * 512:(half + 1) * 512],
                                                start=True, stop=True, skip_group_check=True)
                    last.then_inc(mod_sum, 1)

                def mod_turn(j):
                    pe.wait_ge(mod_copied, j + 1)
                    if j > 0:
                        pe.wait_ge(mod_read, j)
                    for f in range(4):
                        last = nc.tensor.transpose(psum[:, BANK_O, f * P:(f + 1) * P], mod_row[:, f * P:(f + 1) * P],
                                                   ident[:, :])
                    last.then_inc(mod_turned, 1)

                project_first()
                project(2, 4)
                turn(qD, 6, NO["av", 1], av_turned, av_natural)
                project(4, 8)
                pe.wait_ge(av_normal, 1)
                pe.wait_ge(mix_in, 32)
                for q in range(6):
                    j = q // 3
                    if q >= 2:
                        pe.wait_ge(mix_read, q - 1)
                    for i in range(3):
                        t = 3 * (q % 3) + i
                        for r in range(2):
                            last = nc.tensor.matmul(psum[64 * r:64 * r + 64, BANK_A + q % 2, i * P:(i + 1) * P],
                                                    vA[:, t, (2 * j + r) * 64:(2 * j + r + 1) * 64],
                                                    wsT[:, 2 * j + r, :], start=True, stop=True,
                                                    skip_group_check=True)
                    last.then_inc(mixed, 1)
                project(8, 14)
                pe.wait_ge(mix_read, 6)
                mod_sums(0)
                project(14, 16)
                mod_turn(0)
                project(16, 18)
                with pe.If(layer < DEPTH - 1):
                    mod_sums(1)
                project(18, 20)
                with pe.If(layer < DEPTH - 1):
                    mod_turn(1)
                project(20, 22)
                with pe.If(layer < DEPTH - 1):
                    mod_sums(2)
                    pe.wait_ge(mod_read, 2)
                    pe.wait_ge(mod_copied, 3)
                pe.wait_ge(mod_read, 1)
                turn(lambda j: kD(0), 3, NO["cv", 0], cv_turned, cv_natural)
                project(22, 24)
                pe.wait_ge(cv_natural, 3)
                with pe.If(layer < DEPTH - 1):
                    mod_turn(2)
                project(24, 26)
                with pe.If(layer < DEPTH - 1):
                    pe.wait_ge(mod_read, 3)
                tile_read(pe, NO["dv", 0])
                for q in range(N_CG + 1):
                    if q >= 2:
                        pe.wait_ge(dv_natural, q - 1)
                    if q < N_CG:
                        pe.wait_ge(chunk0_put, q + 1)
                    turn_values(chunk0[q] if q < N_CG else dv_kept[0][:, CTX], BANK_O + q % 2, dv_turned)
                project(26, 28)

                pe.wait_ge(set_free0, N_IN // 2)
                pe.wait_ge(set_free1, N_IN // 2)
                pe.wait_ge(dv_natural, N_CG + 1)
                pe.wait_ge(rope_ready, 3)
                pe.wait_ge(layer_in, 16 * LAYER_IN)

                def scores(u):
                    if u >= 2:
                        pe.wait_ge(biased, u - 1)
                    for src, at, width in score_pieces(u):
                        last = nc.tensor.matmul(psum[:, u % 2, at:at + width], queries(u), src, start=True, stop=True,
                                                skip_group_check=True)
                    last.then_inc(scores_ready, 1)

                def turn_probs(u):
                    n = BLOCKS[u]
                    pe.wait_ge(normed, u + 1)
                    if u >= 2:
                        if copies_a(u - 2):
                            pe.wait_ge(copied_a, copies_a(u - 2))
                        pe.wait_ge(copied_b, u - 1)
                    bank = 2 + 2 * (u % 2)
                    for b in range(n):
                        into = psum[:, bank, b * P:(b + 1) * P] if b < n - 1 else psum[:, bank + 1, 0:P]
                        last = nc.tensor.transpose(into, prob[:, u % 3, b * P:(b + 1) * P], ident[:, :])
                        if b == n - 2:
                            last.then_inc(turned_a, 1)
                    last.then_inc(turned_b, 1)

                def values(pair):
                    u = 2 * pair
                    if copies_a(u + 1):
                        pe.wait_ge(copied_a, copies_a(u + 1))
                    pe.wait_ge(copied_b, u + 2)
                    if pair >= 1:
                        pe.wait_ge(gated, pair)
                    if pair == 0:
                        pe.wait_ge(cache0_in, 16)
                    if pair == 3 * GROUP_P:
                        pe.wait_ge(cache1_in, 16)
                        pe.wait_ge(v1_natural, N_CG + 1)
                    for b in range(BLOCKS[u]):
                        for r in range(2):
                            last = nc.tensor.matmul(psum[64 * r:64 * r + 64, BANK_O, 0:P], unit_values(u + r)[b],
                                                    probT[:, r, b * P:(b + 1) * P], start=(b == 0),
                                                    stop=(b == BLOCKS[u] - 1), skip_group_check=True)
                    last.then_inc(values_ready, 1)

                for s in range(NU + 3):
                    if s < NU:
                        scores(s)
                    if 2 <= s < NU + 2:
                        turn_probs(s - 2)
                    if s >= 4 and s % 2 == 0:
                        values((s - 4) // 2)
                    if s in V1_STEPS:
                        q = V1_STEPS[s]
                        if q >= 1:
                            pe.wait_ge(v1_natural, q)
                        if q < N_CG:
                            pe.wait_ge(chunk1_put, q + 1)
                        turn_values(chunk1 if q < N_CG else dv_kept[1][:, CTX], BANK_V, v1_turned)
                def y_there(k):
                    if k == Y_ORDER[0]:
                        pe.wait_ge(y_split, KT - 1)
                    if k == Y_ORDER[-1]:
                        pe.wait_ge(y_last, 1)

                project_pair(N_IN // 2, order=Y_ORDER, until=y_there)
                project(N_IN + 2, N_TILES, order=Y_ORDER)

            @block.vector
            def _(dve):
                told, pending = {}, {}

                def tell(ins, signal=dve_step, count=None):
                    ins.then_inc(signal, 1)
                    told[signal.name] = count or told.get(signal.name, 0) + 1
                    pending[signal.name] = (signal, told[signal.name])

                def settle():
                    for signal, count in pending.values():
                        dve.wait_ge(signal, count)
                    pending.clear()

                norm_dve(dve, tell, settle)
                dve.wait_ge(rstd_copied, NCH)
                dve.wait_ge(mod_ready, 1)

                def low(k):
                    dve.wait_ge(h_hi_ready, k + 1)
                    for cols, c in PARTS:
                        last = nc.vector.scalar_tensor_tensor(h_lo[:, k, cols], slots[:, k, cols],
                                                              mod[:, k, c:c + 1], h_hi[:, k, cols],
                                                              ALU.add, ALU.subtract)
                    last.then_inc(h_even, 1)

                for k in range(KT):
                    for cols, c in PARTS:
                        ins = nc.vector.scalar_tensor_tensor(slots[:, k, cols], xy[:, k, cols],
                                                             mod[:, KT + k, c:c + 1], rstd_all[:, cols],
                                                             ALU.mult, ALU.mult)
                        tell(ins, scaled if c == 1 else dve_step)
                    if k % 2:
                        low(k - 1)
                settle()

                def y_of(part, t):
                    return xy[:, 2 * "abcd".index(part[0]) + t]

                def multiply(step):
                    for g in range(MOD_ROWS * step, MOD_ROWS * (step + 1)):
                        k = g % KT
                        dve.wait_ge(mod_in[g % 2], 16 * (g // 2 + 1))
                        for c in range(2):
                            if k == 0:
                                ins = nc.vector.tensor_scalar(mod_part[c], mod_rows[g % 2], silu[:, k, c:c + 1],
                                                              None, ALU.mult)
                            else:
                                ins = nc.vector.scalar_tensor_tensor(mod_part[c], mod_rows[g % 2],
                                                                     silu[:, k, c:c + 1], mod_part[c],
                                                                     ALU.mult, ALU.add)
                            tell(ins, part_step if c == 0 else mod_used)
                        settle()

                def copy_third(j):
                    dve.wait_ge(mod_sum, j + 1)
                    nc.vector.tensor_copy(mod_row, psum[:, BANK_V, :]).then_inc(mod_copied, 1)

                def read_third(j):
                    dve.wait_ge(mod_turned, j + 1)
                    dst = mod[:, 2 * KT:, :] if j == 0 else mods[:, 1, (j - 1) * KT:j * KT, :]
                    sums = psum[:, BANK_O, :].rearrange("p (f q m) -> p q f m", f=4, q=4)
                    for c in range(2):
                        to = dst[:, :, c].rearrange("p (h f) -> p h f", h=2)
                        tell(nc.vector.tensor_tensor(to, sums[:, 2 * c:2 * c + 2, :, 0], to, ALU.add),
                             mod_read if c else part_step if j else dve_step)
                    settle()
                    if j == 2:
                        for c in range(2):
                            tell(nc.vector.scalar_tensor_tensor(dst[:, :, c], dst[:, :, c], 1.0, layer_g[:, 1],
                                                                ALU.add, ALU.mult), part_step)
                        settle()

                n_tanh = 0
                n_rope = 0
                for n, (part, t) in enumerate(TILES):
                    if n == SUM_TILES[2]:
                        settle()
                        with dve.If(layer < DEPTH - 1):
                            copy_third(2)
                    y = y_of(part, t)
                    free = set_free[n % 2]
                    if (part, t) == ("az", 0):
                        dve.wait_ge(x_saved, 16 * KT)
                    if part[1] == "z":
                        dve.wait_ge(tanh_ready, n_tanh + 1)
                        th = kD(1 - n_tanh % 2) if part != "dz" else kD(1)
                        tell(nc.vector.scalar_tensor_tensor(chunks(y), chunks(th), 1.0, tile_psum(n),
                                                                 ALU.add, ALU.mult), free, n // 2 + 1)
                        n_tanh += 1
                    elif part in ("au", "bb"):
                        dve.wait_ge(tile_done, n + 1)
                        settle()
                        tell(nc.vector.scalar_tensor_tensor(chunks(y), tile_psum(n), 0.5, chunks(y),
                                                                 ALU.mult, ALU.mult), free, n // 2 + 1)
                    elif part == "bh":
                        dve.wait_ge(tile_done, n + 1)
                        tile_read(dve, NO["bc", t])
                        tell(nc.vector.tensor_tensor(chunks(kC), tile_psum(n), chunks(kC), ALU.mult), free, n // 2 + 1)
                        settle()
                        if t == 0:
                            dve.wait_ge(layer_in, 16 * LAYER_IN)
                        s = qC(t)
                        tell(nc.vector.tensor_scalar(s, kC, conv_w[:, t, 1:2], None, ALU.mult))
                        settle()
                        for a, b in ((0, DEC_SEQ), (DEC_SEQ, T)):
                            tell(nc.vector.scalar_tensor_tensor(s[:, a + 1:b], kC[:, a:b - 1], conv_w[:, t, 0:1],
                                                               s[:, a + 1:b], ALU.mult, ALU.add))
                        settle()
                        for a, b in ((0, DEC_SEQ), (DEC_SEQ, T)):
                            tell(nc.vector.scalar_tensor_tensor(s[:, a:b - 1], kC[:, a + 1:b], conv_w[:, t, 2:3],
                                                               s[:, a:b - 1], ALU.mult, ALU.add))
                        settle()
                        tell(nc.vector.tensor_tensor(y, y, s, ALU.mult), bc_used)
                    elif part in ("cq", "ck"):
                        tile_read(dve, n)
                        raw = slots[:, n_rope, LAT]
                        if n_rope == 0:
                            dve.wait_ge(rope_in, 16)
                        else:
                            settle()
                        tell(nc.vector.stream_shuffle(swapped, raw, [(i + 16) % 32 for i in range(32)]), swap_ready)
                        settle()
                        tell(nc.vector.tensor_tensor(swapped, swapped, sin_t, ALU.mult))
                        settle()
                        dve.wait_ge(cos_ready, n_rope + 1)
                        tell(nc.vector.tensor_tensor(raw, raw, swapped, ALU.add), rope_ready)
                        n_rope += 1
                    if (part, t) == ("az", 1):
                        ss, rs = small[:, 4, :], small[:, 5, :]
                        dve.wait_ge(av_natural, 6)
                        for j in range(2):
                            sq = squares.rearrange("p (t d) -> p t d", t=TT)
                            vj = vA[:, :, j * P:(j + 1) * P]
                            tell(nc.vector.tensor_tensor(sq, vj, vj, ALU.mult))
                            settle()
                            tell(nc.vector.tensor_reduce(
                                ss.rearrange("p (t h) -> p t h", t=TT)[:, :, 2 * j:2 * j + 2],
                                squares.rearrange("p (t h d) -> p t h d", t=TT, h=2), AX_X, ALU.add))
                            settle()
                        tell(nc.vector.tensor_scalar(ss, ss, 1.0 / HEAD_DIM, EPS, ALU.mult, ALU.add))
                        settle()
                        rsqrt(tell, settle, rs, ss, small[:, 6, :], small[:, 7, :])
                        flat = vA[:, :, :].rearrange("p t (h d) -> p (t h) d", h=4)
                        tell(nc.vector.tensor_tensor(
                            flat, flat, rs.rearrange("p (n o) -> p n o", o=1).broadcast_to([P, 36, HEAD_DIM]),
                            ALU.mult), av_normal)
                    if (part, t) == ("bb", 0):
                        dve.wait_ge(mix_in, 32)
                        for q in range(6):
                            j, c = q // 3, q % 3
                            dve.wait_ge(mixed, q + 1)
                            tmp = flat_prob[:, (q % 2) * CH:(q % 2 + 1) * CH].rearrange("p (t n) -> p t n", t=3)
                            tell(nc.vector.tensor_tensor(
                                tmp, psum[:, BANK_A + q % 2, 0:CH].rearrange("p (t n) -> p t n", t=3),
                                bs[:, j:j + 1, :].broadcast_to([P, 3, P]), ALU.add), mix_read)
                            settle()
                            yq = xy[:, j, c * CH:(c + 1) * CH].rearrange("p (t n) -> p t n", t=3)
                            tell(nc.vector.tensor_tensor(yq, yq, tmp, ALU.mult), ya_ready)

                    step = n - MOD_TILE
                    if 0 <= step < MOD_STEPS:
                        settle()
                        if step < MOD_STEPS // THIRDS:
                            multiply(step)
                        else:
                            if n == SUM_TILES[0]:
                                copy_third(0)
                            if n == TURN_TILES[0]:
                                read_third(0)
                            with dve.If(layer < DEPTH - 1):
                                if n == SUM_TILES[1]:
                                    copy_third(1)
                                if n == TURN_TILES[1]:
                                    read_third(1)
                                multiply(step)
                    if n == TURN_TILES[2]:
                        settle()
                        with dve.If(layer < DEPTH - 1):
                            read_third(2)

                settle()
                tell(nc.vector.tensor_scalar(sinks[:, :], sinks[:, :], -1.0, None, ALU.mult))
                settle()

                def bias_unit(u):
                    mixer, i, t, r = UNITS[u]
                    width = unit_width(u)
                    row = prob[:, u % 3, :]
                    dve.wait_ge(scores_ready, u + 1)
                    if u >= 3:
                        dve.wait_ge(turned_b, u - 2)
                    if mixer == "C":
                        if u == GROUP_U:
                            dve.wait_ge(band_in, 16)
                        at = 2 * P if i == LT else base(u)
                        bias = band[:, at:at + width]
                        first = sinks[:, 2 * t + r:2 * t + r + 1]
                        tell(nc.vector.tensor_copy(row[:, width:width + 1], first), sink_put)
                    else:
                        first = -NEG
                        if u == 0:
                            dve.wait_ge(zeros_put, 1)
                        if i < LT:
                            dve.wait_ge(bias_ready, bias_table(u) + 1)
                        bias = table[:, bias_table(u) % TABLES if i < LT else 0, 0:width]
                    nc.vector.tensor_tensor_reduce(out=row[:, 0:width], in0=psum[:, u % 2, 0:width], in1=bias,
                                                   scale=1.0, scalar=first, op0=ALU.add, op1=ALU.min,
                                                   accum_out=stat[:, u % 4, 0:1]).then_inc(biased, 1)

                def norm_unit(u):
                    width = unit_width(u)
                    dve.wait_ge(expd, u + 1)
                    tell(nc.vector.reciprocal(stat[:, u % 4, 2:3], stat[:, u % 4, 1:2]))
                    settle()
                    row = prob[:, u % 3, 0:width]
                    nc.vector.tensor_scalar(row, row, stat[:, u % 4, 2:3], None, ALU.mult).then_inc(normed, 1)

                def copy_probs(u):
                    b = BLOCKS[u] - 1
                    dve.wait_ge(turned_b, u + 1)
                    if u >= 2:
                        dve.wait_ge(values_ready, u // 2)
                    nc.vector.tensor_copy(probT[:, u % 2, b * P:(b + 1) * P], psum[:, 3 + 2 * (u % 2), 0:P]
                                          ).then_inc(copied_b, 1)

                def gate_pair(pair):
                    mixer, i, t, _ = UNITS[2 * pair]
                    dve.wait_ge(values_ready, pair + 1)
                    y, out = xy[:, (4 if mixer == "C" else 6) + t], psum[:, BANK_O, 0:P]
                    if mixer == "D" and i < LT:
                        rg, cg = divmod(i, N_CG)
                        y = grid(y)[:, rg * QR:(rg + 1) * QR, cg * QC:(cg + 1) * QC]
                        out = out.rearrange("p (r c) -> p r c", c=QC)
                    else:
                        y = y[:, i * P:(i + 1) * P]
                    nc.vector.scalar_tensor_tensor(y, out, 0.5, y, ALU.mult, ALU.mult).then_inc(gated, 1)

                for s in range(NU + 4):
                    if s < NU:
                        bias_unit(s)
                    if 1 <= s < NU + 1:
                        norm_unit(s - 1)
                    if 2 <= s < NU + 2:
                        copy_probs(s - 2)
                    if s >= 5 and s % 2:
                        gate_pair((s - 5) // 2)
                dve.wait_ge(y_hi_ready, KT)
                nc.vector.tensor_tensor(h_lo[:, 7], xy[:, 7], h_hi[:, 7], ALU.subtract).then_inc(y_last, 1)
                dve.wait_ge(y_last, 1)
                dve.wait_ge(y_split, KT - 1)
                for f in range(KT):
                    n = N_IN + f
                    dve.wait_ge(tile_done, n + 1)
                    dve.wait_ge(x_loaded[f % 2], 16 * (f // 2 + 1))
                    new, old = chunks(xy[:, f]), chunks(x_new[:, f % 2])
                    for ch, cols, c in pieces():
                        last = nc.vector.scalar_tensor_tensor(new[:, ch, cols], tile_psum(n)[:, ch, cols],
                                                              mod[:, 2 * KT + f, c:c + 1], old[:, ch, cols],
                                                              ALU.mult, ALU.add)
                        if c == 1:
                            last.then_inc(set_free[n % 2], 1)
                    if f >= 2:
                        dve.wait_ge(x_sq, f)
                        if f >= 3:
                            dve.wait_ge(sq_added, f - 2)
                        nc.vector.tensor_tensor(squares, squares, square, ALU.add).then_inc(sq_added, 1)
                dve.wait_ge(x_sq, KT)
                dve.wait_ge(sq_added, KT - 2)
                nc.vector.tensor_tensor(squares, squares, square, ALU.add).then_inc(sq_added, 1)

          nc.all_engine_barrier(sems_to_clear=layer_sems)

        y_scaled = sem("y_scaled")
        y_out = sem("y_out")
        with nc.Block() as block:
            @block.sync
            def _(sp):
                for k in range(KT):
                    sp.wait_ge(y_scaled, k + 1)
                    sp.dma_start(yT[k], slots[:, k]).then_inc(y_out, 16)
                sp.wait_ge(y_out, 16 * KT)

            @block.tensor
            def _(pe):
                norm_pe(pe)

            @block.vector
            def _(dve):
                step = [0]

                def own(ins):
                    ins.then_inc(dve_step, 1)
                    step[0] += 1

                def settle():
                    dve.wait_ge(dve_step, step[0])

                norm_dve(dve, own, settle)
                dve.wait_ge(rstd_ready, TT)
                for k in range(KT):
                    nc.vector.scalar_tensor_tensor(chunks(slots[:, k]), chunks(xy[:, k]), fin_g[:, k:k + 1],
                                                   psum[:, RSTD_BANK:RSTD_BANK + 3, 0:CH], ALU.mult, ALU.mult
                                                   ).then_inc(y_scaled, 1)


def constants():
    f = np.float32
    ident = np.eye(P, dtype=f)
    half = HEAD_DIM // 4
    freqs = f(ROPE_BASE) ** (-np.arange(half, dtype=f) / f(half))
    t = np.arange(DEC_SEQ)
    d = np.arange(P) % HEAD_DIM
    pos = np.where(d[:, None] < HEAD_DIM // 2, (t // GRID_W)[None, :], (t % GRID_W)[None, :]).astype(f)
    ang = (pos * freqs[d % half][:, None]).astype(f)
    sign = np.where(d % (2 * half) < half, f(-1), f(1))[:, None]
    rope = np.concatenate([np.cos(ang), sign * np.sin(ang)], axis=1).astype(f)
    q, k = np.arange(P)[:, None], np.arange(P)[None, :]
    zero = np.zeros((P, P), f)
    band = np.concatenate([np.where(k >= q, f(0), f(-NEG)), zero, zero, np.where(k <= q, f(0), f(-NEG))],
                          axis=1).astype(f)
    row, col = np.arange(P) // QC, np.arange(P) % QC
    row_masks, col_masks = [], []
    for rg in range(2):
        key, query = d_keys(rg * N_CG)[0] + np.arange(KR)[None, :], (rg * QR + row)[:, None]
        start = np.clip(query - WIN_R // 2, 0, ROWS - WIN_R)
        row_masks.append(np.where((key >= start) & (key < start + WIN_R), f(0), f(-NEG)))
    for cg in range(N_CG):
        key, query = d_keys(cg)[1] + np.arange(KC)[None, :], (cg * QC + col)[:, None]
        start = np.clip(query - WIN_C // 2, 0, GRID_W - WIN_C)
        if cg == BIAS_CLASS.index(BIAS_CLASS[cg]):
            col_masks.append(np.where((key >= start) & (key < start + WIN_C), f(0), f(-NEG)))
    return ident, rope, band, np.stack(row_masks, axis=1).astype(f), np.stack(col_masks, axis=1).astype(f)


def rpb_tables(rpb):
    padded = np.pad(rpb, ((0, 0), (0, 0), (WIN_R, WIN_R), (2 * WIN_C, 2 * WIN_C)))
    row, col = np.arange(P)[:, None, None] // QC, np.arange(P)[:, None, None] % QC
    tables = []
    for t in range(2):
        for rg in range(2):
            for cls in range(N_CLASS):
                cg = BIAS_CLASS.index(cls)
                first_row, first_col = d_keys(rg * N_CG + cg)
                dr = first_row + np.arange(KR)[None, :, None] - (rg * QR + row) + WIN_R - 1 + WIN_R
                dc = first_col + np.arange(KC)[None, None, :] - (cg * QC + col) + WIN_C - 1 + 2 * WIN_C
                for r in range(2):
                    tables.append(padded[:, 2 * t + r, dr, dc].reshape(DEPTH, P, KR * KC))
    return np.stack(tables, axis=1)


def kernel(x_prompt, x_sample, cache_c_k, cache_c_v, cache_d_k, cache_d_v, c, c_ctx, norm_g, w_mod, b_mod,
           w_in, w_out, w_s, b_s, w_conv, sink, rpb, final_g):
    import concourse.bacc as bacc
    from concourse.bass_utils import run_bass_kernel_spmd

    a = dict(x_prompt=x_prompt, x_sample=x_sample, cache_c_k=cache_c_k, cache_c_v=cache_c_v, cache_d_k=cache_d_k,
             cache_d_v=cache_d_v, c=c, c_ctx=c_ctx, norm_g=norm_g, w_mod=w_mod, b_mod=b_mod, w_in=w_in,
             w_out=w_out, w_s=w_s, b_s=b_s, w_conv=w_conv, sink=sink, rpb=rpb, final_g=final_g)
    a = {k: np.asarray(v) for k, v in a.items()}
    cat, con = np.concatenate, np.ascontiguousarray

    def heads_c(m, axis):
        parts = np.split(m, 4, axis=axis)
        return cat([parts[h] for h in C_HEADS], axis=axis)

    def columns(part, t):
        m = a["w_in"][:, :, COLUMNS[part]:COLUMNS[part] + (P if part in ("ck", "cv") else 2 * P)]
        if part in ("cq", "cz"):
            m = heads_c(m, 2)
        return m[:, :, t * P:(t + 1) * P]

    w_out_p = cat([a["w_out"][:, :512], heads_c(a["w_out"][:, 512:768], 1), a["w_out"][:, 768:]], axis=1)
    tiles = [columns(*x) for x in TILES] + [w_out_p[:, :, f * P:(f + 1) * P] for f in range(KT)]
    ident, rope, band, rows, cols = constants()
    by_p = lambda m: con(np.moveaxis(m.reshape(*m.shape[:-1], -1, P), -1, 1))
    data = {
        "xT": cat([a["x_sample"][0], a["x_prompt"][0]]).T.reshape(KT, P, T),
        "cond": np.stack([a["c"][0], a["c_ctx"]], axis=1).reshape(KT, P, 2).transpose(1, 0, 2),
        "w_mod": a["w_mod"],
        "b_mod": a["b_mod"].reshape(DEPTH, 24, P).transpose(2, 0, 1),
        "norm_g": a["norm_g"].reshape(DEPTH, KT, P).transpose(2, 0, 1),
        "final_g": a["final_g"].reshape(KT, P).T,
        "w_tiles": np.stack([m.reshape(DEPTH, KT, P, P).transpose(0, 2, 1, 3) for m in tiles], axis=1),
        "w_sT": a["w_s"].transpose(0, 3, 1, 2),
        "b_s": np.repeat(a["b_s"].reshape(DEPTH, 2, 2, 1, P), HEAD_DIM, axis=3
                         ).reshape(DEPTH, 2, P, P).transpose(0, 2, 1, 3),
        "w_conv": a["w_conv"].reshape(DEPTH, 3, 2, P).transpose(0, 3, 2, 1),
        "sink": np.repeat(a["sink"][:, None, list(C_HEADS)], P, axis=1),
        "rpb": rpb_tables(a["rpb"]),
        "cckT": a["cache_c_k"][0].reshape(DEPTH, P, P).transpose(0, 2, 1),
        "ccv": a["cache_c_v"][0].reshape(DEPTH, P, P),
        "cdkT": a["cache_d_k"][0].reshape(DEPTH, P, 2, P).transpose(0, 3, 2, 1),
        "cdv": a["cache_d_v"][0].reshape(DEPTH, P, 2, P),
        "ident_c": ident, "rope_c": rope, "band_c": band, "row_c": rows, "col_c": cols,
    }
    outs = {"yT": (KT, P, T), "sckT": (DEPTH, P, P), "scvT": (DEPTH, P, P), "sdkT": (DEPTH, 2, P, P),
            "sdvT": (DEPTH, 2, P, P)}
    nc = bacc.Bacc("TRN2", target_bir_lowering=False, num_devices=1)
    data = {k: con(v) for k, v in data.items()}
    args = {k: nc.dram_tensor("in_" + k, v.shape, F32, kind="ExternalInput").ap() for k, v in data.items()}
    args |= {k: nc.dram_tensor("out_" + k, s, F32, kind="ExternalOutput").ap() for k, s in outs.items()}
    build(nc, **args)
    r = run_bass_kernel_spmd(nc, [{"in_" + k: v for k, v in data.items()}], core_ids=[0]).results[0]

    y = r["out_yT"].reshape(D_MODEL, T).T
    natural = lambda m: m.reshape(DEPTH, -1, SEQ).transpose(0, 2, 1).reshape(1, DEPTH, SEQ, -1, HEAD_DIM)
    return (con(y[DEC_SEQ:])[None], con(y[:DEC_SEQ])[None], con(natural(r["out_sckT"])),
            con(natural(r["out_scvT"])), con(natural(r["out_sdkT"])), con(natural(r["out_sdvT"])))
```

```python
from contextlib import ExitStack

import numpy as np

import concourse.bass as bass
from concourse import mybir

F32 = mybir.dt.float32
F32R = mybir.dt.float32r
I32 = mybir.dt.int32
ALU = mybir.AluOpType
ACT = mybir.ActivationFunctionType
AX_X = mybir.AxisListType.X

P = 128
D_MODEL = 1024
DEPTH = 2
SEQ = 128
DEC_SEQ = 1024
T = DEC_SEQ + SEQ
KT = D_MODEL // P
CH = 384
NCH = T // CH
TT = T // P
LT = DEC_SEQ // P
GRID_W = 64
ROWS = DEC_SEQ // GRID_W
WIN_R = 8
WIN_C = 16
HEAD_DIM = 64
EPS = 1e-6
NEG = -1e30
SCALE = HEAD_DIM ** -0.5
ROPE_BASE = 10000.0

TILES = [("av", 0), ("av", 1), ("az", 0), ("au", 0), ("az", 1), ("au", 1),
         ("bz", 0), ("bb", 0), ("bc", 0), ("bh", 0), ("bz", 1), ("bb", 1), ("bc", 1), ("bh", 1),
         ("cz", 0), ("cz", 1), ("cq", 0), ("cq", 1), ("ck", 0), ("cv", 0),
         ("dz", 0), ("dz", 1), ("dv", 0), ("dv", 1), ("dk", 0), ("dk", 1), ("dq", 0), ("dq", 1)]
N_IN = len(TILES)
NO = {x: n for n, x in enumerate(TILES)}
N_TILES = N_IN + KT
COLUMNS = {"au": 0, "av": 256, "az": 512, "bb": 768, "bc": 1024, "bh": 1280, "bz": 1536, "cq": 1792,
           "ck": 2048, "cv": 2176, "cz": 2304, "dq": 2560, "dk": 2816, "dv": 3072, "dz": 3328}
C_HEADS = (0, 2, 1, 3)
COPIED = ("av", "bc", "cq", "ck", "cv", "dv", "dk", "dq")

RSQRT_MAGIC = 0x5F3759DF

QR, QC = 8, 16
KR, KC = QR + WIN_R // 2, 2 * WIN_C
BLK_R = P // KC
N_CG = GRID_W // QC
N_BLK = ROWS // BLK_R
BIAS_CLASS = (0, 1, 1, 2)
N_CLASS = 3
TABLES = 5
S_W = P + KR * KC
PROBS = 4
assert S_W == 512


def d_keys(i):
    rg, cg = divmod(i, N_CG)
    return (0, ROWS - KR)[rg], min(max(cg * QC - WIN_C // 2, 0), GRID_W - KC)


GROUPS = (("D", 0), ("C", 0), ("C", 1), ("D", 1))
UNITS = [(mixer, i, t, r) for mixer, t in GROUPS for i in range(LT + 1) for r in range(2)]
NU = len(UNITS)
GROUP_U = 2 * (LT + 1)
GROUP_P = LT + 1


def bias_table(u):
    _, i, t, r = UNITS[u]
    rg, cg = divmod(i, N_CG)
    return (((t * 2 + rg) * N_CLASS + BIAS_CLASS[cg]) * 2) + r


N_TABLES = 4 * 2 * N_CLASS
READERS = [[u for u in range(NU) if UNITS[u][0] == "D" and UNITS[u][1] < LT and bias_table(u) == m]
           for m in range(N_TABLES)]


def build(nc, xT, cond, w_mod, b_mod, norm_g, final_g, w_tiles, w_sT, b_s, w_conv, sink, rpb,
          cckT, ccv, cdkT, cdv, ident_c, rope_c, band_c, row_c, col_c, yT, sckT, scvT, sdkT, sdvT):
    with ExitStack() as ctx:
        def sb(name, shape, dt=F32):
            return ctx.enter_context(nc.sbuf_tensor(name, shape, dt))

        def sem(name):
            return ctx.enter_context(nc.semaphore(name))

        x_kept = nc.dram_tensor("x_kept", [P, KT, T], F32, kind="Internal").ap()

        h_hi = sb("h_hi", [P, KT, T], F32R)
        h_lo = sb("h_lo", [P, KT, T], F32R)
        xy = sb("xy", [P, KT, T])
        slots = sb("slots", [P, 11, T])
        w_raw = sb("w_raw", [P, 2, KT, P])
        w_hi = sb("w_hi", [P, 2, KT, P], F32R)
        w_lo = sb("w_lo", [P, 2, KT, P], F32R)
        prob = sb("prob", [P, PROBS, S_W + 2])
        probT = sb("probT", [P, 2, S_W])
        table = sb("table", [P, TABLES, S_W])
        ident = sb("ident", [P, P])
        row_mask = sb("row_mask", [P, 2, KR])
        col_mask = sb("col_mask", [P, N_CLASS, KC])
        ck_c = sb("ck_c", [P, P])
        cv_c = sb("cv_c", [P, P])
        ck_d = sb("ck_d", [P, 2, P])
        mods = sb("mods", [P, DEPTH, 24, 2])
        mod = sb("mod", [P, 24, 2])
        layer_g = sb("layer_g", [P, DEPTH, KT])
        ones_m = sb("ones_m", [P, 32])
        silu = sb("silu", [P, KT, 2])
        fin_g = sb("fin_g", [P, KT])
        conv_w = sb("conv_w", [P, 2, 3])
        sinks = sb("sinks", [P, 4])
        stat = sb("stat", [P, 4, 4])
        psum = ctx.enter_context(nc.psum_tensor("psum", [P, 8, 512], F32))

        qC, kC, qD, kD = (lambda t: slots[:, t]), slots[:, 2], (lambda t: slots[:, 3 + t]), (lambda t: slots[:, 5 + t])
        vC = slots[:, 7].rearrange("p (t d) -> p t d", t=TT)
        v_flat = slots[:, 8:10].rearrange("p a n -> p (a n)")
        vA = v_flat.rearrange("p (t d) -> p t d", t=TT)
        vD = v_flat.rearrange("p (b d) -> p b d", d=P)
        V_CTX, V_CACHE = N_CG * N_BLK, N_CG * N_BLK + 1
        dv_kept = (slots[:, 3], slots[:, 10])
        flat_prob = prob[:, :, :].rearrange("p a n -> p (a n)")
        flat_probT = probT[:, :, :].rearrange("p a n -> p (a n)")
        flat_table = table[:, :, :].rearrange("p a n -> p (a n)")
        squares = flat_prob[:, 0:T]
        square = slots[:, 10]
        small = flat_prob[:, T:T + 8 * 36].rearrange("p (a n) -> p a n", a=8)
        wsT = flat_probT[:, 0:4 * P].rearrange("p (h n) -> p h n", h=4)
        bs = flat_probT[:, 4 * P:6 * P].rearrange("p (j n) -> p j n", j=2)
        cos_t = flat_table[:, 0:DEC_SEQ]
        sin_t = flat_table[:, DEC_SEQ:2 * DEC_SEQ]
        swapped = slots[:, 4, 0:DEC_SEQ]
        x_new = flat_table[:, 0:2 * T].rearrange("p (a n) -> p a n", a=2)
        band = w_raw[:, 1].rearrange("p k n -> p (k n)")[:, 0:4 * P]
        BANK_A = 6

        LAT, CTX = slice(0, DEC_SEQ), slice(DEC_SEQ, T)

        def chunks(ap):
            return ap.rearrange("p (c n) -> p c n", c=NCH)

        def tile_read(eng, n):
            eng.wait_ge(set_free[n % 2], n // 2 + 1)

        def tile_psum(n):
            return psum[:, 3 * (n % 2):3 * (n % 2) + 3, 0:CH]

        diag = slots[:, 8].rearrange("p (t n) -> p t n", t=TT)
        ones = slots[:, 9, 0:P]
        RSTD_BANK = 3

        rstd_all = slots[:, 10]

        def norm_sums(tiles):
            for t in tiles:
                last = nc.tensor.matmul(psum[:, BANK_A, t:t + 1], squares[:, t * P:(t + 1) * P], ones[:, 0:1],
                                        start=True, stop=True)
            return last

        def norm_spread(pe, signals):
            diag_ready, rstd_ready = signals
            for t in range(TT):
                pe.wait_ge(diag_ready, t + 1)
                nc.tensor.matmul(psum[:, RSTD_BANK + t // 3, (t % 3) * P:(t % 3 + 1) * P], ones[:, :], diag[:, t],
                                 start=True, stop=True).then_inc(rstd_ready, 1)

        def rsqrt(own, settle, out, v, s0, s1):
            own(nc.vector.tensor_scalar(s0.bitcast(I32), v.bitcast(I32), 1, None, ALU.arith_shift_right))
            settle()
            own(nc.vector.tensor_scalar(out.bitcast(I32), s0.bitcast(I32), -1, RSQRT_MAGIC, ALU.mult, ALU.add))
            settle()
            for _ in range(3):
                own(nc.vector.tensor_tensor(s0, out, out, ALU.mult))
                settle()
                own(nc.vector.tensor_tensor(s1, s0, v, ALU.mult))
                settle()
                own(nc.vector.tensor_scalar(s0, s1, -0.5, 1.5, ALU.mult, ALU.add))
                settle()
                own(nc.vector.tensor_tensor(out, out, s0, ALU.mult))
                settle()

        def norm_dve(dve, own, settle, signals):
            diag_ready, _ = signals
            ms, rstd = small[:, 0, 0:TT], small[:, 1, 0:TT]
            own(nc.vector.tensor_scalar(ms, psum[:, BANK_A, 0:TT], 1.0 / D_MODEL, EPS, ALU.mult, ALU.add))
            settle()
            rsqrt(own, settle, rstd, ms, small[:, 2, 0:TT], small[:, 3, 0:TT])
            for t in range(TT):
                nc.vector.tensor_scalar(diag[:, t], ident[:, :], rstd[:, t:t + 1], None, ALU.mult
                                        ).then_inc(diag_ready, 1)

        consts_in = sem("consts_in")
        x_in = sem("x_in")
        wmod_in = [sem(f"wmod_in{i}") for i in range(3)]
        cond_tanh = sem("cond_tanh")
        cond_ready = sem("cond_ready")
        wmod_used = sem("wmod_used")
        modrow_ready = sem("modrow_ready")
        modT_ready = sem("modT_ready")
        x_squared = sem("x_squared")
        squares_added = sem("squares_added")
        pro_step = sem("pro_step")
        pro_norm = [sem("pro_" + x) for x in ("diag_ready", "rstd_ready")]
        pro_ones, pro_sums = sem("pro_ones"), sem("pro_sums")
        vectors_put = sem("vectors_put")

        stage = slots[:, :, :].rearrange("p a n -> p (a n)")
        MOD_W = 2 * D_MODEL
        wmod_sb = stage[:, 0:3 * MOD_W].rearrange("p (b n) -> p b n", b=3)
        modrow = w_raw[:, 0].rearrange("p k n -> p (k n)")[:, 0:512]
        vectors = stage[:, 3 * MOD_W:6 * T]
        silu_c = vectors[:, 0:KT * 32].rearrange("p (k m) -> p k m", k=KT)
        cond_sb = vectors[:, 256:256 + 2 * KT].rearrange("p (k c) -> p k c", c=2)
        tanh_c = vectors[:, 272:272 + 2 * KT].rearrange("p (k c) -> p k c", c=2)
        bmod_sb = vectors[:, 288:288 + 24 * DEPTH].rearrange("p (l n) -> p l n", l=DEPTH)
        square_of = lambda k: slots[:, 10 if k % 2 else 7]
        CONSTS = 7

        with nc.Block() as block:
            @block.sync
            def _(sp):
                sp.dma_start(cond_sb, cond).then_inc(consts_in, 16)
                sp.dma_start(ident[:, :], ident_c).then_inc(consts_in, 16)
                sp.dma_start(bmod_sb, b_mod).then_inc(consts_in, 16)
                sp.dma_start(layer_g[:, :, :], norm_g).then_inc(consts_in, 16)
                sp.dma_start(row_mask[:, :, :], row_c).then_inc(consts_in, 16)
                sp.dma_start(col_mask[:, :, :], col_c).then_inc(consts_in, 16)
                sp.dma_start(fin_g[:, :], final_g).then_inc(consts_in, 16)
                for k in range(KT):
                    sp.dma_start(xy[:, k], xT[k]).then_inc(x_in, 16)
                for n in range(KT):
                    if n >= 3:
                        sp.wait_ge(wmod_used, n - 2)
                    sp.dma_start(wmod_sb[:, n % 3], w_mod[0, n * P:(n + 1) * P, 0:MOD_W]
                                 ).then_inc(wmod_in[n % 3], 16)
                sp.wait_ge(x_in, 16 * KT)

            @block.scalar
            def _(act):
                act.wait_ge(consts_in, 16 * CONSTS)
                nc.scalar.activation(tanh_c, cond_sb, ACT.Tanh, scale=0.5).then_inc(cond_tanh, 1)
                act.wait_ge(x_in, 16 * KT)
                nc.scalar.activation(squares, xy[:, 0], ACT.Square).then_inc(x_squared, 1)
                for k in range(1, KT):
                    if k > 2:
                        act.wait_ge(squares_added, k - 2)
                    nc.scalar.activation(square_of(k), xy[:, k], ACT.Square).then_inc(x_squared, 1)

            @block.tensor
            def _(pe):
                pe.wait_ge(cond_ready, 1)
                for k in range(KT):
                    pe.wait_ge(wmod_in[k % 3], 16 * (k // 3 + 1))
                    for c in range(4):
                        q = 32 * c
                        last = nc.tensor.matmul(psum[q:q + 32, 0, :], silu_c[:, k, :],
                                                wmod_sb[:, k % 3, c * 512:(c + 1) * 512],
                                                start=(k == 0), stop=(k == KT - 1), skip_group_check=True)
                    last.then_inc(wmod_used, 1)
                    if k == 3:
                        pe.wait_ge(pro_ones, 1)
                        pe.wait_ge(squares_added, KT - 1)
                        norm_sums(range(TT)).then_inc(pro_sums, 1)
                    if k == 5:
                        norm_spread(pe, pro_norm)
                pe.wait_ge(modrow_ready, 1)
                for j in range(4):
                    last = nc.tensor.transpose(psum[:, 1, j * P:(j + 1) * P], modrow[:, j * P:(j + 1) * P],
                                               ident[:, :])
                last.then_inc(modT_ready, 1)

            @block.vector
            def _(dve):
                step = [0]

                def own(ins):
                    ins.then_inc(pro_step, 1)
                    step[0] += 1

                def settle():
                    dve.wait_ge(pro_step, step[0])

                own(nc.vector.memset(silu_c, 0.0))
                nc.vector.memset(ones, 1.0).then_inc(pro_ones, 1)
                nc.vector.memset(ones_m[:, :], 1.0).then_inc(vectors_put, 1)
                dve.wait_ge(cond_tanh, 1)
                settle()
                own(nc.vector.scalar_tensor_tensor(tanh_c, tanh_c, 1.0, cond_sb, ALU.add, ALU.mult))
                settle()
                nc.vector.tensor_scalar(silu_c[:, :, 0:2], tanh_c, 0.5, None, ALU.mult).then_inc(cond_ready, 1)
                nc.vector.tensor_scalar(silu[:, :, :], tanh_c, 0.5, None, ALU.mult).then_inc(vectors_put, 1)
                for k in range(1, KT):
                    dve.wait_ge(x_squared, k + 1)
                    if k > 1:
                        dve.wait_ge(squares_added, k - 1)
                    nc.vector.tensor_tensor(squares, squares, square_of(k), ALU.add).then_inc(squares_added, 1)
                dve.wait_ge(pro_sums, 1)
                norm_dve(dve, own, settle, pro_norm)
                dve.wait_ge(consts_in, 16 * CONSTS)
                for cnd in range(2):
                    own(nc.vector.tensor_copy(mods[:, :, :, cnd], bmod_sb))
                settle()
                dve.wait_ge(wmod_used, KT)
                nc.vector.tensor_copy(modrow, psum[:, 0, :]).then_inc(modrow_ready, 1)
                dve.wait_ge(modT_ready, 1)
                src = psum[:, 1, :].rearrange("p (j q m) -> p q j m", j=4, q=4)
                for cnd in range(2):
                    dst = mods[:, 0, 0:16, cnd].rearrange("p (q j) -> p q j", q=4)
                    own(nc.vector.tensor_tensor(dst, src[:, :, :, cnd], dst, ALU.add))
                settle()
                for cnd in range(2):
                    own(nc.vector.scalar_tensor_tensor(mods[:, 0, 8:16, cnd], mods[:, 0, 8:16, cnd], 1.0,
                                                       layer_g[:, 0], ALU.add, ALU.mult))

        names = ["layer_in", "w_loaded0", "w_loaded1", "hi_ready", "lo_ready", "tile_done", "set_free0",
                 "set_free1", "ones_ready", "sums_ready", "diag_ready", "rstd_ready", "scaled", "h_hi_ready",
                 "shifted", "h_even", "h_odd", "mod_ready", "x_saved", "tanh_ready", "av_turned", "av_natural",
                 "av_normal", "mixed", "mix_read", "ya_ready", "cv_turned", "cv_natural", "dv_turned",
                 "dv_natural", "swap_ready", "cos_ready", "rope_ready", "c_out", "v_out", "k_out", "rope_in",
                 "band_in", "cache0_in", "cache1_in", "bias_ready", "scores_ready", "biased", "expd", "normed",
                 "turned", "copied", "values_ready", "gated", "y_hi_ready", "y_split", "y_last", "x_loaded0",
                 "x_loaded1", "x_sq", "sq_added", "norm_step", "last_chunk", "x_chunk", "dve_step", "pool_step",
                 "mix_in", "sink_put", "bc_used", "v1_turned", "v1_natural", "chunk0_put", "chunk1_put",
                 "zeros_put", "rstd_copied", "mod_in0", "mod_in1", "mod_used", "mod_sum", "mod_copied",
                 "mod_turned", "mod_read", "part_step", "bias_in0", "bias_in1", "bias_in2", "bias_in3",
                 "bias_in4"]
        S = {n: sem(n) for n in names}
        nums = [S[n].num for n in names]
        layer_sems = range(min(nums), max(nums) + 1)
        assert len(layer_sems) == len(names)
        (layer_in, w_loaded0, w_loaded1, hi_ready, lo_ready, tile_done, set_free0, set_free1, ones_ready,
         sums_ready, diag_ready, rstd_ready, scaled, h_hi_ready, shifted, h_even, h_odd, mod_ready, x_saved,
         tanh_ready, av_turned, av_natural, av_normal, mixed, mix_read, ya_ready, cv_turned, cv_natural,
         dv_turned, dv_natural, swap_ready, cos_ready, rope_ready, c_out, v_out, k_out, rope_in, band_in,
         cache0_in, cache1_in, bias_ready, scores_ready, biased, expd, normed, turned, copied, values_ready,
         gated, y_hi_ready, y_split, y_last, x_loaded0, x_loaded1, x_sq, sq_added, norm_step, last_chunk,
         x_chunk, dve_step, pool_step, mix_in, sink_put, bc_used, v1_turned, v1_natural, chunk0_put, chunk1_put,
         zeros_put, rstd_copied, mod_in0, mod_in1, mod_used, mod_sum, mod_copied, mod_turned, mod_read,
         part_step, bias_in0, bias_in1, bias_in2, bias_in3, bias_in4) = [S[n] for n in names]
        w_loaded = (w_loaded0, w_loaded1)
        layer_norm = (diag_ready, rstd_ready)
        set_free = (set_free0, set_free1)
        bias_in = (bias_in0, bias_in1, bias_in2, bias_in3, bias_in4)
        x_loaded = (x_loaded0, x_loaded1)

        def pieces():
            return [(slice(0, 2), slice(0, CH), 0), (slice(2, 3), slice(0, DEC_SEQ - 2 * CH), 0),
                    (slice(2, 3), slice(DEC_SEQ - 2 * CH, CH), 1)]

        PARTS = ((LAT, 0), (CTX, 1))

        def c_keys(i):
            return [(i + d, at) for d, at in ((-1, 0), (0, P), (1, 3 * P)) if 0 <= i + d < LT]

        def base(u):
            return P if (UNITS[u][0] == "C" and UNITS[u][1] == 0) else 0

        def grid(ap):
            return ap[:, LAT].rearrange("p (r c) -> p r c", c=GRID_W)

        def queries(u):
            mixer, i, t, r = UNITS[u]
            half = slice(64 * r, 64 * r + 64)
            return (qC if mixer == "C" else qD)(t)[half, i * P:(i + 1) * P]

        def score_pieces(u):
            mixer, i, t, r = UNITS[u]
            half = slice(64 * r, 64 * r + 64)
            k = kC if mixer == "C" else kD(t)
            if i == LT:
                return [(k[half, CTX], 0, P)]
            if mixer == "C":
                off = base(u)
                return ([(k[half, j * P:(j + 1) * P], at - off, P) for j, at in c_keys(i)]
                        + [(ck_c[half, :], 2 * P - off, P)])
            row, col = d_keys(i)
            return [(ck_d[half, t, :], 0, P), (grid(k[half])[:, row:row + KR, col:col + KC], P, KR * KC)]

        def unit_width(u):
            return sum(w for _, _, w in score_pieces(u))

        def unit_values(u):
            mixer, i, t, r = UNITS[u]
            d = slice(64 * r, 64 * r + 64)
            if mixer == "C":
                if i == LT:
                    return [vC[:, LT, d]]
                off = base(u)
                at = {a - off: vC[:, j, d] for j, a in c_keys(i)} | {2 * P - off: cv_c[:, d]}
                return [at[x] for x in sorted(at)]
            if i == LT:
                return [vD[:, V_CTX, d]]
            rg, cg = divmod(i, N_CG)
            first = d_keys(i)[0] // BLK_R
            return [vD[:, V_CACHE, d]] + [vD[:, cg * N_BLK + first + b, d] for b in range(KR // BLK_R)]

        BLOCKS = [len(unit_values(u)) for u in range(NU)]

        SCORE_BANKS, BANK_T, TURN_BANKS = 4, 4, 2
        BANK_O, BANK_V = 6, 7
        LAYER_IN = 5

        def put_chunk(q, src, dst):
            col = d_keys(q)[1]
            return nc.gpsimd.tensor_copy(dst.rearrange("p (r c) -> p r c", c=KC), grid(src)[:, :, col:col + KC])

        CHUNK_W = N_BLK * P
        chunk0 = [probT[:, 0, :], probT[:, 1, :], flat_prob[:, 0:CHUNK_W], flat_prob[:, CHUNK_W:2 * CHUNK_W]]
        chunk1 = w_raw[:, 1].rearrange("p k n -> p (k n)")[:, 4 * P:4 * P + CHUNK_W]

        MOD_TILE, MOD_ROWS, THIRDS = 9, 2, 3
        NEXT = DEPTH - 1
        assert NEXT == 1
        mod_in = (mod_in0, mod_in1)
        mod_rows = (slots[:, 8, 0:D_MODEL], slots[:, 9, 0:D_MODEL])
        mod_part = (slots[:, 7, 0:D_MODEL], slots[:, 10, 0:D_MODEL])
        mod_row = flat_prob[:, 2 * CHUNK_W:3 * CHUNK_W]
        MOD_STEPS = THIRDS * KT // MOD_ROWS
        SUM_TILES, TURN_TILES = (13, 17, 21), (15, 19, 23)

        Y_SPLIT = {6: 0, 11: 1, 16: 2, 21: 3, GROUP_U + 8: 6, 2 * GROUP_U + 11: 4, 3 * GROUP_U + 8: 5}
        V1_STEPS = {GROUP_U + 10 + 4 * q: q for q in range(N_CG + 1)}
        W29_STEP = 3 * GROUP_U + 4
        Y_ORDER = list(Y_SPLIT.values()) + [7]

        with nc.Fori(0, DEPTH) as layer:
          with nc.Block() as block:

            @block.sync
            def _(sp):
                def load_weights(n):
                    sp.dma_start(w_raw[:, n % 2], w_tiles[layer, n]).then_inc(w_loaded[n % 2], 16)

                load_weights(0)
                load_weights(1)
                sp.dma_start(conv_w[:, :, :], w_conv[layer]).then_inc(layer_in, 16)
                sp.dma_start(sinks[:, :], sink[layer]).then_inc(layer_in, 16)
                sp.dma_start(ck_c[:, :], cckT[layer]).then_inc(layer_in, 16)
                sp.dma_start(cv_c[:, :], ccv[layer]).then_inc(layer_in, 16)
                sp.dma_start(ck_d[:, :, :], cdkT[layer]).then_inc(layer_in, 16)
                for k in range(KT):
                    sp.dma_start(x_kept[:, k], xy[:, k]).then_inc(x_saved, 16)
                sp.dma_start(wsT, w_sT[layer]).then_inc(mix_in, 16)
                sp.dma_start(bs, b_s[layer]).then_inc(mix_in, 16)
                sp.dma_start(flat_table[:, 0:2 * DEC_SEQ], rope_c).then_inc(rope_in, 16)

                def weights(lo, hi):
                    with sp.Fori(lo // 2, hi // 2) as pair:
                        for p in range(2):
                            sp.wait_ge(lo_ready, 2 * pair + p - 1)
                            sp.dma_start(w_raw[:, p], w_tiles[layer, 2 * pair + p]).then_inc(w_loaded[p], 16)

                def mod_loads(step):
                    for g in range(MOD_ROWS * step, MOD_ROWS * (step + 1)):
                        j, k = divmod(g, KT)
                        if g >= 2:
                            sp.wait_ge(mod_used, g - 1)
                        rows = (w_mod[layer, k * P:(k + 1) * P, MOD_W:] if j == 0
                                else w_mod[NEXT, k * P:(k + 1) * P, (j - 1) * D_MODEL:j * D_MODEL])
                        sp.dma_start(mod_rows[g % 2], rows).then_inc(mod_in[g % 2], 16)

                weights(2, MOD_TILE + 1)
                sp.wait_ge(mixed, 6)
                sp.dma_start(vD[:, V_CACHE], cdv[layer, :, 0, :]).then_inc(cache0_in, 16)
                for n in range(MOD_TILE + 1, 24):
                    sp.wait_ge(lo_ready, n - 1)
                    load_weights(n)
                    step = n - MOD_TILE - 2
                    if 0 <= step < MOD_STEPS // THIRDS:
                        mod_loads(step)
                    elif MOD_STEPS // THIRDS <= step < MOD_STEPS:
                        with sp.If(layer < DEPTH - 1):
                            mod_loads(step)
                weights(24, 28)

                def load_table(m):
                    if m >= TABLES:
                        sp.wait_ge(biased, READERS[m - TABLES][-1] + 1)
                    sp.dma_start(table[:, m % TABLES, P:S_W], rpb[layer, m]).then_inc(bias_in[m % TABLES], 16)

                sp.wait_ge(rope_ready, 3)
                for m in range(TABLES):
                    load_table(m)
                sp.wait_ge(lo_ready, N_IN - 1)
                load_weights(N_IN)
                sp.wait_ge(lo_ready, N_IN)
                sp.dma_start(band, band_c).then_inc(band_in, 16)
                steps = [(READERS[m - TABLES][-1], "table", m) for m in range(TABLES, N_TABLES)]
                steps += [(GROUP_U + 3, "cache", 1), (3 * GROUP_U, "weights", 1)]
                for _, what, m in sorted(steps):
                    if what == "table":
                        load_table(m)
                    elif what == "cache":
                        sp.wait_ge(values_ready, GROUP_P)
                        sp.dma_start(vD[:, V_CACHE], cdv[layer, :, 1, :]).then_inc(cache1_in, 16)
                    else:
                        sp.wait_ge(biased, 3 * GROUP_U)
                        sp.wait_ge(v1_turned, N_CG)
                        load_weights(N_IN + 1)
                for n in (N_IN + 2, N_IN + 3):
                    sp.wait_ge(lo_ready, n - 1)
                    load_weights(n)
                sp.wait_ge(biased, NU)
                sp.wait_ge(x_saved, 16 * KT)
                for f in range(KT):
                    n = N_IN + f
                    if f >= 4:
                        sp.wait_ge(lo_ready, n - 1)
                        load_weights(n)
                    if f >= 2:
                        tile_read(sp, n - 2)
                    sp.dma_start(x_new[:, f % 2], x_kept[:, f]).then_inc(x_loaded[f % 2], 16)
                for done in (c_out, v_out, k_out):
                    sp.wait_ge(done, 32)

            @block.gpsimd
            def _(pool):
                def low_halves(lo, hi):
                    with pool.Fori(lo // 2, hi // 2) as pair:
                        for p in range(2):
                            pool.wait_ge(hi_ready, 2 * pair + p + 1)
                            nc.gpsimd.tensor_tensor(w_lo[:, p], w_raw[:, p], w_hi[:, p], ALU.subtract
                                                    ).then_inc(lo_ready, 1)

                def low_half(n):
                    pool.wait_ge(hi_ready, n + 1)
                    nc.gpsimd.tensor_tensor(w_lo[:, n % 2], w_raw[:, n % 2], w_hi[:, n % 2], ALU.subtract
                                            ).then_inc(lo_ready, 1)

                low_half(0)
                low_half(1)
                for k in range(1, KT, 2):
                    pool.wait_ge(shifted, k // 2 + 1)
                    pool.wait_ge(h_hi_ready, k + 1)
                    nc.gpsimd.tensor_tensor(h_lo[:, k], slots[:, k], h_hi[:, k], ALU.subtract).then_inc(h_odd, 1)
                low_halves(2, 18)
                for t in range(3):
                    low_half(NO["ck", 0] + t)
                    pool.wait_ge(swap_ready, t + 1)
                    if t == 0:
                        pool.wait_ge(rope_in, 16)
                    raw = slots[:, t, LAT]
                    nc.gpsimd.tensor_tensor(raw, raw, cos_t, ALU.mult).then_inc(cos_ready, 1)
                low_half(21)
                low_halves(22, 26)
                tile_read(pool, NO["dv", 0])
                for q in range(N_CG):
                    put_chunk(q, dv_kept[0], chunk0[q]).then_inc(chunk0_put, 1)
                low_halves(26, 28)
                step = [0]

                def own(ins):
                    ins.then_inc(pool_step, 1)
                    step[0] += 1

                def settle():
                    pool.wait_ge(pool_step, step[0])

                pool.wait_ge(rope_ready, 3)
                nc.gpsimd.memset(table[:, :, 0:P], 0.0).then_inc(zeros_put, 1)

                def make_table(m):
                    tab = table[:, m % TABLES, P:S_W].rearrange("p (r c) -> p r c", c=KC)
                    rg, cls = m // (2 * N_CLASS) % 2, m // 2 % N_CLASS
                    rows = row_mask[:, rg, :].rearrange("p (r o) -> p r o", o=1).broadcast_to([P, KR, KC])
                    cols = col_mask[:, cls:cls + 1, :].broadcast_to([P, KR, KC])
                    pool.wait_ge(bias_in[m % TABLES], 16 * (m // TABLES + 1))
                    own(nc.gpsimd.tensor_tensor(tab, rows, tab, ALU.subtract))
                    settle()
                    nc.gpsimd.tensor_tensor(tab, tab, cols, ALU.add).then_inc(bias_ready, 1)

                def y_low(k):
                    pool.wait_ge(y_hi_ready, Y_ORDER.index(k) + 1)
                    nc.gpsimd.tensor_tensor(h_lo[:, k], xy[:, k], h_hi[:, k], ALU.subtract).then_inc(y_split, 1)

                def chunk_1(q):
                    if q >= 1:
                        pool.wait_ge(v1_turned, q)
                    put_chunk(q, dv_kept[1], chunk1).then_inc(chunk1_put, 1)

                for m in range(TABLES):
                    make_table(m)
                low_half(N_IN)
                steps = [(READERS[m - TABLES][-1], make_table, m) for m in range(TABLES, N_TABLES)]
                steps += [(s - 3, chunk_1, q) for s, q in V1_STEPS.items() if q < N_CG]
                steps += [(s, y_low, k) for s, k in Y_SPLIT.items()] + [(W29_STEP, low_half, N_IN + 1)]
                for _, work, m in sorted(steps, key=lambda x: (x[0], x[2])):
                    work(m)
                low_halves(N_IN + 2, N_TILES)

            @block.scalar
            def _(act):
                def high_half(n):
                    act.wait_ge(w_loaded[n % 2], 16 * (n // 2 + 1))
                    if n >= 2:
                        act.wait_ge(tile_done, n - 1)
                    nc.scalar.copy(w_hi[:, n % 2], w_raw[:, n % 2]).then_inc(hi_ready, 1)

                nc.scalar.copy(mod[:, :, :], mods[:, layer]).then_inc(mod_ready, 1)
                for c in range(NCH):
                    with act.If(layer > 0):
                        act.wait_ge(rstd_ready, 3 * (c + 1))
                    nc.scalar.copy(rstd_all[:, c * CH:(c + 1) * CH], psum[:, RSTD_BANK + c, 0:CH]
                                   ).then_inc(rstd_copied, 1)
                high_half(0)
                act.wait_ge(mod_ready, 1)
                for k in range(KT):
                    act.wait_ge(scaled, k + 1)
                    for cols, c in PARTS:
                        last = nc.scalar.activation(h_hi[:, k, cols], slots[:, k, cols], ACT.Identity,
                                                    bias=mod[:, k, c:c + 1])
                    last.then_inc(h_hi_ready, 1)
                    if k == 0:
                        high_half(1)
                    if k % 2:
                        for cols, c in PARTS:
                            last = nc.scalar.activation(slots[:, k, cols], slots[:, k, cols], ACT.Identity,
                                                        bias=mod[:, k, c:c + 1])
                        last.then_inc(shifted, 1)
                naturals = {"av": (av_turned, av_natural), "cv": (cv_turned, cv_natural)}

                def copy_chunk(q, bank, signal):
                    dst = vD[:, q * N_BLK:(q + 1) * N_BLK, :] if q < N_CG else vD[:, V_CTX:V_CTX + 1, :]
                    src = psum[:, bank, 0:N_BLK * P if q < N_CG else P].rearrange("p (b d) -> p b d", d=P)
                    nc.scalar.copy(dst, src).then_inc(signal, 1)

                def copy_turned(part, dst_of, count):
                    sem_in, sem_out = naturals[part]
                    for q in range(count):
                        act.wait_ge(sem_in, q + 1)
                        nc.scalar.copy(dst_of(q), psum[:, BANK_A + q % 2, 0:CH].rearrange("p (t d) -> p t d", t=3)
                                       ).then_inc(sem_out, 1)

                two_tiles = lambda v: (lambda q: v[:, 3 * (q % 3):3 * (q % 3) + 3, P * (q // 3):P * (q // 3) + P])
                n_tanh = 0
                gates = [n for n, x in enumerate(TILES) if x[0][1] == "z"]
                for n, (part, t) in enumerate(TILES):
                    if n != 1:
                        high_half(n + 1 if n else 2)
                    if part[1] == "z":
                        act.wait_ge(tile_done, n + 1)
                        before = gates[n_tanh - 2] if part != "dz" else NO[("cz", 0) if t == 0 else ("dz", 0)]
                        if n_tanh >= 2:
                            tile_read(act, before)
                        nc.scalar.activation(chunks(kD(1 - n_tanh % 2) if part != "dz" else kD(1)),
                                             tile_psum(n), ACT.Tanh, scale=0.5).then_inc(tanh_ready, 1)
                        n_tanh += 1
                    elif part in COPIED:
                        dst = {"av": qD(t), "bc": kC, "cq": qC(t), "ck": kC, "cv": kD(0), "dv": dv_kept[t],
                               "dk": kD(t), "dq": qD(t)}[part]
                        act.wait_ge(tile_done, n + 1)
                        if (part, t) == ("bc", 1) or part == "ck":
                            act.wait_ge(bc_used, 1 + (part == "ck"))
                        if part == "cv":
                            tile_read(act, NO["cz", 1])
                        if part == "cq" and t == 0:
                            act.wait_ge(bc_used, 2)
                        if part == "dk":
                            tile_read(act, NO["dz", 1])
                            act.wait_ge(c_out, 32)
                            act.wait_ge(cv_turned, 3)
                        if part == "dq":
                            act.wait_ge(dv_turned, N_CG + 1)
                            act.wait_ge(v_out, 32)
                        scale = -SCALE if part[1] == "q" else 1.0
                        if part == "dq":
                            for lo, hi in ((0, 6), (6, 8), (8, 12), (12, 16)):
                                rg, c = lo // QR, lo * GRID_W // CH
                                src = tile_psum(n)[:, c, lo * GRID_W - c * CH:hi * GRID_W - c * CH]
                                to = dst[:, rg * QR * GRID_W:(rg + 1) * QR * GRID_W].rearrange(
                                    "p (g r c) -> p g r c", g=N_CG, r=QR)[:, :, lo - rg * QR:hi - rg * QR, :]
                                nc.scalar.mul(to.rearrange("p g r c -> p r g c"),
                                              src.rearrange("p (r g c) -> p r g c", g=N_CG, c=QC), scale)
                            nc.scalar.mul(dst[:, CTX], tile_psum(n)[:, 2, DEC_SEQ - 2 * CH:CH], scale
                                          ).then_inc(set_free[n % 2], 1)
                            continue
                        nc.scalar.mul(chunks(dst), tile_psum(n), scale).then_inc(set_free[n % 2], 1)
                        if part in ("ck", "cv", "dv", "dk"):
                            tile_read(act, n)
                            out = {"ck": sckT[layer], "cv": scvT[layer], "dv": sdvT[layer, t],
                                   "dk": sdkT[layer, t]}[part]
                            done = {"dv": v_out, "dk": k_out}.get(part, c_out)
                            act.dma_start(out, dst[:, CTX]).then_inc(done, 16)
                    if (part, t) == ("au", 0):
                        copy_turned("av", two_tiles(vA), 6)
                    if (part, t) == ("dz", 1):
                        copy_turned("cv", lambda q: vC[:, 3 * q:3 * q + 3, :], 3)
                    if (part, t) == ("dk", 1):
                        for q in range(N_CG + 1):
                            act.wait_ge(dv_turned, q + 1)
                            copy_chunk(q, BANK_O + q % 2, dv_natural)

                def exp_unit(u):
                    width = unit_width(u)
                    act.wait_ge(biased, u + 1)
                    if UNITS[u][0] == "C":
                        act.wait_ge(sink_put, u - GROUP_U + 1)
                        width += 1
                    row = prob[:, u % PROBS, 0:width]
                    nc.scalar.activation(row, row, ACT.Exp, scale=-1.0, bias=stat[:, u % 4, 0:1],
                                         accum_out=stat[:, u % 4, 1:2]).then_inc(expd, 1)

                def copy_probs(u):
                    n = BLOCKS[u]
                    act.wait_ge(turned, u + 1)
                    if u >= 2:
                        act.wait_ge(values_ready, u // 2)
                    nc.scalar.copy(probT[:, u % 2, 0:n * P], psum[:, BANK_T + u % TURN_BANKS, 0:n * P]
                                   ).then_inc(copied, 1)

                def y_high(k):
                    act.wait_ge(tile_done, N_IN)
                    if k < 2:
                        act.wait_ge(ya_ready, 6)
                    elif k < 4:
                        act.wait_ge(bc_used, k - 1)
                    else:
                        act.wait_ge(gated, GROUP_P * {6: 1, 4: 2, 5: 3, 7: 4}[k])
                    nc.scalar.copy(h_hi[:, k], xy[:, k]).then_inc(y_hi_ready, 1)

                for pair in range(NU // 2 + 1):
                    if 2 * pair < NU:
                        exp_unit(2 * pair)
                        exp_unit(2 * pair + 1)
                    if pair >= 1:
                        copy_probs(2 * pair - 2)
                        copy_probs(2 * pair - 1)
                    for s in (2 * pair, 2 * pair + 1):
                        if s in V1_STEPS:
                            q = V1_STEPS[s]
                            act.wait_ge(v1_turned, q + 1)
                            act.wait_ge(values_ready, GROUP_P)
                            copy_chunk(q, BANK_V, v1_natural)
                        if s in Y_SPLIT:
                            y_high(Y_SPLIT[s])
                        if s == W29_STEP:
                            high_half(N_IN + 1)
                y_high(7)
                for f in range(KT):
                    if f + 2 < KT:
                        high_half(N_IN + f + 2)
                    if f == KT - 1:
                        act.wait_ge(sq_added, f - 1)
                        for c in range(NCH):
                            act.wait_ge(x_chunk, c + 1)
                            cols = slice(c * CH, (c + 1) * CH)
                            nc.scalar.activation(square[:, cols], xy[:, f, cols], ACT.Square).then_inc(x_sq, 1)
                        continue
                    tile_read(act, N_IN + f)
                    dst = squares if f == 0 else square
                    if f >= 2:
                        act.wait_ge(sq_added, f - 1)
                    nc.scalar.activation(dst, xy[:, f], ACT.Square).then_inc(x_sq, 1)

            @block.tensor
            def _(pe):
                with pe.If(layer > 0):
                    norm_spread(pe, layer_norm)

                def products(p, k, order, chunks_=range(NCH)):
                    for w, h in ((w_hi, h_hi), (w_hi, h_lo), (w_lo, h_hi)):
                        for c in chunks_:
                            last = nc.tensor.matmul(psum[:, 3 * p + c, 0:CH], w[:, p, k, :],
                                                    h[:, k, c * CH:(c + 1) * CH],
                                                    start=(k == order[0] and w is w_hi and h is h_hi),
                                                    stop=(k == order[-1] and w is w_lo))
                    return last

                def project_pair(pair, order=range(KT), until=None):
                    for p in range(2):
                        pe.wait_ge(lo_ready, 2 * pair + p + 1)
                        pe.wait_ge(set_free[p], pair)
                        for k in order:
                            if p == 0 and until:
                                until(k)
                            last = products(p, k, order)
                        last.then_inc(tile_done, 1)

                def project_first():
                    pe.wait_ge(rstd_copied, NCH)
                    together = 5
                    for k in range(together):
                        pe.wait_ge(h_odd if k % 2 else h_even, k // 2 + 1)
                        for p in range(2):
                            if k == 0:
                                pe.wait_ge(lo_ready, p + 1)
                            products(p, k, range(KT))
                    for p in range(2):
                        for k in range(together, KT):
                            if p == 0:
                                pe.wait_ge(h_odd if k % 2 else h_even, k // 2 + 1)
                            last = products(p, k, range(KT))
                        last.then_inc(tile_done, 1)

                def sums_of(c):
                    pe.wait_ge(ones_ready, 1)
                    pe.wait_ge(sq_added, KT - 1 + c)
                    norm_sums(range(3 * c, 3 * c + 3)).then_inc(sums_ready, 1)

                def project_last():
                    pair = N_TILES // 2 - 1
                    for p in range(2):
                        pe.wait_ge(lo_ready, 2 * pair + p + 1)
                        pe.wait_ge(set_free[p], pair)
                        for chunks_ in (range(NCH),) if p == 0 else [(c,) for c in range(NCH)]:
                            for k in Y_ORDER:
                                last = products(p, k, Y_ORDER, chunks_)
                            last.then_inc(tile_done if p == 0 else last_chunk, 1)
                            if p == 1 and chunks_[0] == NCH - 1:
                                sums_of(chunks_[0] - 2)
                                sums_of(chunks_[0] - 1)
                    sums_of(NCH - 1)

                def project(lo, hi, order=range(KT)):
                    with pe.Fori(lo // 2, hi // 2) as pair:
                        project_pair(pair, order=order)

                def turn(src_of, count, tile, sem_out, sem_read):
                    tile_read(pe, tile - 1)
                    tile_read(pe, tile)
                    for q in range(count):
                        if q >= 2:
                            pe.wait_ge(sem_read, q - 1)
                        for i in range(3):
                            t = 3 * (q % 3) + i
                            last = nc.tensor.transpose(psum[:, BANK_A + q % 2, i * P:(i + 1) * P],
                                                       src_of(q // 3)[:, t * P:(t + 1) * P], ident[:, :])
                        last.then_inc(sem_out, 1)

                def turn_values(src, bank, signal):
                    for b in range(src.shape[-1] // P):
                        last = nc.tensor.transpose(psum[:, bank, b * P:(b + 1) * P], src[:, b * P:(b + 1) * P],
                                                   ident[:, :])
                    last.then_inc(signal, 1)

                def mod_sums(j):
                    pe.wait_ge(mod_used, KT * (j + 1))
                    if j > 0:
                        pe.wait_ge(mod_copied, j)
                    for q in range(4):
                        c, half = divmod(q, 2)
                        last = nc.tensor.matmul(psum[32 * q:32 * q + 32, BANK_V, :], ones_m[:, :],
                                                mod_part[c][:, half * 512:(half + 1) * 512],
                                                start=True, stop=True, skip_group_check=True)
                    last.then_inc(mod_sum, 1)

                def mod_turn(j):
                    pe.wait_ge(mod_copied, j + 1)
                    if j > 0:
                        pe.wait_ge(mod_read, j)
                    for f in range(4):
                        last = nc.tensor.transpose(psum[:, BANK_O, f * P:(f + 1) * P], mod_row[:, f * P:(f + 1) * P],
                                                   ident[:, :])
                    last.then_inc(mod_turned, 1)

                project_first()
                project(2, 4)
                turn(qD, 6, NO["av", 1], av_turned, av_natural)
                project(4, 8)
                pe.wait_ge(av_normal, 1)
                pe.wait_ge(mix_in, 32)
                for q in range(6):
                    j = q // 3
                    if q >= 2:
                        pe.wait_ge(mix_read, q - 1)
                    for i in range(3):
                        t = 3 * (q % 3) + i
                        for r in range(2):
                            last = nc.tensor.matmul(psum[64 * r:64 * r + 64, BANK_A + q % 2, i * P:(i + 1) * P],
                                                    vA[:, t, (2 * j + r) * 64:(2 * j + r + 1) * 64],
                                                    wsT[:, 2 * j + r, :], start=True, stop=True,
                                                    skip_group_check=True)
                    last.then_inc(mixed, 1)
                project(8, 14)
                pe.wait_ge(mix_read, 6)
                mod_sums(0)
                project(14, 16)
                mod_turn(0)
                project(16, 18)
                with pe.If(layer < DEPTH - 1):
                    mod_sums(1)
                project(18, 20)
                with pe.If(layer < DEPTH - 1):
                    mod_turn(1)
                project(20, 22)
                with pe.If(layer < DEPTH - 1):
                    mod_sums(2)
                    pe.wait_ge(mod_read, 2)
                    pe.wait_ge(mod_copied, 3)
                pe.wait_ge(mod_read, 1)
                turn(lambda j: kD(0), 3, NO["cv", 0], cv_turned, cv_natural)
                project(22, 24)
                pe.wait_ge(cv_natural, 3)
                with pe.If(layer < DEPTH - 1):
                    mod_turn(2)
                project(24, 26)
                with pe.If(layer < DEPTH - 1):
                    pe.wait_ge(mod_read, 3)
                tile_read(pe, NO["dv", 0])
                for q in range(N_CG + 1):
                    if q >= 2:
                        pe.wait_ge(dv_natural, q - 1)
                    if q < N_CG:
                        pe.wait_ge(chunk0_put, q + 1)
                    turn_values(chunk0[q] if q < N_CG else dv_kept[0][:, CTX], BANK_O + q % 2, dv_turned)
                project(26, 28)

                pe.wait_ge(set_free0, N_IN // 2)
                pe.wait_ge(set_free1, N_IN // 2)
                pe.wait_ge(dv_natural, N_CG + 1)
                pe.wait_ge(rope_ready, 3)
                pe.wait_ge(layer_in, 16 * LAYER_IN)

                def scores(u):
                    if u >= SCORE_BANKS:
                        pe.wait_ge(biased, u - SCORE_BANKS + 2)
                    parts = [score_pieces(u), score_pieces(u + 1)]
                    for b in range(len(parts[0])):
                        for r in range(2):
                            src, at, width = parts[r][b]
                            last = nc.tensor.matmul(psum[:, (u + r) % SCORE_BANKS, at:at + width], queries(u + r),
                                                    src, start=True, stop=True, skip_group_check=True)
                            if b == len(parts[0]) - 1:
                                last.then_inc(scores_ready, 1)

                def turn_probs(u):
                    pe.wait_ge(normed, u + 1)
                    if u >= TURN_BANKS:
                        pe.wait_ge(copied, u - TURN_BANKS + 1)
                    for b in range(BLOCKS[u]):
                        last = nc.tensor.transpose(psum[:, BANK_T + u % TURN_BANKS, b * P:(b + 1) * P],
                                                   prob[:, u % PROBS, b * P:(b + 1) * P], ident[:, :])
                    last.then_inc(turned, 1)

                def values(pair):
                    u = 2 * pair
                    pe.wait_ge(copied, u + 2)
                    if pair >= 1:
                        pe.wait_ge(gated, pair)
                    if pair == 0:
                        pe.wait_ge(cache0_in, 16)
                    if pair == 3 * GROUP_P:
                        pe.wait_ge(cache1_in, 16)
                        pe.wait_ge(v1_natural, N_CG + 1)
                    for b in range(BLOCKS[u]):
                        for r in range(2):
                            last = nc.tensor.matmul(psum[64 * r:64 * r + 64, BANK_O, 0:P], unit_values(u + r)[b],
                                                    probT[:, r, b * P:(b + 1) * P], start=(b == 0),
                                                    stop=(b == BLOCKS[u] - 1), skip_group_check=True)
                    last.then_inc(values_ready, 1)

                for s in range(NU + 4):
                    if s < NU and s % 2 == 0:
                        scores(s)
                    if 2 <= s < NU + 2:
                        turn_probs(s - 2)
                    if s >= 5 and s % 2:
                        values((s - 5) // 2)
                    if s in V1_STEPS:
                        q = V1_STEPS[s]
                        if q >= 1:
                            pe.wait_ge(v1_natural, q)
                        if q < N_CG:
                            pe.wait_ge(chunk1_put, q + 1)
                        turn_values(chunk1 if q < N_CG else dv_kept[1][:, CTX], BANK_V, v1_turned)
                def y_there(k):
                    if k == Y_ORDER[0]:
                        pe.wait_ge(y_split, KT - 1)
                    if k == Y_ORDER[-1]:
                        pe.wait_ge(y_last, 1)

                project_pair(N_IN // 2, order=Y_ORDER, until=y_there)
                project(N_IN + 2, N_TILES - 2, order=Y_ORDER)
                project_last()

            @block.vector
            def _(dve):
                told, pending = {}, {}

                def tell(ins, signal=dve_step, count=None):
                    ins.then_inc(signal, 1)
                    told[signal.name] = count or told.get(signal.name, 0) + 1
                    pending[signal.name] = (signal, told[signal.name])

                def settle():
                    for signal, count in pending.values():
                        dve.wait_ge(signal, count)
                    pending.clear()

                with dve.If(layer > 0):
                    norm_dve(dve, lambda ins: tell(ins, norm_step), settle, layer_norm)
                dve.wait_ge(rstd_copied, NCH)
                dve.wait_ge(mod_ready, 1)

                def low(k):
                    dve.wait_ge(h_hi_ready, k + 1)
                    for cols, c in PARTS:
                        last = nc.vector.scalar_tensor_tensor(h_lo[:, k, cols], slots[:, k, cols],
                                                              mod[:, k, c:c + 1], h_hi[:, k, cols],
                                                              ALU.add, ALU.subtract)
                    last.then_inc(h_even, 1)

                for k in range(KT):
                    for cols, c in PARTS:
                        ins = nc.vector.scalar_tensor_tensor(slots[:, k, cols], xy[:, k, cols],
                                                             mod[:, KT + k, c:c + 1], rstd_all[:, cols],
                                                             ALU.mult, ALU.mult)
                        tell(ins, scaled if c == 1 else dve_step)
                    if k % 2:
                        low(k - 1)
                settle()

                def y_of(part, t):
                    return xy[:, 2 * "abcd".index(part[0]) + t]

                def multiply(step):
                    for g in range(MOD_ROWS * step, MOD_ROWS * (step + 1)):
                        k = g % KT
                        dve.wait_ge(mod_in[g % 2], 16 * (g // 2 + 1))
                        for c in range(2):
                            if k == 0:
                                ins = nc.vector.tensor_scalar(mod_part[c], mod_rows[g % 2], silu[:, k, c:c + 1],
                                                              None, ALU.mult)
                            else:
                                ins = nc.vector.scalar_tensor_tensor(mod_part[c], mod_rows[g % 2],
                                                                     silu[:, k, c:c + 1], mod_part[c],
                                                                     ALU.mult, ALU.add)
                            tell(ins, part_step if c == 0 else mod_used)
                        settle()

                def copy_third(j):
                    dve.wait_ge(mod_sum, j + 1)
                    nc.vector.tensor_copy(mod_row, psum[:, BANK_V, :]).then_inc(mod_copied, 1)

                def read_third(j):
                    dve.wait_ge(mod_turned, j + 1)
                    dst = mod[:, 2 * KT:, :] if j == 0 else mods[:, NEXT, (j - 1) * KT:j * KT, :]
                    sums = psum[:, BANK_O, :].rearrange("p (f q m) -> p q f m", f=4, q=4)
                    for c in range(2):
                        to = dst[:, :, c].rearrange("p (h f) -> p h f", h=2)
                        tell(nc.vector.tensor_tensor(to, sums[:, 2 * c:2 * c + 2, :, 0], to, ALU.add),
                             mod_read if c else part_step if j else dve_step)
                    settle()
                    if j == 2:
                        for c in range(2):
                            tell(nc.vector.scalar_tensor_tensor(dst[:, :, c], dst[:, :, c], 1.0, layer_g[:, NEXT],
                                                                ALU.add, ALU.mult), part_step)
                        settle()

                n_tanh = 0
                n_rope = 0
                for n, (part, t) in enumerate(TILES):
                    if n == SUM_TILES[2]:
                        settle()
                        with dve.If(layer < DEPTH - 1):
                            copy_third(2)
                    y = y_of(part, t)
                    free = set_free[n % 2]
                    if (part, t) == ("az", 0):
                        dve.wait_ge(x_saved, 16 * KT)
                    if part[1] == "z":
                        dve.wait_ge(tanh_ready, n_tanh + 1)
                        th = kD(1 - n_tanh % 2) if part != "dz" else kD(1)
                        tell(nc.vector.scalar_tensor_tensor(chunks(y), chunks(th), 1.0, tile_psum(n),
                                                                 ALU.add, ALU.mult), free, n // 2 + 1)
                        n_tanh += 1
                    elif part in ("au", "bb"):
                        dve.wait_ge(tile_done, n + 1)
                        settle()
                        tell(nc.vector.scalar_tensor_tensor(chunks(y), tile_psum(n), 0.5, chunks(y),
                                                                 ALU.mult, ALU.mult), free, n // 2 + 1)
                    elif part == "bh":
                        dve.wait_ge(tile_done, n + 1)
                        tile_read(dve, NO["bc", t])
                        tell(nc.vector.tensor_tensor(chunks(kC), tile_psum(n), chunks(kC), ALU.mult), free, n // 2 + 1)
                        settle()
                        if t == 0:
                            dve.wait_ge(layer_in, 16 * LAYER_IN)
                        s = qC(t)
                        tell(nc.vector.tensor_scalar(s, kC, conv_w[:, t, 1:2], None, ALU.mult))
                        settle()
                        for a, b in ((0, DEC_SEQ), (DEC_SEQ, T)):
                            tell(nc.vector.scalar_tensor_tensor(s[:, a + 1:b], kC[:, a:b - 1], conv_w[:, t, 0:1],
                                                               s[:, a + 1:b], ALU.mult, ALU.add))
                        settle()
                        for a, b in ((0, DEC_SEQ), (DEC_SEQ, T)):
                            tell(nc.vector.scalar_tensor_tensor(s[:, a:b - 1], kC[:, a + 1:b], conv_w[:, t, 2:3],
                                                               s[:, a:b - 1], ALU.mult, ALU.add))
                        settle()
                        tell(nc.vector.tensor_tensor(y, y, s, ALU.mult), bc_used)
                    elif part in ("cq", "ck"):
                        tile_read(dve, n)
                        raw = slots[:, n_rope, LAT]
                        if n_rope == 0:
                            dve.wait_ge(rope_in, 16)
                        else:
                            settle()
                        tell(nc.vector.stream_shuffle(swapped, raw, [(i + 16) % 32 for i in range(32)]), swap_ready)
                        settle()
                        tell(nc.vector.tensor_tensor(swapped, swapped, sin_t, ALU.mult))
                        settle()
                        dve.wait_ge(cos_ready, n_rope + 1)
                        tell(nc.vector.tensor_tensor(raw, raw, swapped, ALU.add), rope_ready)
                        n_rope += 1
                    if (part, t) == ("az", 1):
                        ss, rs = small[:, 4, :], small[:, 5, :]
                        dve.wait_ge(av_natural, 6)
                        for j in range(2):
                            sq = squares.rearrange("p (t d) -> p t d", t=TT)
                            vj = vA[:, :, j * P:(j + 1) * P]
                            tell(nc.vector.tensor_tensor(sq, vj, vj, ALU.mult))
                            settle()
                            tell(nc.vector.tensor_reduce(
                                ss.rearrange("p (t h) -> p t h", t=TT)[:, :, 2 * j:2 * j + 2],
                                squares.rearrange("p (t h d) -> p t h d", t=TT, h=2), AX_X, ALU.add))
                            settle()
                        tell(nc.vector.tensor_scalar(ss, ss, 1.0 / HEAD_DIM, EPS, ALU.mult, ALU.add))
                        settle()
                        rsqrt(tell, settle, rs, ss, small[:, 6, :], small[:, 7, :])
                        flat = vA[:, :, :].rearrange("p t (h d) -> p (t h) d", h=4)
                        tell(nc.vector.tensor_tensor(
                            flat, flat, rs.rearrange("p (n o) -> p n o", o=1).broadcast_to([P, 36, HEAD_DIM]),
                            ALU.mult), av_normal)
                    if (part, t) == ("bb", 0):
                        dve.wait_ge(mix_in, 32)
                        for q in range(6):
                            j, c = q // 3, q % 3
                            dve.wait_ge(mixed, q + 1)
                            tmp = flat_prob[:, (q % 2) * CH:(q % 2 + 1) * CH].rearrange("p (t n) -> p t n", t=3)
                            tell(nc.vector.tensor_tensor(
                                tmp, psum[:, BANK_A + q % 2, 0:CH].rearrange("p (t n) -> p t n", t=3),
                                bs[:, j:j + 1, :].broadcast_to([P, 3, P]), ALU.add), mix_read)
                            settle()
                            yq = xy[:, j, c * CH:(c + 1) * CH].rearrange("p (t n) -> p t n", t=3)
                            tell(nc.vector.tensor_tensor(yq, yq, tmp, ALU.mult), ya_ready)

                    step = n - MOD_TILE
                    if 0 <= step < MOD_STEPS:
                        settle()
                        if step < MOD_STEPS // THIRDS:
                            multiply(step)
                        else:
                            if n == SUM_TILES[0]:
                                copy_third(0)
                            if n == TURN_TILES[0]:
                                read_third(0)
                            with dve.If(layer < DEPTH - 1):
                                if n == SUM_TILES[1]:
                                    copy_third(1)
                                if n == TURN_TILES[1]:
                                    read_third(1)
                                multiply(step)
                    if n == TURN_TILES[2]:
                        settle()
                        with dve.If(layer < DEPTH - 1):
                            read_third(2)

                settle()
                tell(nc.vector.tensor_scalar(sinks[:, :], sinks[:, :], -1.0, None, ALU.mult))
                settle()

                def bias_unit(u):
                    mixer, i, t, r = UNITS[u]
                    width = unit_width(u)
                    row = prob[:, u % PROBS, :]
                    dve.wait_ge(scores_ready, u + 1)
                    if u >= PROBS:
                        dve.wait_ge(turned, u - PROBS + 1)
                    if mixer == "C":
                        if u == GROUP_U:
                            dve.wait_ge(band_in, 16)
                        at = 2 * P if i == LT else base(u)
                        bias = band[:, at:at + width]
                        first = sinks[:, 2 * t + r:2 * t + r + 1]
                        tell(nc.vector.tensor_copy(row[:, width:width + 1], first), sink_put)
                    else:
                        first = -NEG
                        if u == 0:
                            dve.wait_ge(zeros_put, 1)
                        if i < LT:
                            dve.wait_ge(bias_ready, bias_table(u) + 1)
                        bias = table[:, bias_table(u) % TABLES if i < LT else 0, 0:width]
                    nc.vector.tensor_tensor_reduce(out=row[:, 0:width], in0=psum[:, u % SCORE_BANKS, 0:width], in1=bias,
                                                   scale=1.0, scalar=first, op0=ALU.add, op1=ALU.min,
                                                   accum_out=stat[:, u % 4, 0:1]).then_inc(biased, 1)

                def norm_unit(u):
                    width = unit_width(u)
                    dve.wait_ge(expd, u + 1)
                    tell(nc.vector.reciprocal(stat[:, u % 4, 2:3], stat[:, u % 4, 1:2]))
                    settle()
                    row = prob[:, u % PROBS, 0:width]
                    nc.vector.tensor_scalar(row, row, stat[:, u % 4, 2:3], None, ALU.mult).then_inc(normed, 1)

                def gate_pair(pair):
                    mixer, i, t, _ = UNITS[2 * pair]
                    dve.wait_ge(values_ready, pair + 1)
                    y, out = xy[:, (4 if mixer == "C" else 6) + t], psum[:, BANK_O, 0:P]
                    if mixer == "D" and i < LT:
                        rg, cg = divmod(i, N_CG)
                        y = grid(y)[:, rg * QR:(rg + 1) * QR, cg * QC:(cg + 1) * QC]
                        out = out.rearrange("p (r c) -> p r c", c=QC)
                    else:
                        y = y[:, i * P:(i + 1) * P]
                    nc.vector.scalar_tensor_tensor(y, out, 0.5, y, ALU.mult, ALU.mult).then_inc(gated, 1)

                for pair in range(NU // 2 + 2):
                    if 2 * pair < NU:
                        bias_unit(2 * pair)
                        bias_unit(2 * pair + 1)
                        norm_unit(2 * pair)
                        norm_unit(2 * pair + 1)
                    if pair >= 2:
                        gate_pair(pair - 2)
                dve.wait_ge(y_hi_ready, KT)
                nc.vector.tensor_tensor(h_lo[:, 7], xy[:, 7], h_hi[:, 7], ALU.subtract).then_inc(y_last, 1)
                dve.wait_ge(y_last, 1)
                dve.wait_ge(y_split, KT - 1)
                def add_squares(f, c=None):
                    cols = slice(0, T) if c is None else slice(c * CH, (c + 1) * CH)
                    dve.wait_ge(x_sq, f + 1 + (c or 0))
                    if f >= 2:
                        dve.wait_ge(sq_added, f - 1 + (c or 0))
                    nc.vector.tensor_tensor(squares[:, cols], squares[:, cols], square[:, cols], ALU.add
                                            ).then_inc(sq_added, 1)

                def new_x(f, parts, signal):
                    new, old = chunks(xy[:, f]), chunks(x_new[:, f % 2])
                    for ch, cols, c in parts:
                        last = nc.vector.scalar_tensor_tensor(new[:, ch, cols], tile_psum(N_IN + f)[:, ch, cols],
                                                              mod[:, 2 * KT + f, c:c + 1], old[:, ch, cols],
                                                              ALU.mult, ALU.add)
                    last.then_inc(signal, 1)

                for f in range(KT):
                    dve.wait_ge(x_loaded[f % 2], 16 * (f // 2 + 1))
                    if f < KT - 1:
                        dve.wait_ge(tile_done, N_IN + f + 1)
                        new_x(f, pieces(), set_free[f % 2])
                    if f >= 2:
                        add_squares(f - 1)
                nc.vector.memset(ones, 1.0).then_inc(ones_ready, 1)
                f = KT - 1
                by_chunk = [[(slice(c, c + 1), slice(0, CH), 0)] for c in range(NCH - 1)] + [pieces()[1:]]
                for c in range(NCH):
                    dve.wait_ge(last_chunk, c + 1)
                    new_x(f, by_chunk[c], x_chunk)
                    if c >= 1:
                        add_squares(f, c - 1)
                add_squares(f, NCH - 1)

          nc.all_engine_barrier(sems_to_clear=layer_sems)

        y_scaled = sem("y_scaled")
        y_out = sem("y_out")
        with nc.Block() as block:
            @block.sync
            def _(sp):
                for k in range(KT):
                    sp.wait_ge(y_scaled, k + 1)
                    sp.dma_start(yT[k], slots[:, k]).then_inc(y_out, 16)
                sp.wait_ge(y_out, 16 * KT)

            @block.tensor
            def _(pe):
                norm_spread(pe, layer_norm)

            @block.vector
            def _(dve):
                step = [0]

                def own(ins):
                    ins.then_inc(dve_step, 1)
                    step[0] += 1

                def settle():
                    dve.wait_ge(dve_step, step[0])

                norm_dve(dve, own, settle, layer_norm)
                dve.wait_ge(rstd_ready, TT)
                for k in range(KT):
                    nc.vector.scalar_tensor_tensor(chunks(slots[:, k]), chunks(xy[:, k]), fin_g[:, k:k + 1],
                                                   psum[:, RSTD_BANK:RSTD_BANK + 3, 0:CH], ALU.mult, ALU.mult
                                                   ).then_inc(y_scaled, 1)


def constants():
    f = np.float32
    ident = np.eye(P, dtype=f)
    half = HEAD_DIM // 4
    freqs = f(ROPE_BASE) ** (-np.arange(half, dtype=f) / f(half))
    t = np.arange(DEC_SEQ)
    d = np.arange(P) % HEAD_DIM
    pos = np.where(d[:, None] < HEAD_DIM // 2, (t // GRID_W)[None, :], (t % GRID_W)[None, :]).astype(f)
    ang = (pos * freqs[d % half][:, None]).astype(f)
    sign = np.where(d % (2 * half) < half, f(-1), f(1))[:, None]
    rope = np.concatenate([np.cos(ang), sign * np.sin(ang)], axis=1).astype(f)
    q, k = np.arange(P)[:, None], np.arange(P)[None, :]
    zero = np.zeros((P, P), f)
    band = np.concatenate([np.where(k >= q, f(0), f(-NEG)), zero, zero, np.where(k <= q, f(0), f(-NEG))],
                          axis=1).astype(f)
    row, col = np.arange(P) // QC, np.arange(P) % QC
    row_masks, col_masks = [], []
    for rg in range(2):
        key, query = d_keys(rg * N_CG)[0] + np.arange(KR)[None, :], (rg * QR + row)[:, None]
        start = np.clip(query - WIN_R // 2, 0, ROWS - WIN_R)
        row_masks.append(np.where((key >= start) & (key < start + WIN_R), f(0), f(-NEG)))
    for cg in range(N_CG):
        key, query = d_keys(cg)[1] + np.arange(KC)[None, :], (cg * QC + col)[:, None]
        start = np.clip(query - WIN_C // 2, 0, GRID_W - WIN_C)
        if cg == BIAS_CLASS.index(BIAS_CLASS[cg]):
            col_masks.append(np.where((key >= start) & (key < start + WIN_C), f(0), f(-NEG)))
    return ident, rope, band, np.stack(row_masks, axis=1).astype(f), np.stack(col_masks, axis=1).astype(f)


def rpb_tables(rpb):
    padded = np.pad(rpb, ((0, 0), (0, 0), (WIN_R, WIN_R), (2 * WIN_C, 2 * WIN_C)))
    row, col = np.arange(P)[:, None, None] // QC, np.arange(P)[:, None, None] % QC
    tables = []
    for t in range(2):
        for rg in range(2):
            for cls in range(N_CLASS):
                cg = BIAS_CLASS.index(cls)
                first_row, first_col = d_keys(rg * N_CG + cg)
                dr = first_row + np.arange(KR)[None, :, None] - (rg * QR + row) + WIN_R - 1 + WIN_R
                dc = first_col + np.arange(KC)[None, None, :] - (cg * QC + col) + WIN_C - 1 + 2 * WIN_C
                for r in range(2):
                    tables.append(padded[:, 2 * t + r, dr, dc].reshape(DEPTH, P, KR * KC))
    return np.stack(tables, axis=1)


def kernel(x_prompt, x_sample, cache_c_k, cache_c_v, cache_d_k, cache_d_v, c, c_ctx, norm_g, w_mod, b_mod,
           w_in, w_out, w_s, b_s, w_conv, sink, rpb, final_g):
    import concourse.bacc as bacc
    from concourse.bass_utils import run_bass_kernel_spmd

    a = dict(x_prompt=x_prompt, x_sample=x_sample, cache_c_k=cache_c_k, cache_c_v=cache_c_v, cache_d_k=cache_d_k,
             cache_d_v=cache_d_v, c=c, c_ctx=c_ctx, norm_g=norm_g, w_mod=w_mod, b_mod=b_mod, w_in=w_in,
             w_out=w_out, w_s=w_s, b_s=b_s, w_conv=w_conv, sink=sink, rpb=rpb, final_g=final_g)
    a = {k: np.asarray(v) for k, v in a.items()}
    cat, con = np.concatenate, np.ascontiguousarray

    def heads_c(m, axis):
        parts = np.split(m, 4, axis=axis)
        return cat([parts[h] for h in C_HEADS], axis=axis)

    def columns(part, t):
        m = a["w_in"][:, :, COLUMNS[part]:COLUMNS[part] + (P if part in ("ck", "cv") else 2 * P)]
        if part in ("cq", "cz"):
            m = heads_c(m, 2)
        return m[:, :, t * P:(t + 1) * P]

    w_out_p = cat([a["w_out"][:, :512], heads_c(a["w_out"][:, 512:768], 1), a["w_out"][:, 768:]], axis=1)
    tiles = [columns(*x) for x in TILES] + [w_out_p[:, :, f * P:(f + 1) * P] for f in range(KT)]
    ident, rope, band, rows, cols = constants()
    data = {
        "xT": cat([a["x_sample"][0], a["x_prompt"][0]]).T.reshape(KT, P, T),
        "cond": np.stack([a["c"][0], a["c_ctx"]], axis=1).reshape(KT, P, 2).transpose(1, 0, 2),
        "w_mod": a["w_mod"],
        "b_mod": a["b_mod"].reshape(DEPTH, 24, P).transpose(2, 0, 1),
        "norm_g": a["norm_g"].reshape(DEPTH, KT, P).transpose(2, 0, 1),
        "final_g": a["final_g"].reshape(KT, P).T,
        "w_tiles": np.stack([m.reshape(DEPTH, KT, P, P).transpose(0, 2, 1, 3) for m in tiles], axis=1),
        "w_sT": a["w_s"].transpose(0, 3, 1, 2),
        "b_s": np.repeat(a["b_s"].reshape(DEPTH, 2, 2, 1, P), HEAD_DIM, axis=3
                         ).reshape(DEPTH, 2, P, P).transpose(0, 2, 1, 3),
        "w_conv": a["w_conv"].reshape(DEPTH, 3, 2, P).transpose(0, 3, 2, 1),
        "sink": np.repeat(a["sink"][:, None, list(C_HEADS)], P, axis=1),
        "rpb": rpb_tables(a["rpb"]),
        "cckT": a["cache_c_k"][0].reshape(DEPTH, P, P).transpose(0, 2, 1),
        "ccv": a["cache_c_v"][0].reshape(DEPTH, P, P),
        "cdkT": a["cache_d_k"][0].reshape(DEPTH, P, 2, P).transpose(0, 3, 2, 1),
        "cdv": a["cache_d_v"][0].reshape(DEPTH, P, 2, P),
        "ident_c": ident, "rope_c": rope, "band_c": band, "row_c": rows, "col_c": cols,
    }
    outs = {"yT": (KT, P, T), "sckT": (DEPTH, P, P), "scvT": (DEPTH, P, P), "sdkT": (DEPTH, 2, P, P),
            "sdvT": (DEPTH, 2, P, P)}
    nc = bacc.Bacc("TRN2", target_bir_lowering=False, num_devices=1)
    data = {k: con(v) for k, v in data.items()}
    args = {k: nc.dram_tensor("in_" + k, v.shape, F32, kind="ExternalInput").ap() for k, v in data.items()}
    args |= {k: nc.dram_tensor("out_" + k, s, F32, kind="ExternalOutput").ap() for k, s in outs.items()}
    build(nc, **args)
    r = run_bass_kernel_spmd(nc, [{"in_" + k: v for k, v in data.items()}], core_ids=[0]).results[0]

    y = r["out_yT"].reshape(D_MODEL, T).T
    natural = lambda m: m.reshape(DEPTH, -1, SEQ).transpose(0, 2, 1).reshape(1, DEPTH, SEQ, -1, HEAD_DIM)
    return (con(y[DEC_SEQ:])[None], con(y[:DEC_SEQ])[None], con(natural(r["out_sckT"])),
            con(natural(r["out_scvT"])), con(natural(r["out_sdkT"])), con(natural(r["out_sdvT"])))
```
